# Optimizing a Trainium2 kernel written in Bass

```python
import jax, jax.numpy as jnp
from jax import lax
import numpy as np

D_MODEL = 1024
BATCH = 1
SEQ = 512
DEPTH = 1
DEC_BATCH = 8
DEC_SEQ = 16
PAST_LEN = 256

CHUNK = 64
Q_BLOCK = 128
EPS = 1e-6

FOX_HEADS = 8
FOX_HEAD_DIM = 64
FOX_WIDTH = FOX_HEADS * FOX_HEAD_DIM
FORGET_BIAS_INIT = 2.0

MLA_HEADS = 8
MLA_NOPE_DIM = 64
MLA_ROPE_DIM = 32
MLA_V_DIM = 64
MLA_Q_LORA = 256
MLA_KV_LORA = 128
MLA_WIDTH = MLA_HEADS * MLA_V_DIM
ROPE_BASE = 10000.0

MIX_WIDTH = FOX_WIDTH + MLA_WIDTH

OFF_FQ = 0
OFF_FK = OFF_FQ + FOX_WIDTH
OFF_FV = OFF_FK + FOX_WIDTH
OFF_FF = OFF_FV + FOX_WIDTH
OFF_CQ = OFF_FF + FOX_HEADS
OFF_CKV = OFF_CQ + MLA_Q_LORA
OFF_KR = OFF_CKV + MLA_KV_LORA
IN_WIDTH = OFF_KR + MLA_ROPE_DIM

PEER_HEADS = 8
PEER_N_KEYS = 128
PEER_EXPERTS = PEER_N_KEYS * PEER_N_KEYS
PEER_KEY_DIM = 256
PEER_HALF = PEER_KEY_DIM // 2
PEER_TOPK = 16
PEER_TOK_BLOCK = 128

kernel_name = "fox_mla_peer_streaming_step"

F32 = jnp.float32

def _rmsnorm(x, g):
    xf = x.astype(F32)
    y = xf * lax.rsqrt(jnp.mean(xf * xf, axis=-1, keepdims=True) + EPS)
    return (y * g.astype(F32)).astype(x.dtype)

def _rope(x, pos):
    half = x.shape[-1] // 2
    inv = ROPE_BASE ** (-jnp.arange(half, dtype=F32) / half)
    ang = pos.astype(F32)[:, None] * inv[None, :]
    shape = (1, pos.shape[0]) + (1,) * (x.ndim - 3) + (half,)
    cos = jnp.cos(ang).reshape(shape)
    sin = jnp.sin(ang).reshape(shape)
    xf = x.astype(F32)
    x1, x2 = xf[..., :half], xf[..., half:]
    return jnp.concatenate([x1 * cos - x2 * sin, x1 * sin + x2 * cos], axis=-1).astype(x.dtype)

def _attend(q, k, v, q_pos, k_pos, c_q, c_k, chunk_causal):
    scale = q.shape[-1] ** -0.5
    s = jnp.einsum('bqhd,bkhd->bhqk', q, k, preferred_element_type=F32) * scale
    if c_q is not None:
        s = s + (jnp.transpose(c_q, (0, 2, 1))[..., :, None]
                 - jnp.transpose(c_k, (0, 2, 1))[..., None, :])
    if chunk_causal:
        mask = (k_pos[None, :] // CHUNK) <= (q_pos[:, None] // CHUNK)
    else:
        mask = k_pos[None, :] <= q_pos[:, None]
    s = jnp.where(mask, s, -jnp.inf)
    p = jax.nn.softmax(s, axis=-1)
    return jnp.einsum('bhqk,bkhd->bqhd', p.astype(v.dtype), v)

def _sweep(q, k, v, pos, c, chunk_causal):
    B, S = q.shape[0], q.shape[1]
    nb = S // Q_BLOCK

    def one(i):
        start = i * Q_BLOCK
        qb = lax.dynamic_slice_in_dim(q, start, Q_BLOCK, 1)
        pb = lax.dynamic_slice_in_dim(pos, start, Q_BLOCK, 0)
        cb = None if c is None else lax.dynamic_slice_in_dim(c, start, Q_BLOCK, 1)
        return _attend(qb, k, v, pb, pos, cb, c, chunk_causal)

    out = lax.map(one, jnp.arange(nb))
    return jnp.moveaxis(out, 0, 1).reshape(B, S, out.shape[-2], out.shape[-1])

def _peer(h, w_pq, sub_keys, peer_u, peer_v):
    T, D = h.shape
    pad = (-T) % PEER_TOK_BLOCK
    blocks = jnp.pad(h, ((0, pad), (0, 0))).reshape(-1, PEER_TOK_BLOCK, D)

    def one(xb):
        q = (xb @ w_pq).reshape(PEER_TOK_BLOCK, PEER_HEADS, PEER_KEY_DIM).astype(F32)
        q = q * lax.rsqrt(jnp.mean(q * q, axis=-1, keepdims=True) + EPS)
        s1 = jnp.einsum('thd,hnd->thn', q[..., :PEER_HALF], sub_keys[0].astype(F32))
        s2 = jnp.einsum('thd,hnd->thn', q[..., PEER_HALF:], sub_keys[1].astype(F32))
        v1, i1 = lax.top_k(s1, PEER_TOPK)
        v2, i2 = lax.top_k(s2, PEER_TOPK)
        cand = (v1[..., :, None] + v2[..., None, :]).reshape(PEER_TOK_BLOCK, PEER_HEADS, PEER_TOPK * PEER_TOPK)
        sv, si = lax.top_k(cand, PEER_TOPK)
        e = (jnp.take_along_axis(i1, si // PEER_TOPK, axis=-1) * PEER_N_KEYS
             + jnp.take_along_axis(i2, si % PEER_TOPK, axis=-1))
        g = jax.nn.softmax(sv, axis=-1).reshape(PEER_TOK_BLOCK, PEER_HEADS * PEER_TOPK)
        e = e.reshape(PEER_TOK_BLOCK, PEER_HEADS * PEER_TOPK)
        a = jnp.einsum('tkd,td->tk', peer_u[e], xb, preferred_element_type=F32)
        act = (jax.nn.gelu(a, approximate=False) * g).astype(peer_v.dtype)
        return jnp.einsum('tk,tkd->td', act, peer_v[e])

    out = lax.map(one, blocks).reshape(-1, D)
    return out[:T]

def _layer(x, pos, past, g_mix, w_in, b_f, g_q, w_uq, g_kv, w_ukv, w_o, g_ffn,
           w_pq, sub_keys, peer_u, peer_v):
    B, S, D = x.shape
    h = _rmsnorm(x, g_mix)
    z = h @ w_in
    fq = z[..., OFF_FQ:OFF_FK].reshape(B, S, FOX_HEADS, FOX_HEAD_DIM)
    fk = z[..., OFF_FK:OFF_FV].reshape(B, S, FOX_HEADS, FOX_HEAD_DIM)
    fv = z[..., OFF_FV:OFF_FF].reshape(B, S, FOX_HEADS, FOX_HEAD_DIM)
    flogf = jax.nn.log_sigmoid(z[..., OFF_FF:OFF_CQ].astype(F32) + b_f.astype(F32))
    cq = _rmsnorm(z[..., OFF_CQ:OFF_CKV], g_q)
    q = (cq @ w_uq).reshape(B, S, MLA_HEADS, MLA_NOPE_DIM + MLA_ROPE_DIM)
    q = jnp.concatenate([q[..., :MLA_NOPE_DIM], _rope(q[..., MLA_NOPE_DIM:], pos)], axis=-1)
    ckv = _rmsnorm(z[..., OFF_CKV:OFF_KR], g_kv)
    krope = _rope(z[..., OFF_KR:IN_WIDTH], pos)
    new_state = (fk, fv, flogf, ckv, krope)

    if past is None:
        fk_all, fv_all, logf_all, ckv_all, kr_all = new_state
        k_pos = pos
    else:
        pk, pv, plf, pckv, pkr = past
        fk_all = jnp.concatenate([pk, fk.astype(pk.dtype)], axis=1)
        fv_all = jnp.concatenate([pv, fv.astype(pv.dtype)], axis=1)
        logf_all = jnp.concatenate([plf.astype(F32), flogf], axis=1)
        ckv_all = jnp.concatenate([pckv, ckv.astype(pckv.dtype)], axis=1)
        kr_all = jnp.concatenate([pkr, krope.astype(pkr.dtype)], axis=1)
        k_pos = jnp.arange(pk.shape[1] + S, dtype=jnp.int32)
    L = fk_all.shape[1]
    c_all = jnp.cumsum(logf_all.astype(F32), axis=1)
    kv = (ckv_all @ w_ukv).reshape(B, L, MLA_HEADS, MLA_NOPE_DIM + MLA_V_DIM)
    mk = jnp.concatenate([kv[..., :MLA_NOPE_DIM],
                          jnp.broadcast_to(kr_all[:, :, None, :], (B, L, MLA_HEADS, MLA_ROPE_DIM)).astype(kv.dtype)],
                         axis=-1)
    mv = kv[..., MLA_NOPE_DIM:]

    if past is None:
        fo = _sweep(fq, fk_all, fv_all, pos, c_all, False)
        mo = _sweep(q, mk, mv, pos, None, True)
    else:
        fo = _attend(fq, fk_all, fv_all, pos, k_pos, c_all[:, L - S:], c_all, False)
        mo = _attend(q, mk, mv, pos, k_pos, None, None, True)

    o = jnp.concatenate([fo.reshape(B, S, FOX_WIDTH), mo.reshape(B, S, MLA_WIDTH).astype(fo.dtype)], axis=-1) @ w_o
    x = x + o
    h2 = _rmsnorm(x, g_ffn)
    x = x + _peer(h2.reshape(B * S, D), w_pq, sub_keys, peer_u, peer_v).reshape(B, S, D)
    return x, new_state

def setup_inputs(seed: int = 0) -> dict:
    key = jax.random.key(seed)
    ks = jax.random.split(key, 24)
    n = jax.random.normal
    D = D_MODEL
    return {
        "x_prompt": n(ks[0], (BATCH, SEQ, D), F32),
        "x_sample": n(ks[1], (DEC_BATCH, DEC_SEQ, D), F32),
        "cache_fox_k": n(ks[2], (DEPTH, DEC_BATCH, PAST_LEN, FOX_HEADS, FOX_HEAD_DIM), F32),
        "cache_fox_v": n(ks[3], (DEPTH, DEC_BATCH, PAST_LEN, FOX_HEADS, FOX_HEAD_DIM), F32),
        "cache_fox_logf": jax.nn.log_sigmoid(FORGET_BIAS_INIT + n(ks[4], (DEPTH, DEC_BATCH, PAST_LEN, FOX_HEADS), F32)),
        "cache_mla_ckv": n(ks[5], (DEPTH, DEC_BATCH, PAST_LEN, MLA_KV_LORA), F32),
        "cache_mla_krope": n(ks[6], (DEPTH, DEC_BATCH, PAST_LEN, MLA_ROPE_DIM), F32),
        "g_mix": 1.0 + 0.02 * n(ks[7], (DEPTH, D), F32),
        "w_in": n(ks[8], (DEPTH, D, IN_WIDTH), F32) * D ** -0.5,
        "b_f": FORGET_BIAS_INIT + 0.1 * n(ks[9], (DEPTH, FOX_HEADS), F32),
        "g_q": 1.0 + 0.02 * n(ks[10], (DEPTH, MLA_Q_LORA), F32),
        "w_uq": n(ks[11], (DEPTH, MLA_Q_LORA, MLA_HEADS * (MLA_NOPE_DIM + MLA_ROPE_DIM)), F32) * MLA_Q_LORA ** -0.5,
        "g_kv": 1.0 + 0.02 * n(ks[12], (DEPTH, MLA_KV_LORA), F32),
        "w_ukv": n(ks[13], (DEPTH, MLA_KV_LORA, MLA_HEADS * (MLA_NOPE_DIM + MLA_V_DIM)), F32) * MLA_KV_LORA ** -0.5,
        "w_o": n(ks[14], (DEPTH, MIX_WIDTH, D), F32) * MIX_WIDTH ** -0.5,
        "g_ffn": 1.0 + 0.02 * n(ks[15], (DEPTH, D), F32),
        "w_pq": n(ks[16], (DEPTH, D, PEER_HEADS * PEER_KEY_DIM), F32) * D ** -0.5,
        "peer_sub_keys": n(ks[17], (DEPTH, 2, PEER_HEADS, PEER_N_KEYS, PEER_HALF), F32) * PEER_HALF ** -0.5,
        "peer_u": n(ks[18], (DEPTH, PEER_EXPERTS, D), F32) * D ** -0.5,
        "peer_v": n(ks[19], (DEPTH, PEER_EXPERTS, D), F32) * PEER_HEADS ** -0.5,
        "g_final": 1.0 + 0.02 * n(ks[20], (D,), F32),
    }

def reference(x_prompt, x_sample, cache_fox_k, cache_fox_v, cache_fox_logf, cache_mla_ckv,
              cache_mla_krope, g_mix, w_in, b_f, g_q, w_uq, g_kv, w_ukv, w_o, g_ffn, w_pq,
              peer_sub_keys, peer_u, peer_v, g_final):
    pos_p = jnp.arange(x_prompt.shape[1], dtype=jnp.int32)
    past_len = cache_fox_k.shape[2]
    pos_s = past_len + jnp.arange(x_sample.shape[1], dtype=jnp.int32)
    yp, ys = x_prompt, x_sample
    st_p, st_s = [], []
    for l in range(DEPTH):
        lw = (g_mix[l], w_in[l], b_f[l], g_q[l], w_uq[l], g_kv[l], w_ukv[l], w_o[l], g_ffn[l],
              w_pq[l], peer_sub_keys[l], peer_u[l], peer_v[l])
        yp, new_p = _layer(yp, pos_p, None, *lw)
        past = (cache_fox_k[l], cache_fox_v[l], cache_fox_logf[l], cache_mla_ckv[l], cache_mla_krope[l])
        ys, new_s = _layer(ys, pos_s, past, *lw)
        st_p.append(new_p)
        st_s.append(new_s)
    y_prompt = _rmsnorm(yp, g_final)
    y_sample = _rmsnorm(ys, g_final)
    p_fox_k = jnp.stack([s[0] for s in st_p])
    p_fox_v = jnp.stack([s[1] for s in st_p])
    p_fox_logf = jnp.stack([s[2] for s in st_p])
    p_mla_ckv = jnp.stack([s[3] for s in st_p])
    p_mla_krope = jnp.stack([s[4] for s in st_p])
    s_fox_k = jnp.stack([s[0] for s in st_s])
    s_fox_v = jnp.stack([s[1] for s in st_s])
    s_fox_logf = jnp.stack([s[2] for s in st_s])
    s_mla_ckv = jnp.stack([s[3] for s in st_s])
    s_mla_krope = jnp.stack([s[4] for s in st_s])
    return (y_prompt, y_sample, p_fox_k, p_fox_v, p_fox_logf, p_mla_ckv, p_mla_krope,
            s_fox_k, s_fox_v, s_fox_logf, s_mla_ckv, s_mla_krope)


_drawn_inputs = setup_inputs


def setup_inputs(seed=0):
    import zlib

    import numpy as np

    out = dict(_drawn_inputs(seed))
    spreads = {}
    factors = {'g_mix': 2.823, 'g_q': 6.605, 'g_kv': 3.053, 'g_final': 8.645, 'g_ffn': 5.769}
    for name, (base, spread) in spreads.items():
        noise = np.random.default_rng([zlib.crc32(name.encode()), seed]).standard_normal(out[name].shape)
        drawn = base * np.exp(spread * noise) if base else spread * noise
        out[name] = __import__('jax').numpy.asarray(drawn.astype(out[name].dtype))
    for name, factor in factors.items():
        out[name] = (out[name] * factor).astype(out[name].dtype)
    return out
```

```python
from contextlib import ExitStack

import numpy as np
import concourse.bass as bass
from concourse import mybir

F32 = mybir.dt.float32
BF16 = mybir.dt.bfloat16
U32 = mybir.dt.uint32
ALU = mybir.AluOpType
ACT = mybir.ActivationFunctionType
AX = mybir.AxisListType

P = 128
D = 1024
KD = D // P
SEQ, DB, DS, PAST = 512, 8, 16, 256
TP = SEQ // P
T = TP + 1
NT = T * P
FH, HD = 8, 64
MH, NOPE, ROPE, VD = 8, 64, 32, 64
QL, KVL = 256, 128
L = PAST + DS
R_FF, R_CQ, R_CKV, R_KR = 0, FH, FH + QL, FH + QL + KVL
RW = R_KR + ROPE
FOX_SCALE = float(HD) ** -0.5
MLA_SCALE = float(NOPE + ROPE) ** -0.5
PH, NK, TK = 8, 128, 16
SEL = PH * TK
EPS = 1e-6
NEG = -1e30
XCHG = 4
GI = SEL // (2 * XCHG)


def peer_step_kernel(nc, t_in, t_out):
    base, end = 16512, 229344

    class Region:

        def __init__(self, at):
            self.at = at

        def __call__(self, name, shape, dtype=F32):
            size = int(np.prod(shape[1:])) * {F32: 4, U32: 4, BF16: 2}[dtype]
            t = nc.alloc_sbuf_tensor_at(name, shape, dtype, offset=self.at)
            self.at += (size + 31) // 32 * 32
            assert self.at <= end, (name, self.at)
            return t

    with ExitStack() as ctx:
        def sem(name):
            return ctx.enter_context(nc.semaphore(name))

        r = Region(base)
        ident = r("ident", [P, P])
        ones = r("ones", [P, P])
        small = r("small", [P, 64])
        eps_col = r("eps_col", [P, 8])
        late_at = r.at
        c_rope = r("c_rope", [P, 2, NT])
        c_rrow = r("c_rrow", [P, 2, T, ROPE // 2])
        selh = r("selh", [P, FH, P])
        selb = r("selb", [P, DB, P])
        cb = r("cb", [P, 3 * P + DS], BF16)
        gm = r("gm", [P, KD])
        bfb = r("bfb", [P, T, FH])
        gq = r("gq", [P, QL])
        gkv = r("gkv", [P, KVL])
        fv = r("fv", [P, T, FH * HD])
        zT = r("zT", [P, T, 4, P])
        fqT = r("fqT", [P, 4, NT])
        kT = r("kT", [P, 4, NT])
        ncT = r("ncT", [P, SEQ])
        w_uv = r("w_uv", [P, MH * VD])
        wu_at = r.at
        w_uq = r("w_uq", [P, 2, MH, P])
        w_uk = r("w_uk", [P, MH, NOPE])
        w_ukT = r("w_ukT", [P, MH, P])
        zr_at = r.at
        zr = r("zr", [P, T, RW])
        r2_at = r.at
        krl = r("krl", [P, T, P])
        cqn = r("cqn", [P, T, QL])
        ckvn = r("ckvn", [P, T, KVL])
        fk = r("fk", [P, T, FH * HD])
        a_at = r.at
        z = Region(zr_at)
        qps = z("qps", [P, DB, MH, DS])
        qrs = z("qrs", [P, DB, MH, DS])
        assert z.at <= r2_at
        a1 = Region(a_at)
        hT = a1("hT", [P, KD, NT])
        rmsb = a1("rmsb", [P, NT])
        rstdb = a1("rstdb", [P, NT])
        wr = a1("wr", [P, KD, RW])
        wk = a1("wk", [P, KD, FH * HD])
        sq_at = a1.at
        wv = a1("wv", [P, KD, FH * HD])
        wq = a1("wq", [P, KD, FH * HD])
        sq = Region(sq_at)("sq", [P, KD, NT])
        a2 = Region(a_at)
        qmT = a2("qmT", [P, MH, NT])
        kmT = a2("kmT", [P, MH, SEQ])
        vm = a2("vm", [P, TP, MH * VD])
        prob = a2("prob", [P, 4, SEQ])
        probT = a2("probT", [P, 3, SEQ])
        qbd = a2("qbd", [P, 4, DB, FH, DS])
        oT = a2("oT", [P, 8, NT])
        s1 = Region(wu_at)
        vs = s1("vs", [P, 2, 2, FH * HD])
        ckTs = s1("ckTs", [P, 2, L])
        krTs = s1("krTs", [P, 2, L])
        assert s1.at <= zr_at
        s2 = Region(r2_at)
        kTs = s2("kTs", [P, 2, 4, L])
        vn = s2("vn", [P, 2, FH * HD])
        ckr = s2("ckr", [P, 2, 2, KVL])
        ckn = s2("ckn", [P, 2, KVL])
        lfs = s2("lfs", [P, L])
        ncS = s2("ncS", [P, L])
        assert s2.at <= a_at
        l1 = Region(late_at)
        x2 = l1("x2", [P, T, D])
        h2 = l1("h2", [P, T, D])
        gffn = l1("gffn", [P, D])
        gfin = l1("gfin", [P, D])
        eidx = l1("eidx", [P, NT + 2 * XCHG], U32)
        gate = l1("gate", [P, NT])
        g_at = l1.at
        h2T = l1("h2T", [P, KD, NT])
        wpq = l1("wpq", [P, 2, KD, 2 * P])
        assert l1.at <= a_at
        l2 = Region(a_at)
        w_o = l2("w_o", [P, 8, D])
        latT = l2("latT", [P, MH, P])
        assert l2.at <= a_at + 4 * MH * (NT + SEQ)
        l3 = Region(a_at)
        sc = l3("sc", [P, T, PH, 2 * NK])
        v_at = l3.at
        pq = l3("pq", [P, 2, 2, NT])
        pq2 = l3("pq2", [P, 2, 2, NT])
        keysT = l3("keysT", [P, 2 * PH, NK])
        k1 = Region(g_at)
        sw = k1("sw", [P, PH, 2, NK])
        sr = k1("sr", [P, PH, 2, NK])
        cand = k1("cand", [P, PH, TK, TK])
        candr = k1("candr", [P, PH, TK, TK])
        onehot = k1("onehot", [P, SEL, TK])
        v16 = k1("v16", [P, PH, 2, TK])
        i16 = k1("i16", [P, PH, 2, TK], U32)
        cv = k1("cv", [P, PH, TK])
        ci = k1("ci", [P, PH, TK], U32)
        hi = k1("hi", [P, SEL], U32)
        lo = k1("lo", [P, SEL], U32)
        e1 = k1("e1", [P, SEL])
        e2 = k1("e2", [P, SEL])
        iota = k1("iota", [P, TK])
        gsum = k1("gsum", [P, 3, PH])
        g1 = Region(g_at)
        ubuf = g1("ubuf", [P, 2, XCHG, D])
        gscr = g1("gscr", [P, D])
        yout = g1("yout", [P, D])
        ixu = g1("ixu", [P, 2, XCHG], U32)
        ixv = g1("ixv", [P, 2, XCHG], U32)
        dots = g1("dots", [P, 2, XCHG])
        gelu = g1("gelu", [P, 2, XCHG])
        wts = g1("wts", [P, 2, XCHG])
        assert g1.at <= a_at
        vbuf = Region(v_at)("vbuf", [P, 2, XCHG, D])

        ps = ctx.enter_context(nc.psum_tensor("ps", [P, 8, 512], F32))

        x_loaded, c_loaded, wr_loaded, wk_loaded, wv_loaded, wq_loaded, wu_loaded = (
            sem(n) for n in ("x_loaded", "c_loaded", "wr_loaded", "wk_loaded", "wv_loaded", "wq_loaded", "wu_loaded"))
        squares, meansq, rms_ready, h_ready = (sem(n) for n in ("squares", "meansq", "rms_ready", "h_ready"))
        proj_done, proj_copied = sem("proj_done"), sem("proj_copied")
        ss_ready, rt_ready, ff_abs, ff_log, rows_ready = (
            sem(n) for n in ("ss_ready", "rt_ready", "ff_abs", "ff_log", "rows_ready"))
        state_stored = sem("state_stored")
        tr_done, tr_copied = sem("tr_done"), sem("tr_copied")
        nc_ready, ncs_ready, lfs_loaded = sem("nc_ready"), sem("ncs_ready"), sem("lfs_loaded")
        mq_done, mq_nope, mq_rope = sem("mq_done"), sem("mq_nope"), sem("mq_rope")
        mk_done, mk_copied, kr_copied = sem("mk_done"), sem("mk_copied"), sem("kr_copied")
        qp_done, qs_ready, qbd_ready = sem("qp_done"), sem("qs_ready"), sem("qbd_ready")
        s_done, max_ready, exp_done, p_ready = sem("s_done"), sem("max_ready"), sem("exp_done"), sem("p_ready")
        pt_done, pt_copied, pv_done, o_copied = sem("pt_done"), sem("pt_copied"), sem("pv_done"), sem("o_copied")
        batch_loaded = [sem("batch_loaded0"), sem("batch_loaded1")]
        new_keys = sem("new_keys")
        up_done = sem("up_done")
        wo_loaded, late_loaded, wpq_loaded = sem("wo_loaded"), sem("late_loaded"), [sem("wpq0"), sem("wpq1")]
        out_done, x2_ready, ss2_ready, rt2_ready, h2_ready = (
            sem(n) for n in ("out_done", "x2_ready", "ss2_ready", "rt2_ready", "h2_ready"))
        h2t_done, h2t_copied = sem("h2t_done"), sem("h2t_copied")
        pq_done, pq_copied, sc_done, rt3_ready, rs3_ready, sc_copied = (
            sem(n) for n in ("pq_done", "pq_copied", "sc_done", "rt3_ready", "rs3_ready", "sc_copied"))
        gate_in, gate_exp, topk_done = sem("gate_in"), sem("gate_exp"), sem("topk_done")
        ixu_ready, ixv_ready = sem("ixu_ready"), sem("ixv_ready")
        u_loaded = [sem("u_loaded0"), sem("u_loaded1")]
        v_loaded = [sem("v_loaded0"), sem("v_loaded1")]
        dots_done, gelu_done, acc_done = sem("dots_done"), sem("gelu_done"), sem("acc_done")
        ss3_ready, rt4_ready, y_ready, y_stored = (
            sem(n) for n in ("ss3_ready", "rt4_ready", "y_ready", "y_stored"))
        act_chain, dve_chain, dve_loop, pool_chain = (
            sem(n) for n in ("act_chain", "dve_chain", "dve_loop", "pool_chain"))
        tile_in = sem("tile_in")
        y_free = sem("y_free")
        wait_carrier = sem("wait_carrier")

        UNITS = 64
        ALL = UNITS + 2 * DB

        def unit(n):
            pair, hh, i = n // 8, n // 4 % 2, n % 4
            return pair // 4, pair % 4, hh, i, (i + 1) * P

        def keys_of(n):
            return unit(n)[4] if n < UNITS else L

        block = ctx.enter_context(nc.Block())

        @block.sync
        def _(sp):
            ld = sp.dma_start
            ld(hT[:], t_in["xT"]).then_inc(x_loaded, 16)
            for dst, name in ((ident, "ident"), (ones, "ones"), (gm, "gm"), (c_rope, "c_rope"), (c_rrow, "c_rrow"),
                              (cb, "cb"), (bfb, "bfb"), (gq, "gq"), (gkv, "gkv")):
                ld(dst[:], t_in[name]).then_inc(c_loaded, 16)
            ld(selh[0:FH], t_in["selh"]).then_inc(c_loaded, 16)
            ld(selb[0:DB * FH], t_in["selb"]).then_inc(c_loaded, 16)
            ld(wr[:], t_in["wr"]).then_inc(wr_loaded, 16)
            ld(wk[:], t_in["wk"]).then_inc(wk_loaded, 16)
            for dst, name in ((w_uq, "w_uq"), (w_uk, "w_uk"), (w_uv, "w_uv")):
                ld(dst[:], t_in[name]).then_inc(wu_loaded, 16)
            ld(w_ukT[0:NOPE], t_in["w_ukT"]).then_inc(wu_loaded, 16)
            sp.wait_ge(meansq, 1)
            ld(wv[:], t_in["wv"]).then_inc(wv_loaded, 16)
            ld(wq[:], t_in["wq"]).then_inc(wq_loaded, 16)
            sp.wait_ge(proj_copied, 15)
            rows = lambda name: t_out[name].rearrange("(t p) c -> p t c", p=P)
            ld(rows("fk"), fk[:]).then_inc(state_stored, 16)
            ld(rows("fv"), fv[:]).then_inc(state_stored, 16)
            sp.wait_ge(rows_ready, 1)
            ld(rows("ckv"), ckvn[:]).then_inc(state_stored, 16)
            ld(rows("logf"), krl[:, :, 0:FH]).then_inc(state_stored, 16)
            ld(rows("krope"), krl[:, :, 64:64 + ROPE]).then_inc(state_stored, 16)
            sp.wait_ge(state_stored, 16 * 5)
            sp.wait_ge(tr_copied, 10)
            ld(lfs[0:64, 0:PAST], t_in["past_logf"]).then_inc(lfs_loaded, 16)
            new_logf = t_out["logf"][SEQ:NT].rearrange("(b q) h -> b h q", b=DB)
            for b in range(DB):
                ld(lfs[b * FH:(b + 1) * FH, PAST:L], new_logf[b], allow_slow_non_contiguous=True).then_inc(lfs_loaded, 16)

            def load_batch(b):
                s = b % 2
                if b == 0:
                    sp.wait_ge(qs_ready, 3)
                    sp.wait_ge(mk_copied, 8)
                if b >= 2:
                    sp.wait_ge(pv_done, UNITS + 2 * (b - 2) + 2)
                q = batch_loaded[s]
                new = slice(SEQ + b * DS, SEQ + (b + 1) * DS)
                ld(kTs[:, s, :, 0:PAST], t_in["past_k"][b]).then_inc(q, 16)
                ld(vs[:, s], t_in["past_v"][b].rearrange("(j p) c -> p j c", p=P)).then_inc(q, 16)
                ld(vn[0:DS, s], t_out["fv"][new]).then_inc(q, 16)
                ld(ckTs[:, s, 0:PAST], t_in["past_ckvT"][b]).then_inc(q, 16)
                ld(krTs[64:96, s, 0:PAST], t_in["past_krT"][b]).then_inc(q, 16)
                ld(ckr[:, s], t_in["past_ckv"][b].rearrange("(j p) c -> p j c", p=P)).then_inc(q, 16)
                ld(ckn[0:DS, s], t_out["ckv"][new]).then_inc(q, 16)

            load_batch(0)
            load_batch(1)
            sp.wait_ge(pv_done, UNITS)
            ld(w_o[:], t_in["w_o"]).then_inc(wo_loaded, 16)
            for b in range(2, DB):
                load_batch(b)
            sp.wait_ge(up_done, 1)
            sp.wait_ge(o_copied, 8 + 2 * DB + 1)
            ld(x2[:], t_in["xr"].rearrange("(t p) c -> p t c", p=P)).then_inc(late_loaded, 16)
            ld(gffn[:], t_in["gffn"]).then_inc(late_loaded, 16)
            ld(gfin[:], t_in["gfin"]).then_inc(late_loaded, 16)
            for h in range(PH):
                if h >= 2:
                    sp.wait_ge(pq_done, h - 1)
                ld(wpq[:, h % 2], t_in["wpq"][h]).then_inc(wpq_loaded[h % 2], 16)
                if h == 1:
                    sp.wait_ge(out_done, T)
                    ld(keysT[:], t_in["keysT"]).then_inc(late_loaded, 16)
            sp.sem_inc(y_free, 1)
            with sp.Fori(0, T) as t:
                sp.wait_ge(y_ready, t + 1)
                ld(t_out["y"][bass.ts(t, P)], yout[:]).then_inc(y_stored, 16)
                sp.wait_ge(y_stored, 16 * t + 16)
                sp.sem_inc(y_free, 1)

        @block.gpsimd
        def _(pool):
            n = [0]

            def link(ins):
                n[0] += 1
                ins.then_inc(pool_chain, 1)
                pool.wait_ge(pool_chain, n[0])

            pool.wait_ge(tr_copied, 5)
            pool.wait_ge(proj_done, 23)
            for h in range(MH):
                nc.gpsimd.tensor_copy(kmT[64:96, h, :].rearrange("p (t k) -> p t k", t=TP),
                                      zT[64:96, 0:TP, 3, :]).then_inc(kr_copied, 1)
                pool.wait_ge(kr_copied, h + 1)
            link(nc.gpsimd.memset(qbd[:], 0.0))
            pool.wait_ge(proj_copied, 23)
            for c in range(4):
                for hh in range(2):
                    rows = slice(64 * hh, 64 * hh + 64)
                    nc.gpsimd.tensor_copy(qbd[rows, c, :, 2 * c + hh, :],
                                          fqT[rows, c, SEQ:NT].rearrange("p (b q) -> p b q", b=DB)).then_inc(qbd_ready, 1)
                    pool.wait_ge(qbd_ready, 2 * c + hh + 1)
            for b in range(DB):
                s = b % 2
                new = slice(b * DS, (b + 1) * DS)
                if b == 0:
                    pool.wait_ge(state_stored, 16 * 5)
                    pool.wait_ge(qs_ready, 3)
                    pool.wait_ge(mk_copied, 8)
                    pool.wait_ge(tr_copied, 10)
                if b >= 2:
                    pool.wait_ge(pv_done, UNITS + 2 * (b - 2) + 2)
                for i, (dst, src) in enumerate(((kTs[:, s, :, PAST:L], kT[:, :, SEQ + b * DS:SEQ + (b + 1) * DS]),
                                                (ckTs[:, s, PAST:L], zT[:, TP, 2, new]),
                                                (krTs[64:96, s, PAST:L], zT[64:96, TP, 3, new]))):
                    nc.gpsimd.tensor_copy(dst, src).then_inc(new_keys, 1)
                    pool.wait_ge(new_keys, 3 * b + i + 1)

            def gather(dst, table, ix, half, s, done):
                nc.gpsimd.indirect_dma_start(
                    out=dst[:, half, s, :], out_offset=None, in_=t_in[table],
                    in_offset=bass.IndirectOffsetOnAxis(ix[:, half, s:s + 1], 0),
                    bounds_check=NK * NK - 1, oob_is_err=True).then_inc(done[half], 16)

            with pool.Fori(0, T) as t:
                with pool.Fori(0, GI) as j:
                    i2 = (t * GI + j) * 2
                    for half in range(2):
                        pool.wait_ge(ixu_ready, i2 + half + 1)
                        pool.wait_ge(dots_done, i2 + half + 1)
                        pool.sem_inc(wait_carrier, 1)
                        for s in range(XCHG):
                            gather(ubuf, "peer_u", ixu, half, s, u_loaded)
                    for half in range(2):
                        pool.wait_ge(ixv_ready, i2 + half + 1)
                        pool.wait_ge(acc_done, i2 + half + 1)
                        pool.sem_inc(wait_carrier, 1)
                        for s in range(XCHG):
                            gather(vbuf, "peer_v", ixv, half, s, v_loaded)

        @block.scalar
        def _(act):
            n = [0]
            A = nc.scalar.activation

            def link(ins):
                n[0] += 1
                ins.then_inc(act_chain, 1)
                act.wait_ge(act_chain, n[0])

            act.wait_ge(x_loaded, 16)
            for k in range(KD):
                A(sq[:, k], hT[:, k], ACT.Square).then_inc(squares, 1)
            act.wait_ge(meansq, 1)
            act.wait_ge(dve_chain, 1)
            A(rmsb[:, 0:SEQ], ps[:, 0, :], ACT.Sqrt, scale=1.0 / D, bias=eps_col[:, 0:1]).then_inc(rms_ready, 1)
            A(rmsb[:, SEQ:NT], ps[:, 1, 0:P], ACT.Sqrt, scale=1.0 / D, bias=eps_col[:, 0:1]).then_inc(rms_ready, 1)

            def copy_projection(n):
                act.wait_ge(proj_done, n + 1)
                bank = ps[:, 2 + n % 4]
                if n < 5:
                    A(zr[:, n], bank[:, 0:RW], ACT.Copy).then_inc(proj_copied, 1)
                elif n < 10:
                    A(fk[:, n - 5], bank, ACT.Copy).then_inc(proj_copied, 1)
                elif n < 15:
                    A(fv[:, n - 10], bank, ACT.Copy).then_inc(proj_copied, 1)
                else:
                    c, part = divmod(n - 15, 2)
                    dst = fqT[:, c, SEQ:NT] if part else fqT[:, c, 0:SEQ]
                    A(dst, bank[:, 0:P] if part else bank, ACT.Copy, scale=FOX_SCALE).then_inc(proj_copied, 1)

            for n_ in range(10):
                copy_projection(n_)
            act.wait_ge(ss_ready, 1)
            A(small[:, 10:15], small[:, 0:5], ACT.Sqrt, scale=1.0 / QL, bias=eps_col[:, 0:1])
            A(small[:, 15:20], small[:, 5:10], ACT.Sqrt, scale=1.0 / KVL, bias=eps_col[:, 0:1]).then_inc(rt_ready, 1)
            act.wait_ge(ff_abs, 1)
            link(A(krl[:, :, 8:16], krl[:, :, 24:32], ACT.Exp))
            A(krl[:, :, 16:24], krl[:, :, 8:16], ACT.Ln, bias=1.0).then_inc(ff_log, 1)
            for n_ in range(10, 23):
                copy_projection(n_)
            for u in range(10):
                act.wait_ge(tr_done, u + 1)
                bank = ps[:, 6 + u % 2].rearrange("p (c k) -> p c k", c=4)
                if u < 5:
                    A(zT[:, u], bank, ACT.Copy).then_inc(tr_copied, 1)
                else:
                    A(kT[:, :, (u - 5) * P:(u - 4) * P], bank, ACT.Copy).then_inc(tr_copied, 1)
            for h in range(MH):
                b = 3 * (h % 2)
                act.wait_ge(mq_done, h + 1)
                A(qmT[0:NOPE, h, 0:SEQ], ps[0:NOPE, b], ACT.Copy, scale=MLA_SCALE)
                A(qmT[0:NOPE, h, SEQ:NT], ps[0:NOPE, b + 2, 0:P], ACT.Copy, scale=MLA_SCALE).then_inc(mq_nope, 1)
            for u in range(12):
                act.wait_ge(mk_done, u + 1)
                bank = ps[:, u % 4]
                if u < 8:
                    A(kmT[0:NOPE, u], bank[0:NOPE], ACT.Copy).then_inc(mk_copied, 1)
                else:
                    A(vm[:, u - 8], bank, ACT.Copy).then_inc(mk_copied, 1)
            for g in range(2):
                act.wait_ge(qp_done, g + 1)
                if g == 0:
                    act.wait_ge(rows_ready, 1)
                A(qps[:, :, 4 * g:4 * g + 4, :].rearrange("p b h q -> p h b q"),
                  ps[:, 4 + g].rearrange("p (h b q) -> p h b q", h=4, b=DB), ACT.Copy).then_inc(qs_ready, 1)
            act.wait_ge(mq_rope, MH)
            A(qrs[64:96].rearrange("p b h q -> p h b q"),
              qmT[64:96, :, SEQ:NT].rearrange("p h (b q) -> p h b q", b=DB), ACT.Copy).then_inc(qs_ready, 1)

            def exponentials(n):
                nk = keys_of(n)
                act.wait_ge(max_ready, n + 1)
                if n >= 4:
                    act.wait_ge(pt_done, n - 3)
                A(prob[:, n % 4, 0:nk], ps[:, n % 3, 0:nk], ACT.Exp, bias=small[:, 32 + n % 4:33 + n % 4],
                  accum_out=small[:, 36 + n % 4:37 + n % 4]).then_inc(exp_done, 1)

            def copy_transposed(n):
                act.wait_ge(pt_done, n + 1)
                if n >= 3:
                    act.wait_ge(pv_done, n - 2)
                bank = ps[:, 3 + n % 2]
                if n < UNITS:
                    nk = keys_of(n)
                    A(probT[:, n % 3, 0:nk], bank[:, 0:nk], ACT.Copy).then_inc(pt_copied, 1)
                else:
                    A(probT[:, n % 3, 0:PAST], bank[:, 0:PAST], ACT.Copy)
                    A(probT[0:DS, n % 3, PAST:PAST + P], bank[0:DS, PAST:PAST + P], ACT.Copy).then_inc(pt_copied, 1)

            for n_ in range(ALL + 2):
                if n_ < ALL:
                    exponentials(n_)
                if n_ >= 2:
                    copy_transposed(n_ - 2)
            for t in range(T):
                act.wait_ge(ss2_ready, t + 1)
                A(small[:, 45 + t:46 + t], small[:, 40 + t:41 + t], ACT.Sqrt, scale=1.0 / D,
                  bias=eps_col[:, 0:1]).then_inc(rt2_ready, 1)
                for g in range(2):
                    act.wait_ge(h2t_done, 2 * t + g + 1)
                    A(h2T[:, 4 * g:4 * g + 4, t * P:(t + 1) * P],
                      ps[:, 4 + g].rearrange("p (c k) -> p c k", c=4), ACT.Copy).then_inc(h2t_copied, 1)

            def copy_queries(h):
                act.wait_ge(pq_done, h + 1)
                if h >= 2:
                    act.wait_ge(sc_done, h - 1)
                s = h % 2
                A(pq[:, s, :, 0:SEQ], ps[:, 0:2, :], ACT.Copy)
                link(A(pq[:, s, :, SEQ:NT], ps[:, 2, 0:2 * P].rearrange("p (c k) -> p c k", c=2), ACT.Copy))
                A(pq2[:, s], pq[:, s], ACT.Square).then_inc(pq_copied, 1)

            def copy_scores(h):
                act.wait_ge(sc_done, h + 1)
                if h >= 1:
                    act.wait_ge(rs3_ready, h)
                A(small[:, 50:55], ps[:, 6, 0:T], ACT.Sqrt, scale=1.0 / (2 * P), bias=eps_col[:, 0:1]).then_inc(rt3_ready, 1)
                act.wait_ge(rs3_ready, h + 1)
                for t in range(T):
                    ins = A(sc[:, t, h], ps[:, 3 + t // 2, 256 * (t % 2):256 * (t % 2) + 256], ACT.Copy,
                            scale=small[:, 55 + t:56 + t])
                ins.then_inc(sc_copied, 1)

            copy_queries(0)
            for h in range(PH):
                if h + 1 < PH:
                    copy_queries(h + 1)
                copy_scores(h)
            with act.Fori(0, T) as t:
                act.wait_ge(gate_in, t + 1)
                A(cv[:], cv[:], ACT.Exp).then_inc(gate_exp, 1)

            def take_indices(ix, ready, first, half):
                A(ix[:, half], eidx[:, bass.ds(first, XCHG)], ACT.Copy).then_inc(ready, 1)

            act.wait_ge(topk_done, T)
            for half in range(2):
                take_indices(ixu, ixu_ready, half * XCHG, half)
                take_indices(ixv, ixv_ready, half * XCHG, half)
            with act.Fori(0, T) as t:
                with act.Fori(0, GI) as j:
                    i = t * GI + j
                    for half in range(2):
                        act.wait_ge(dots_done, 2 * i + half + 3)
                        A(gelu[:, half], dots[:, half], ACT.Gelu).then_inc(gelu_done, 1)
                        take_indices(ixu, ixu_ready, (i + 1) * 2 * XCHG + XCHG * half, half)
                    for half in range(2):
                        act.wait_ge(v_loaded[half], 16 * XCHG * i + 16 * XCHG)
                        act.sem_inc(wait_carrier, 1)
                        take_indices(ixv, ixv_ready, (i + 1) * 2 * XCHG + XCHG * half, half)
                act.wait_ge(ss3_ready, t + 1)
                A(small[:, 61:62], small[:, 60:61], ACT.Sqrt, scale=1.0 / D, bias=eps_col[:, 0:1]).then_inc(rt4_ready, 1)

        @block.tensor
        def _(pe):
            mm, tr = nc.tensor.matmul, nc.tensor.transpose
            identb, fmask, mmask, nmask = cb[:, 0:P], cb[:, P:2 * P], cb[:, 2 * P:3 * P], cb[:, 3 * P:3 * P + DS]
            pe.wait_ge(c_loaded, 16 * 11)
            for k in range(KD):
                pe.wait_ge(squares, k + 1)
                mm(ps[:, 0, :], ones[:], sq[:, k, 0:SEQ], start=(k == 0), stop=(k == KD - 1))
                last = mm(ps[:, 1, 0:P], ones[:], sq[:, k, SEQ:NT], start=(k == 0), stop=(k == KD - 1))
            last.then_inc(meansq, 1)
            for n in range(23):
                if n >= 4:
                    pe.wait_ge(proj_copied, n - 3)
                bank = ps[:, 2 + n % 4]
                if n in (0, 5, 10, 15):
                    pe.wait_ge({0: wr_loaded, 5: wk_loaded, 10: wv_loaded, 15: wq_loaded}[n], 16)
                for k in range(KD):
                    if n == 0:
                        pe.wait_ge(h_ready, k + 1)
                    on = dict(start=(k == 0), stop=(k == KD - 1))
                    if n < 15:
                        t, w = n % 5, (wr, wk, wv)[n // 5]
                        last = mm(bank[:, 0:w.shape[2]], hT[:, k, t * P:(t + 1) * P], w[:, k, :], **on)
                    else:
                        c, part = divmod(n - 15, 2)
                        last = mm(bank[:, 0:P] if part else bank, wq[:, k, c * P:(c + 1) * P],
                                  hT[:, k, SEQ:NT] if part else hT[:, k, 0:SEQ], **on)
                last.then_inc(proj_done, 1)
            for u in range(10):
                if u == 0:
                    pe.wait_ge(rows_ready, 1)
                if u >= 2:
                    pe.wait_ge(tr_copied, u - 1)
                t = u % 5
                src = [cqn[:, t, 0:P], cqn[:, t, P:2 * P], ckvn[:, t], krl[:, t]] if u < 5 else \
                      [fk[:, t, c * P:(c + 1) * P] for c in range(4)]
                for c in range(4):
                    last = tr(ps[:, 6 + u % 2, c * P:(c + 1) * P], src[c], ident[:])
                last.then_inc(tr_done, 1)
            pe.wait_ge(wu_loaded, 16 * 4)
            pe.wait_ge(tr_copied, 5)
            pe.wait_ge(proj_copied, 23)
            for h in range(MH):
                b = 3 * (h % 2)
                if h >= 2:
                    pe.wait_ge(mq_nope, h - 1)
                    pe.wait_ge(mq_rope, h - 1)
                for k in range(2):
                    on = dict(start=(k == 0), stop=(k == 1))
                    mm(ps[0:96, b, :], w_uq[:, k, h, 0:96], zT[:, 0:TP, k, :], **on)
                    mm(ps[64:96, b + 1, :], w_uq[:, k, h, 96:P], zT[:, 0:TP, k, :], **on)
                for k in range(2):
                    mm(ps[0:96, b + 2, 0:P], w_uq[:, k, h, 0:96], zT[:, TP, k, :], start=(k == 0), stop=(k == 1))
                for k in range(2):
                    last = mm(ps[64:96, b + 2, P:2 * P], w_uq[:, k, h, 96:P], zT[:, TP, k, :],
                              start=(k == 0), stop=(k == 1))
                last.then_inc(mq_done, 1)
            pe.wait_ge(mq_nope, MH)
            pe.wait_ge(mq_rope, MH)
            for u in range(12):
                if u >= 4:
                    pe.wait_ge(mk_copied, u - 3)
                if u < 8:
                    mm(ps[0:NOPE, u % 4], w_uk[:, u], zT[:, 0:TP, 2, :], start=True, stop=True).then_inc(mk_done, 1)
                else:
                    mm(ps[:, u % 4], zT[:, u - 8, 2, :], w_uv[:], start=True, stop=True).then_inc(mk_done, 1)
            for h in range(MH):
                last = mm(ps[:, 4 + h // 4, (h % 4) * P:(h % 4 + 1) * P], w_ukT[0:NOPE, h], qmT[0:NOPE, h, SEQ:NT],
                          start=True, stop=True)
                if h % 4 == 3:
                    last.then_inc(qp_done, 1)

            def scores(n):
                bank = ps[:, n % 3]
                if n >= 3:
                    pe.wait_ge(exp_done, n - 2)
                if n == 0:
                    pe.wait_ge(mk_copied, 12)
                    pe.wait_ge(nc_ready, 1)
                if n == 32:
                    pe.wait_ge(kr_copied, MH)
                if n < UNITS:
                    kind, c, hh, i, nk = unit(n)
                    h = 2 * c + hh
                    diag = bank[:, i * P:(i + 1) * P]
                    if kind == 0:
                        rows = slice(64 * hh, 64 * hh + 64)
                        mm(bank[:, 0:nk], fqT[rows, c, i * P:(i + 1) * P], kT[rows, c, 0:nk], start=True, stop=False)
                        mm(bank[:, 0:nk], selh[0:FH, h], ncT[0:FH, 0:nk], start=False, stop=False)
                        mm(diag, identb, fmask, start=False, stop=True).then_inc(s_done, 1)
                    else:
                        mm(bank[:, 0:nk], qmT[0:96, h, i * P:(i + 1) * P], kmT[0:96, h, 0:nk], start=True, stop=False)
                        mm(diag, identb, mmask, start=False, stop=True).then_inc(s_done, 1)
                    return
                b, kind = divmod(n - UNITS, 2)
                s = b % 2
                if kind == 0:
                    pe.wait_ge(batch_loaded[s], 16 * 7 * (b // 2 + 1))
                    pe.wait_ge(new_keys, 3 * (b + 1))
                    if b == 0:
                        pe.wait_ge(qbd_ready, 8)
                        pe.wait_ge(ncs_ready, 1)
                        pe.wait_ge(qs_ready, 3)
                    for c in range(4):
                        mm(bank[:, 0:L], qbd[:, c, b].rearrange("p h q -> p (h q)"), kTs[:, s, c], start=(c == 0), stop=False)
                    mm(bank[:, 0:L], selb[0:64, b], ncS[0:64], start=False, stop=False)
                    mm(bank[:, PAST:L], identb, nmask, start=False, stop=True).then_inc(s_done, 1)
                else:
                    mm(bank[:, 0:L], qps[:, b].rearrange("p h q -> p (h q)"), ckTs[:, s], start=True, stop=False)
                    mm(bank[:, 0:L], qrs[64:96, b].rearrange("p h q -> p (h q)"), krTs[64:96, s],
                       start=False, stop=True).then_inc(s_done, 1)

            def transpose_probabilities(n):
                pe.wait_ge(p_ready, n + 1)
                if n >= 2:
                    pe.wait_ge(pt_copied, n - 1)
                nk = keys_of(n)
                for c in range((nk + P - 1) // P):
                    w = min(P, nk - c * P)
                    last = tr(ps[0:w, 3 + n % 2, c * P:(c + 1) * P], prob[:, n % 4, c * P:c * P + w], ident[:])
                last.then_inc(pt_done, 1)

            def values(n):
                pe.wait_ge(pt_copied, n + 1)
                pT = probT[:, n % 3]
                if n < UNITS:
                    kind, c, hh, i, nk = unit(n)
                    pair = n // 8
                    if n % 8 == 0 and pair >= 2:
                        pe.wait_ge(o_copied, pair - 1)
                    rows = slice(64 * hh, 64 * hh + 64)
                    for k in range(i + 1):
                        v = (fv, vm)[kind][:, k, (2 * c + hh) * 64:(2 * c + hh + 1) * 64]
                        last = mm(ps[rows, 5 + pair % 2, i * P:(i + 1) * P], v, pT[:, k * P:(k + 1) * P],
                                  start=(k == 0), stop=(k == i))
                    last.then_inc(pv_done, 1)
                    return
                m = n - UNITS
                b, kind = divmod(m, 2)
                s = b % 2
                pe.wait_ge(o_copied, 8 + m - 1)
                bank = ps[:, 5 + m % 2]
                for c in range(4 if kind == 0 else 1):
                    for k in range(3):
                        rows = slice(0, P if k < 2 else DS)
                        on = dict(start=(k == 0), stop=(k == 2))
                        if kind == 0:
                            v = vs[:, s, k, c * P:(c + 1) * P] if k < 2 else vn[0:DS, s, c * P:(c + 1) * P]
                            last = mm(bank[:, 32 * c:32 * c + 32], v, pT[rows, k * P + 32 * c:k * P + 32 * c + 32], **on)
                        else:
                            v = ckr[:, s, k] if k < 2 else ckn[0:DS, s]
                            last = mm(bank[:, 0:P], v, pT[rows, k * P:(k + 1) * P], **on)
                last.then_inc(pv_done, 1)

            for n in range(ALL + 3):
                if n >= UNITS + 3:
                    values(n - 3)
                if n < ALL:
                    scores(n)
                if 2 <= n < ALL + 2:
                    transpose_probabilities(n - 2)
                if 3 <= n < UNITS + 3:
                    values(n - 3)
            pe.wait_ge(o_copied, 8 + 2 * DB)
            for h in range(MH):
                last = mm(ps[64 * (h % 2):64 * (h % 2) + 64, 7, (h // 2) * P:(h // 2 + 1) * P],
                          w_uv[:, h * VD:(h + 1) * VD], latT[:, h], start=True, stop=True)
            last.then_inc(up_done, 1)

            def project_out(t):
                if t == 0:
                    pe.wait_ge(wo_loaded, 16)
                    pe.wait_ge(o_copied, 8 + 2 * DB + 1)
                if t >= 2:
                    pe.wait_ge(x2_ready, t - 1)
                for j in range(2):
                    for c in range(8):
                        last = mm(ps[:, 2 * (t % 2) + j], oT[:, c, t * P:(t + 1) * P], w_o[:, c, j * 512:(j + 1) * 512],
                                  start=(c == 0), stop=(c == 7))
                last.then_inc(out_done, 1)

            def transpose_h2(t):
                pe.wait_ge(h2_ready, t + 1)
                for g in range(2):
                    if t >= 1:
                        pe.wait_ge(h2t_copied, 2 * (t - 1) + g + 1)
                    for c in range(4):
                        k = 4 * g + c
                        last = tr(ps[:, 4 + g, c * P:(c + 1) * P], h2[:, t, k * P:(k + 1) * P], ident[:])
                    last.then_inc(h2t_done, 1)

            project_out(0)
            for t in range(T):
                if t + 1 < T:
                    project_out(t + 1)
                transpose_h2(t)

            def queries(h):
                pe.wait_ge(wpq_loaded[h % 2], 16 * (h // 2 + 1))
                if h == 0:
                    pe.wait_ge(h2t_copied, 2 * T)
                    pe.wait_ge(x2_ready, T)
                else:
                    pe.wait_ge(pq_copied, h)
                for k in range(KD):
                    for c in range(2):
                        mm(ps[:, c], wpq[:, h % 2, k, c * P:(c + 1) * P], h2T[:, k, 0:SEQ], start=(k == 0), stop=(k == KD - 1))
                for c in range(2):
                    for k in range(KD):
                        last = mm(ps[:, 2, c * P:(c + 1) * P], wpq[:, h % 2, k, c * P:(c + 1) * P], h2T[:, k, SEQ:NT],
                                  start=(k == 0), stop=(k == KD - 1))
                last.then_inc(pq_done, 1)

            def key_scores(h):
                pe.wait_ge(pq_copied, h + 1)
                if h == 0:
                    pe.wait_ge(late_loaded, 16 * 4)
                else:
                    pe.wait_ge(sc_copied, h)
                for t in range(T):
                    for c in range(2):
                        mm(ps[:, 3 + t // 2, 256 * (t % 2) + c * P:256 * (t % 2) + (c + 1) * P],
                           pq[:, h % 2, c, t * P:(t + 1) * P], keysT[:, 2 * h + c], start=True, stop=True)
                for t in range(T):
                    for c in range(2):
                        last = mm(ps[:, 6, t:t + 1], pq2[:, h % 2, c, t * P:(t + 1) * P], ones[:, 0:1],
                                  start=(c == 0), stop=(c == 1))
                last.then_inc(sc_done, 1)

            queries(0)
            for h in range(PH):
                if h + 1 < PH:
                    queries(h + 1)
                key_scores(h)

        @block.vector
        def _(dve):
            V = nc.vector
            n = [0]

            def link(ins):
                n[0] += 1
                ins.then_inc(dve_chain, 1)
                dve.wait_ge(dve_chain, n[0])

            V.memset(krl[:], 0.0)
            link(V.memset(eps_col[:], EPS))
            dve.wait_ge(c_loaded, 16 * 11)
            dve.wait_ge(rms_ready, 2)
            link(V.reciprocal(rstdb[:], rmsb[:]))
            for k in range(KD):
                V.scalar_tensor_tensor(out=hT[:, k], in0=hT[:, k], scalar=gm[:, k:k + 1], in1=rstdb[:],
                                       op0=ALU.mult, op1=ALU.mult).then_inc(h_ready, 1)
            dve.wait_ge(proj_copied, 5)
            for t in range(T):
                for q, (off, width) in enumerate(((R_CQ, QL), (R_CKV, KVL))):
                    a = zr[:, t, off:off + width]
                    ins = V.tensor_tensor_reduce(out=(cqn, ckvn)[q][:, t], in0=a, in1=a, scale=1.0, scalar=0.0, op0=ALU.mult,
                                                 op1=ALU.add, accum_out=small[:, 5 * q + t:5 * q + t + 1])
            ins.then_inc(ss_ready, 1)
            x_ff = krl[:, :, 32:40]
            link(V.tensor_tensor(x_ff, zr[:, :, R_FF:R_FF + FH], bfb[:], ALU.add))
            V.scalar_tensor_tensor(out=krl[:, :, 24:32], in0=x_ff, scalar=-1.0, in1=x_ff, op0=ALU.mult,
                                   op1=ALU.min).then_inc(ff_abs, 1)
            cos, sin = c_rrow[:, 0], c_rrow[:, 1]
            k1_, k2_ = zr[:, :, R_KR:R_KR + 16], zr[:, :, R_KR + 16:RW]
            V.tensor_tensor(krl[:, :, 64:80], k1_, cos, ALU.mult)
            V.tensor_tensor(krl[:, :, 80:96], k1_, sin, ALU.mult)
            V.tensor_tensor(krl[:, :, 96:112], k2_, sin, ALU.mult)
            link(V.tensor_tensor(krl[:, :, 112:128], k2_, cos, ALU.mult))
            V.tensor_tensor(krl[:, :, 64:80], krl[:, :, 64:80], krl[:, :, 96:112], ALU.subtract)
            V.tensor_tensor(krl[:, :, 80:96], krl[:, :, 80:96], krl[:, :, 112:128], ALU.add)
            dve.wait_ge(rt_ready, 1)
            link(V.reciprocal(small[:, 20:30], small[:, 10:20]))
            for t in range(T):
                V.scalar_tensor_tensor(out=cqn[:, t], in0=zr[:, t, R_CQ:R_CKV], scalar=small[:, 20 + t:21 + t], in1=gq[:],
                                       op0=ALU.mult, op1=ALU.mult)
                V.scalar_tensor_tensor(out=ckvn[:, t], in0=zr[:, t, R_CKV:R_KR], scalar=small[:, 25 + t:26 + t], in1=gkv[:],
                                       op0=ALU.mult, op1=ALU.mult)
            dve.wait_ge(ff_log, 1)
            V.scalar_tensor_tensor(out=krl[:, :, 0:FH], in0=x_ff, scalar=0.0, in1=krl[:, :, 16:24],
                                   op0=ALU.min, op1=ALU.subtract).then_inc(rows_ready, 1)
            dve.wait_ge(tr_copied, 5)
            dve.wait_ge(proj_done, 23)
            lf = prob[0:FH, 0, :]
            link(V.tensor_scalar(lf.rearrange("p (t k) -> p t k", t=TP), zT[0:FH, 0:TP, 3, :], -1.0, None, ALU.mult))
            link(V.memset(prob[0:64, 1, :], 1.0))
            V.tensor_tensor_scan(ncT[0:FH], prob[0:FH, 1, :], lf, 0.0, ALU.mult, ALU.add).then_inc(nc_ready, 1)
            rr = slice(64, 96)
            for h in range(MH):
                b = 3 * (h % 2)
                dve.wait_ge(mq_done, h + 1)
                t1, t2 = prob[rr, 2], prob[rr, 3]
                V.tensor_tensor(t1, ps[rr, b], c_rope[rr, 0, 0:SEQ], ALU.mult)
                V.tensor_tensor(t2, ps[rr, b + 1], c_rope[rr, 1, 0:SEQ], ALU.mult)
                V.tensor_tensor(probT[rr, 0, 0:P], ps[rr, b + 2, 0:P], c_rope[rr, 0, SEQ:NT], ALU.mult)
                link(V.tensor_tensor(probT[rr, 1, 0:P], ps[rr, b + 2, P:2 * P], c_rope[rr, 1, SEQ:NT], ALU.mult))
                V.tensor_tensor(qmT[rr, h, 0:SEQ], t1, t2, ALU.add)
                V.tensor_tensor(qmT[rr, h, SEQ:NT], probT[rr, 0, 0:P], probT[rr, 1, 0:P], ALU.add).then_inc(mq_rope, 1)
                dve.wait_ge(mq_rope, h + 1)
            dve.wait_ge(lfs_loaded, 16 * (1 + DB))
            link(V.tensor_scalar(lfs[0:64], lfs[0:64], -1.0, None, ALU.mult))
            V.tensor_tensor_scan(ncS[0:64], prob[0:64, 1, 0:L], lfs[0:64], 0.0, ALU.mult, ALU.add).then_inc(ncs_ready, 1)
            dve.wait_ge(ncs_ready, 1)

            def row_max(n):
                dve.wait_ge(s_done, n + 1)
                V.tensor_reduce(small[:, 32 + n % 4:33 + n % 4], ps[:, n % 3, 0:keys_of(n)], AX.X, ALU.max,
                                negate=True).then_inc(max_ready, 1)

            def normalise(n):
                dve.wait_ge(exp_done, n + 1)
                q = small[:, 36 + n % 4:37 + n % 4]
                link(V.reciprocal(q, q))
                pr = prob[:, n % 4, 0:keys_of(n)]
                V.tensor_scalar(pr, pr, q, None, ALU.mult).then_inc(p_ready, 1)

            def copy_out(n):
                dve.wait_ge(pv_done, n + 1)
                if n < UNITS:
                    V.tensor_copy(oT[:, n // 8, 0:SEQ], ps[:, 5 + n // 8 % 2]).then_inc(o_copied, 1)
                    return
                m = n - UNITS
                b, kind = divmod(m, 2)
                bank = ps[:, 5 + m % 2, 0:P]
                new = slice(SEQ + b * DS, SEQ + (b + 1) * DS)
                if kind == 0:
                    for hh in range(2):
                        rows = slice(64 * hh, 64 * hh + 64)
                        ins = V.tensor_copy(oT[rows, 0:4, new],
                                            bank[rows].rearrange("p (c x) -> p c x", c=4)[:, :, DS * hh:DS * hh + DS])
                    ins.then_inc(o_copied, 1)
                else:
                    if b == 0:
                        dve.wait_ge(wo_loaded, 16)
                    V.tensor_copy(latT[:, :, b * DS:(b + 1) * DS], bank.rearrange("p (h q) -> p h q", h=MH)).then_inc(o_copied, 1)

            for n_ in range(ALL + 4):
                if n_ < ALL:
                    row_max(n_)
                if 1 <= n_ <= ALL:
                    normalise(n_ - 1)
                if n_ >= 4 and (n_ - 4 >= UNITS or (n_ - 4) % 8 == 7):
                    copy_out(n_ - 4)
            dve.wait_ge(up_done, 1)
            V.tensor_copy(oT[:, 4:8, SEQ:NT], ps[:, 7].rearrange("p (c k) -> p c k", c=4)).then_inc(o_copied, 1)
            dve.wait_ge(late_loaded, 48)
            for t in range(T):
                dve.wait_ge(out_done, t + 1)
                V.tensor_tensor(x2[:, t], x2[:, t], ps[:, 2 * (t % 2):2 * (t % 2) + 2].rearrange("p a b -> p (a b)"),
                                ALU.add).then_inc(x2_ready, 1)
                dve.wait_ge(x2_ready, t + 1)
                V.tensor_tensor_reduce(out=h2[:, t], in0=x2[:, t], in1=x2[:, t], scale=1.0, scalar=0.0, op0=ALU.mult,
                                       op1=ALU.add, accum_out=small[:, 40 + t:41 + t]).then_inc(ss2_ready, 1)
                dve.wait_ge(rt2_ready, t + 1)
                link(V.reciprocal(small[:, 45 + t:46 + t], small[:, 45 + t:46 + t]))
                V.scalar_tensor_tensor(out=h2[:, t], in0=x2[:, t], scalar=small[:, 45 + t:46 + t], in1=gffn[:],
                                       op0=ALU.mult, op1=ALU.mult).then_inc(h2_ready, 1)
            for h in range(PH):
                dve.wait_ge(rt3_ready, h + 1)
                if h >= 1:
                    dve.wait_ge(sc_copied, h)
                V.reciprocal(small[:, 55:60], small[:, 50:55]).then_inc(rs3_ready, 1)
            dve.wait_ge(sc_copied, PH)
            dve.wait_ge(h2_ready, T)
            link(V.memset(onehot[:, 0, :], 1.0))
            link(V.tensor_tensor_scan(onehot[:, 1, :], onehot[:, 0, :], onehot[:, 0, :], -1.0, ALU.mult, ALU.add))
            link(V.tensor_copy(iota[:], onehot[:, 1, :]))
            LINKS = 13
            with dve.Fori(0, T) as t:
                q = [0]

                def step(ins):
                    q[0] += 1
                    ins.then_inc(dve_loop, 1)
                    dve.wait_ge(dve_loop, t * LINKS + q[0])
                    dve.sem_inc(wait_carrier, 1)

                step(V.tensor_copy(sw[:].rearrange("p h c k -> p (h c k)"),
                                   sc[:].rearrange("p t h k -> p t (h k)")[:, bass.ds(t, 1), :].rearrange("p a k -> p (a k)")))

                def top16(src, rest, val, idx):
                    for s, v in zip(src, val):
                        ins = V.max(v[:, 0:8], s)
                    step(ins)
                    for s, r_, v, i_ in zip(src, rest, val, idx):
                        V.max_index(i_[:, 0:8], v[:, 0:8], s)
                        ins = V.match_replace(r_, v[:, 0:8], s, NEG)
                    step(ins)
                    for r_, v in zip(rest, val):
                        ins = V.max(v[:, 8:16], r_)
                    step(ins)
                    for r_, v, i_ in zip(rest, val, idx):
                        ins = V.max_index(i_[:, 8:16], v[:, 8:16], r_)
                    step(ins)

                both = [(h, c) for h in range(PH) for c in range(2)]
                top16([sw[:, h, c] for h, c in both], [sr[:, h, c] for h, c in both],
                      [v16[:, h, c] for h, c in both], [i16[:, h, c] for h, c in both])
                a = v16[:, :, 0, :].unsqueeze(3).broadcast_to([P, PH, TK, TK])
                b_ = v16[:, :, 1, :].unsqueeze(2).broadcast_to([P, PH, TK, TK])
                step(V.tensor_tensor(cand[:], a, b_, ALU.add))
                flat = lambda x, h: x[:, h].rearrange("p a b -> p (a b)")
                top16([flat(cand, h) for h in range(PH)], [flat(candr, h) for h in range(PH)],
                      [cv[:, h] for h in range(PH)], [ci[:, h] for h in range(PH)])
                cflat = ci[:].rearrange("p h k -> p (h k)")
                V.tensor_scalar(hi[:], cflat, 4, None, ALU.logical_shift_right)
                V.tensor_scalar(lo[:], cflat, TK - 1, None, ALU.bitwise_and)
                step(V.tensor_copy(gsum[:, 2].unsqueeze(2), cv[:, :, 0:1]))
                V.tensor_tensor(cv[:], cv[:], gsum[:, 2].unsqueeze(2).broadcast_to([P, PH, TK]), ALU.subtract).then_inc(gate_in, 1)
                for pos, c, e in ((hi, 0, e1), (lo, 1, e2)):
                    V.tensor_tensor(onehot[:], pos[:].unsqueeze(2).broadcast_to([P, SEL, TK]),
                                    iota[:].unsqueeze(1).broadcast_to([P, SEL, TK]), ALU.is_equal).then_inc(tile_in, 1)
                    dve.wait_ge(tile_in, t * 6 + 3 * c + 1)
                    V.tensor_tensor(onehot[:].rearrange("p (h k) j -> p h k j", h=PH), onehot[:].rearrange("p (h k) j -> p h k j", h=PH),
                                    i16[:, :, c, :].unsqueeze(2).broadcast_to([P, PH, TK, TK]), ALU.mult).then_inc(tile_in, 1)
                    dve.wait_ge(tile_in, t * 6 + 3 * c + 2)
                    V.tensor_reduce(e[:], onehot[:], AX.X, ALU.add).then_inc(tile_in, 1)
                    dve.wait_ge(tile_in, t * 6 + 3 * c + 3)
                V.scalar_tensor_tensor(out=eidx[:, bass.ds(t * SEL, SEL)], in0=e1[:], scalar=float(NK), in1=e2[:],
                                       op0=ALU.mult, op1=ALU.add)
                dve.wait_ge(gate_exp, t + 1)
                step(V.tensor_reduce(gsum[:, 0], cv[:], AX.X, ALU.add))
                step(V.reciprocal(gsum[:, 1], gsum[:, 0]))
                V.tensor_tensor(gate[:, bass.ds(t * SEL, SEL)].rearrange("p (h k) -> p h k", h=PH), cv[:],
                                gsum[:, 1].unsqueeze(2).broadcast_to([P, PH, TK]), ALU.mult).then_inc(topk_done, 1)
                dve.wait_ge(topk_done, t + 1)
                dve.sem_inc(wait_carrier, 1)
                assert q[0] == LINKS, q[0]
            V.memset(eidx[:, NT:NT + 2 * XCHG].bitcast(F32), 0.0)
            dve.wait_ge(topk_done, T)
            V.memset(gscr[:, 0:8], 0.0).then_inc(dots_done, 2)
            V.memset(gscr[:, 8:16], 0.0).then_inc(acc_done, 2)
            dve.wait_ge(acc_done, 2)
            y_link = sem("y_link")
            XL = 2 * (XCHG + 1) - 2
            with dve.Fori(0, T) as t:
                row = lambda x: x[:, bass.ds(t, 1), :].rearrange("p a k -> p (a k)")
                with dve.Fori(0, GI) as j:
                    i = t * GI + j
                    for half in range(2):
                        dve.wait_ge(u_loaded[half], 16 * XCHG * i + 16 * XCHG)
                        for s in range(XCHG):
                            ins = V.scalar_tensor_tensor(out=ubuf[:, half, s], in0=ubuf[:, half, s], scalar=1.0, in1=row(h2),
                                                         op0=ALU.mult, op1=ALU.mult, accum_out=dots[:, half, s:s + 1])
                        ins.then_inc(dots_done, 1)
                    q = 0
                    for half in range(2):
                        dve.wait_ge(gelu_done, 2 * i + half + 1)
                        V.tensor_tensor(wts[:, half], gelu[:, half], gate[:, bass.ds(i * 2 * XCHG + XCHG * half, XCHG)],
                                        ALU.mult).then_inc(y_link, 1)
                        q += 1
                        dve.wait_ge(y_link, i * XL + q)
                        dve.wait_ge(v_loaded[half], 16 * XCHG * i + 16 * XCHG)
                        for s in range(XCHG):
                            ins = V.scalar_tensor_tensor(out=row(x2), in0=vbuf[:, half, s], scalar=wts[:, half, s:s + 1],
                                                         in1=row(x2), op0=ALU.mult, op1=ALU.add)
                            if s < XCHG - 1:
                                q += 1
                                ins.then_inc(y_link, 1)
                                dve.wait_ge(y_link, i * XL + q)
                        ins.then_inc(acc_done, 1)
                        dve.wait_ge(acc_done, 2 * i + half + 3)
                    assert q == XL
                dve.wait_ge(y_free, t + 1)
                V.scalar_tensor_tensor(out=gscr[:], in0=row(x2), scalar=1.0, in1=row(x2), op0=ALU.mult, op1=ALU.mult,
                                       accum_out=small[:, 60:61]).then_inc(ss3_ready, 1)
                dve.wait_ge(rt4_ready, t + 1)
                V.reciprocal(small[:, 62:63], small[:, 61:62]).then_inc(tile_in, 1)
                dve.wait_ge(tile_in, T * 6 + t + 1)
                V.scalar_tensor_tensor(out=yout[:], in0=row(x2), scalar=small[:, 62:63], in1=gfin[:],
                                       op0=ALU.mult, op1=ALU.mult).then_inc(y_ready, 1)


def _rope_tables():
    half = ROPE // 2
    inv = (np.float32(10000.0) ** (-np.arange(half, dtype=np.float32) / np.float32(half))).astype(np.float32)
    pos = np.concatenate([np.arange(SEQ), np.tile(PAST + np.arange(DS), DB)]).astype(np.float32)
    ang = pos[:, None] * inv[None, :]
    return np.cos(ang).astype(np.float32), np.sin(ang).astype(np.float32)


def _constants():

    cos, sin = _rope_tables()
    j = np.arange(P) % 32
    sign = np.where(j < 16, -1.0, 1.0).astype(np.float32)[:, None]
    c_rope = np.stack([cos.T[j % 16], sin.T[j % 16] * sign], 1) * np.float32(MLA_SCALE)
    c_rrow = np.stack([cos, sin]).reshape(2, T, P, 16).transpose(2, 0, 1, 3)
    selh = np.zeros((FH, FH, P), np.float32)
    selh[np.arange(FH), np.arange(FH)] = 1
    selb = np.zeros((DB, FH, DB, FH, DS), np.float32)
    for b in range(DB):
        for h in range(FH):
            selb[b, h, b, h] = 1
    q, k = np.arange(P)[:, None], np.arange(P)[None]
    fmask = np.where(k <= q, 0, NEG)
    mmask = np.where(k // 64 <= q // 64, 0, NEG)
    nmask = np.where(np.arange(DS)[None] <= q % DS, 0, NEG)
    cb = np.concatenate([np.eye(P), fmask, mmask, nmask], 1).astype(mybir.dt.np(BF16))
    return {"ident": np.eye(P, dtype=np.float32), "ones": np.ones((P, P), np.float32), "c_rope": c_rope.astype(np.float32),
            "c_rrow": c_rrow, "selh": selh, "selb": selb.reshape(DB * FH, DB, P), "cb": cb}


def _arrays(i):
    f = lambda x: np.asarray(x)
    fold = lambda w: w.reshape(KD, P, -1).transpose(1, 0, 2)
    x = np.concatenate([f(i["x_prompt"]).reshape(SEQ, D), f(i["x_sample"]).reshape(DB * DS, D)])
    w_in = f(i["w_in"])[0]
    fw = FH * HD
    w_ukv = f(i["w_ukv"])[0].reshape(KVL, MH, NOPE + VD)
    w_uq = f(i["w_uq"])[0].reshape(2, P, MH, NOPE + ROPE).transpose(1, 0, 2, 3)
    r1, r2 = w_uq[..., NOPE:NOPE + 16], w_uq[..., NOPE + 16:]
    ck = f(i["cache_fox_k"])[0].reshape(DB, PAST, 4, P)
    keys = f(i["peer_sub_keys"])[0]
    tile = lambda v: np.broadcast_to(v, (P,) + v.shape)
    return {
        **_constants(),
        "xT": fold(x.T), "xr": x,
        "gm": f(i["g_mix"])[0].reshape(KD, P).T,
        "wr": fold(w_in[:, 3 * fw:]), "wk": fold(w_in[:, fw:2 * fw]), "wv": fold(w_in[:, 2 * fw:3 * fw]), "wq": fold(w_in[:, :fw]),
        "bfb": tile(np.broadcast_to(f(i["b_f"])[0], (T, FH))),
        "gq": tile(f(i["g_q"])[0]), "gkv": tile(f(i["g_kv"])[0]),
        "w_uq": np.concatenate([w_uq, r2, r1], -1),
        "w_uk": w_ukv[..., :NOPE], "w_uv": w_ukv[..., NOPE:].reshape(KVL, MH * VD),
        "w_ukT": w_ukv[..., :NOPE].transpose(2, 1, 0),
        "past_k": ck.transpose(0, 3, 2, 1), "past_v": f(i["cache_fox_v"])[0].reshape(DB, PAST, fw),
        "past_logf": f(i["cache_fox_logf"])[0].transpose(0, 2, 1).reshape(DB * FH, PAST),
        "past_ckv": f(i["cache_mla_ckv"])[0], "past_ckvT": f(i["cache_mla_ckv"])[0].transpose(0, 2, 1),
        "past_krT": f(i["cache_mla_krope"])[0].transpose(0, 2, 1),
        "w_o": f(i["w_o"])[0].reshape(8, P, D).transpose(1, 0, 2),
        "gffn": tile(f(i["g_ffn"])[0]), "gfin": tile(f(i["g_final"])),
        "wpq": f(i["w_pq"])[0].reshape(KD, P, PH, 2 * P).transpose(2, 1, 0, 3),
        "keysT": keys.transpose(3, 1, 0, 2).reshape(P, 2 * PH, NK),
        "peer_u": f(i["peer_u"])[0], "peer_v": f(i["peer_v"])[0],
    }


_OUTS = {"y": (NT, D), "fk": (NT, FH * HD), "fv": (NT, FH * HD), "logf": (NT, FH), "ckv": (NT, KVL), "krope": (NT, ROPE)}


def kernel(**inputs):
    import concourse.bacc as _bacc
    from concourse.bass_utils import run_bass_kernel_spmd as _run

    nc = _bacc.Bacc("TRN2", target_bir_lowering=False, num_devices=1)
    arrays, t_in, t_out = {}, {}, {}
    for name, a in _arrays(inputs).items():
        a = np.ascontiguousarray(a)
        arrays[f"in_{name}"] = a
        t_in[name] = nc.dram_tensor(f"in_{name}", a.shape, mybir.dt.from_np(a.dtype), kind="ExternalInput").ap()
    for name, shape in _OUTS.items():
        t_out[name] = nc.dram_tensor(f"out_{name}", shape, F32, kind="ExternalOutput").ap()
    peer_step_kernel(nc, t_in, t_out)
    r = _run(nc, [arrays], core_ids=[0]).results[0]
    o = {name: r[f"out_{name}"] for name in _OUTS}
    p = lambda name, *s: o[name][:SEQ].reshape(1, 1, SEQ, *s)
    d = lambda name, *s: o[name][SEQ:].reshape(1, DB, DS, *s)
    return (o["y"][:SEQ].reshape(1, SEQ, D), o["y"][SEQ:].reshape(DB, DS, D),
            p("fk", FH, HD), p("fv", FH, HD), p("logf", FH), p("ckv", KVL), p("krope", ROPE),
            d("fk", FH, HD), d("fv", FH, HD), d("logf", FH), d("ckv", KVL), d("krope", ROPE))
```

```python
from contextlib import ExitStack

import numpy as np
import concourse.bass as bass
from concourse import mybir

F32 = mybir.dt.float32
F32R = mybir.dt.float32r
BF16 = mybir.dt.bfloat16
U32 = mybir.dt.uint32
ALU = mybir.AluOpType
ACT = mybir.ActivationFunctionType
AX = mybir.AxisListType

P = 128
D = 1024
KD = D // P
SEQ, DB, DS, PAST = 512, 8, 16, 256
TP = SEQ // P
T = TP + 1
NT = T * P
FH, HD = 8, 64
MH, NOPE, ROPE, VD = 8, 64, 32, 64
QL, KVL = 256, 128
L = PAST + DS
R_FF, R_CQ, R_CKV, R_KR = 0, FH, FH + QL, FH + QL + KVL
RW = R_KR + ROPE
FOX_SCALE = float(HD) ** -0.5
MLA_SCALE = float(NOPE + ROPE) ** -0.5
PH, NK, TK = 8, 128, 16
SEL = PH * TK
EPS = 1e-6
NEG = -1e30
GROUP = 2
TD = 3
NTD = TD * P
TG = T - TD
BLOCKS = NK
PER = 4
GI = SEL // (PER * GROUP)
assert TG * GI * PER == BLOCKS
CHUNK = 32
CHUNKS = NTD // CHUNK


def peer_step_kernel(nc, t_in, t_out):
    base, end = 16512, 229344

    class Region:

        def __init__(self, at):
            self.at = at

        def __call__(self, name, shape, dtype=F32):
            size = int(np.prod(shape[1:])) * {F32: 4, F32R: 4, U32: 4, BF16: 2}[dtype]
            t = nc.alloc_sbuf_tensor_at(name, shape, dtype, offset=self.at)
            self.at += (size + 31) // 32 * 32
            assert self.at <= end, (name, self.at)
            return t

    with ExitStack() as ctx:
        def sem(name):
            return ctx.enter_context(nc.semaphore(name))

        r = Region(base)
        ident = r("ident", [P, P])
        ones = r("ones", [P, P])
        small = r("small", [P, 64])
        eps_col = r("eps_col", [P, 8])
        late_at = r.at
        c_rope = r("c_rope", [P, 2, NT])
        c_rrow = r("c_rrow", [P, 2, T, ROPE // 2])
        selh = r("selh", [P, FH, P])
        selb = r("selb", [P, DB, P])
        cb = r("cb", [P, 3 * P + DS], BF16)
        gm = r("gm", [P, KD])
        bfb = r("bfb", [P, T, FH])
        gq = r("gq", [P, QL])
        gkv = r("gkv", [P, KVL])
        fv = r("fv", [P, T, FH * HD])
        zT = r("zT", [P, T, 4, P])
        fqT = r("fqT", [P, 4, NT])
        kT = r("kT", [P, 4, NT])
        ncT = r("ncT", [P, SEQ])
        w_uv = r("w_uv", [P, MH * VD])
        wu_at = r.at
        w_uq = r("w_uq", [P, 2, MH, P])
        w_uk = r("w_uk", [P, MH, NOPE])
        w_ukT = r("w_ukT", [P, MH, P])
        zr_at = r.at
        zr = r("zr", [P, T, RW])
        r2_at = r.at
        krl = r("krl", [P, T, P])
        cqn = r("cqn", [P, T, QL])
        ckvn = r("ckvn", [P, T, KVL])
        fk = r("fk", [P, T, FH * HD])
        a_at = r.at
        z = Region(zr_at)
        qps = z("qps", [P, DB, MH, DS])
        qrs = z("qrs", [P, DB, MH, DS])
        assert z.at <= r2_at
        a1 = Region(a_at)
        hT = a1("hT", [P, KD, NT])
        rmsb = a1("rmsb", [P, NT])
        rstdb = a1("rstdb", [P, NT])
        wr = a1("wr", [P, KD, RW])
        wk = a1("wk", [P, KD, FH * HD])
        sq_at = a1.at
        wv = a1("wv", [P, KD, FH * HD])
        wq = a1("wq", [P, KD, FH * HD])
        sq = Region(sq_at)("sq", [P, KD, NT])
        a2 = Region(a_at)
        qmT = a2("qmT", [P, MH, NT])
        kmT = a2("kmT", [P, MH, SEQ])
        vm = a2("vm", [P, TP, MH * VD])
        prob = a2("prob", [P, 4, SEQ])
        probT = a2("probT", [P, 3, SEQ])
        qbd = a2("qbd", [P, 4, DB, FH, DS])
        oT = a2("oT", [P, 8, NT])
        s1 = Region(wu_at)
        vs = s1("vs", [P, 2, 2, FH * HD])
        ckTs = s1("ckTs", [P, 2, L])
        krTs = s1("krTs", [P, 2, L])
        assert s1.at <= zr_at
        s2 = Region(r2_at)
        kTs = s2("kTs", [P, 2, 4, L])
        vn = s2("vn", [P, 2, FH * HD])
        ckr = s2("ckr", [P, 2, 2, KVL])
        ckn = s2("ckn", [P, 2, KVL])
        lfs = s2("lfs", [P, L])
        ncS = s2("ncS", [P, L])
        assert s2.at <= a_at
        l1 = Region(late_at)
        x2 = l1("x2", [P, T, D])
        h2_at = l1.at
        h2 = l1("h2", [P, T, D])
        gfin = l1("gfin", [P, D])
        gate = l1("gate", [P, T, SEL])
        eidx = l1("eidx", [P, TG * SEL], U32)
        iota = l1("iota", [P, NK])
        e_at = l1.at
        e1 = l1("e1", [P, T, SEL])
        e2 = l1("e2", [P, T, SEL])
        gap = l1("gap", [P, T, SEL])
        g_at = l1.at
        gffn = l1("gffn", [P, D])
        h2T = l1("h2T", [P, KD, NT])
        wpq = l1("wpq", [P, 2, KD, 2 * P])
        assert l1.at <= a_at
        l2 = Region(a_at)
        w_o = l2("w_o", [P, 8, D])
        latT = l2("latT", [P, MH, P])
        assert l2.at <= a_at + 4 * MH * (NT + SEQ)
        top_at = end - 2 * 4 * KD * NTD
        hd = Region(top_at)
        hh = hd("hh", [P, KD, NTD], F32R)
        hl = hd("hl", [P, KD, NTD], F32R)
        l3 = Region(a_at)
        pq = l3("pq", [P, 2, 2, NT])
        pq2 = l3("pq2", [P, 2, 2, NT])
        keysT = l3("keysT", [P, 2 * PH, NK])
        scb = l3("scb", [P, 2, T, 2, NK])
        rt = l3("rt", [P, 2, 8])
        rs = l3("rs", [P, 8])
        sr = l3("sr", [P, T, 2, NK])
        cand = l3("cand", [P, T, TK, TK])
        candr = l3("candr", [P, T, TK, TK])
        onehot = l3("onehot", [P, T, TK, TK])
        onehot2 = l3("onehot2", [P, T, TK, TK])
        v16 = l3("v16", [P, T, 2, TK])
        i16 = l3("i16", [P, T, 2, TK], U32)
        cv = l3("cv", [P, T, TK])
        ci = l3("ci", [P, T, TK], U32)
        hi = l3("hi", [P, T, TK], U32)
        lo = l3("lo", [P, T, TK], U32)
        gsum = l3("gsum", [P, 2, T * PH])
        assert l3.at <= top_at
        k9 = Region(g_at)
        i1T = k9("i1T", [P, NTD])
        i2T = k9("i2T", [P, NTD])
        gT = k9("gT", [P, NTD])
        bsel = k9("bsel", [P, 2, CHUNK // 2, NK])
        asel = k9("asel", [P, 2, CHUNK // 2, NK])
        stage = k9("stage", [P, 2, NK, CHUNK])
        assert k9.at <= top_at
        gbuf = Region(h2_at)("gbuf", [P, 2, CHUNKS, PER, CHUNK])
        assert TD * D >= 2 * PER * NTD
        z0 = Region(e_at)
        ix = z0("ix", [P, PER, GROUP], U32)
        dots = z0("dots", [P, PER, GROUP])
        gelu = z0("gelu", [P, PER, GROUP])
        wts = z0("wts", [P, PER, GROUP])
        zero = z0("zero", [P, 512], F32R)
        actv = z0("actv", [P, 2, NTD])
        assert z0.at <= g_at
        k10 = Region(g_at)
        u_at = k10.at
        ub = k10("ub", [P, PER, KD, P])
        v_at = k10.at
        vb = k10("vb", [P, PER, D])
        ul = Region(u_at)("ul", [P, PER, KD, P], F32R)
        vl = Region(v_at)("vl", [P, PER, D], F32R)
        uh = k10("uh", [P, 2, KD, P], F32R)
        vh = k10("vh", [P, 2, D], F32R)
        ga = k10("ga", [P, 2, NTD])
        acth = k10("acth", [P, 2, NTD], F32R)
        actl = k10("actl", [P, 2, NTD], F32R)
        ubuf = k10("ubuf", [P, PER, GROUP, D])
        vbuf = k10("vbuf", [P, PER, GROUP, D])
        assert k10.at <= top_at, (k10.at, top_at)
        k11 = Region(g_at)
        yout = k11("yout", [P, T, D])

        spill = nc.dram_tensor("gate_matrix", [CHUNKS, P, NK, CHUNK], F32, kind="Internal").ap()
        ps = ctx.enter_context(nc.psum_tensor("ps", [P, 8, 512], F32))

        x_loaded, c_loaded, wr_loaded, wk_loaded, wv_loaded, wq_loaded, wu_loaded = (
            sem(n) for n in ("x_loaded", "c_loaded", "wr_loaded", "wk_loaded", "wv_loaded", "wq_loaded", "wu_loaded"))
        squares, meansq, rms_ready, h_ready = (sem(n) for n in ("squares", "meansq", "rms_ready", "h_ready"))
        proj_done, proj_copied = sem("proj_done"), sem("proj_copied")
        ss_ready, rt_ready, ff_abs, ff_log, rows_ready = (
            sem(n) for n in ("ss_ready", "rt_ready", "ff_abs", "ff_log", "rows_ready"))
        state_stored = sem("state_stored")
        tr_done, tr_copied = sem("tr_done"), sem("tr_copied")
        nc_ready, ncs_ready, lfs_loaded = sem("nc_ready"), sem("ncs_ready"), sem("lfs_loaded")
        mq_done, mq_nope, mq_rope = sem("mq_done"), sem("mq_nope"), sem("mq_rope")
        mk_done, mk_copied, kr_copied = sem("mk_done"), sem("mk_copied"), sem("kr_copied")
        qp_done, qs_ready, qbd_ready = sem("qp_done"), sem("qs_ready"), sem("qbd_ready")
        s_done, max_ready, exp_done, p_ready = sem("s_done"), sem("max_ready"), sem("exp_done"), sem("p_ready")
        pt_done, pt_copied, pv_done, o_copied = sem("pt_done"), sem("pt_copied"), sem("pv_done"), sem("o_copied")
        batch_loaded = [sem("batch_loaded0"), sem("batch_loaded1")]
        new_keys = sem("new_keys")
        up_done = sem("up_done")
        wo_loaded, late_loaded, wpq_loaded = sem("wo_loaded"), sem("late_loaded"), [sem("wpq0"), sem("wpq1")]
        out_done, x2_ready, ss2_ready, rt2_ready, h2_ready = (
            sem(n) for n in ("out_done", "x2_ready", "ss2_ready", "rt2_ready", "h2_ready"))
        h2t_done, h2t_copied = sem("h2t_done"), sem("h2t_copied")
        pq_done, pq_copied, sc_done, sc_copied, sc_read = (
            sem(n) for n in ("pq_done", "pq_copied", "sc_done", "sc_copied", "sc_read"))
        hh_ready, hl_ready = sem("hh_ready"), sem("hl_ready")
        gap_ready, gap_exp, topk_done = sem("gap_ready"), sem("gap_exp"), sem("topk_done")
        selT_done, selT_copied = sem("selT_done"), sem("selT_copied")
        sel_ready, sel_used, g_copied, g_stored = sem("sel_ready"), sem("sel_used"), sem("g_copied"), sem("g_stored")
        stage_free, bank_free, dve_loop2, dense_open = (
            sem(n) for n in ("stage_free", "bank_free", "dve_loop2", "dense_open"))
        ub_loaded = [sem(f"ub_loaded{k}") for k in range(PER)]
        vb_loaded = [sem(f"vb_loaded{k}") for k in range(PER)]
        gb_loaded = sem("gb_loaded")
        uh_ready, vh_ready, ul_ready, vl_ready = sem("uh_ready"), sem("vh_ready"), sem("ul_ready"), sem("vl_ready")
        a_done, ga_ready, act_ready, acth_ready, actl_ready, av_done = (
            sem(n) for n in ("a_done", "ga_ready", "act_ready", "acth_ready", "actl_ready", "av_done"))
        g_used, dense_done = sem("g_used"), sem("dense_done")
        ix_ready = sem("ix_ready")
        u_loaded = [sem(f"u_loaded{k}") for k in range(PER)]
        v_loaded = [sem(f"v_loaded{k}") for k in range(PER)]
        dots_done, gelu_done, acc_done, y_link = sem("dots_done"), sem("gelu_done"), sem("acc_done"), sem("y_link")
        ss3_ready, rt4_ready, y_ready, y_stored = (
            sem(n) for n in ("ss3_ready", "rt4_ready", "y_ready", "y_stored"))
        act_chain, dve_chain, dve_loop, pool_chain = (
            sem(n) for n in ("act_chain", "dve_chain", "dve_loop", "pool_chain"))
        wait_carrier = sem("wait_carrier")

        UNITS = 64
        ALL = UNITS + 2 * DB

        def unit(n):
            pair, hh, i = n // 8, n // 4 % 2, n % 4
            return pair // 4, pair % 4, hh, i, (i + 1) * P

        def keys_of(n):
            return unit(n)[4] if n < UNITS else L

        block = ctx.enter_context(nc.Block())

        @block.sync
        def _(sp):
            ld = sp.dma_start
            ld(hT[:], t_in["xT"]).then_inc(x_loaded, 16)
            for dst, name in ((ident, "ident"), (ones, "ones"), (gm, "gm"), (c_rope, "c_rope"), (c_rrow, "c_rrow"),
                              (cb, "cb"), (bfb, "bfb"), (gq, "gq"), (gkv, "gkv")):
                ld(dst[:], t_in[name]).then_inc(c_loaded, 16)
            ld(selh[0:FH], t_in["selh"]).then_inc(c_loaded, 16)
            ld(selb[0:DB * FH], t_in["selb"]).then_inc(c_loaded, 16)
            ld(wr[:], t_in["wr"]).then_inc(wr_loaded, 16)
            ld(wk[:], t_in["wk"]).then_inc(wk_loaded, 16)
            for dst, name in ((w_uq, "w_uq"), (w_uk, "w_uk"), (w_uv, "w_uv")):
                ld(dst[:], t_in[name]).then_inc(wu_loaded, 16)
            ld(w_ukT[0:NOPE], t_in["w_ukT"]).then_inc(wu_loaded, 16)
            sp.wait_ge(meansq, 1)
            ld(wv[:], t_in["wv"]).then_inc(wv_loaded, 16)
            ld(wq[:], t_in["wq"]).then_inc(wq_loaded, 16)
            sp.wait_ge(proj_copied, 15)
            rows = lambda name: t_out[name].rearrange("(t p) c -> p t c", p=P)
            ld(rows("fk"), fk[:]).then_inc(state_stored, 16)
            ld(rows("fv"), fv[:]).then_inc(state_stored, 16)
            sp.wait_ge(rows_ready, 1)
            ld(rows("ckv"), ckvn[:]).then_inc(state_stored, 16)
            ld(rows("logf"), krl[:, :, 0:FH]).then_inc(state_stored, 16)
            ld(rows("krope"), krl[:, :, 64:64 + ROPE]).then_inc(state_stored, 16)
            sp.wait_ge(state_stored, 16 * 5)
            sp.wait_ge(tr_copied, 10)
            ld(lfs[0:64, 0:PAST], t_in["past_logf"]).then_inc(lfs_loaded, 16)
            new_logf = t_out["logf"][SEQ:NT].rearrange("(b q) h -> b h q", b=DB)
            for b in range(DB):
                ld(lfs[b * FH:(b + 1) * FH, PAST:L], new_logf[b], allow_slow_non_contiguous=True).then_inc(lfs_loaded, 16)

            def load_batch(b):
                s = b % 2
                if b == 0:
                    sp.wait_ge(qs_ready, 3)
                    sp.wait_ge(mk_copied, 8)
                if b >= 2:
                    sp.wait_ge(pv_done, UNITS + 2 * (b - 2) + 2)
                q = batch_loaded[s]
                new = slice(SEQ + b * DS, SEQ + (b + 1) * DS)
                ld(kTs[:, s, :, 0:PAST], t_in["past_k"][b]).then_inc(q, 16)
                ld(vs[:, s], t_in["past_v"][b].rearrange("(j p) c -> p j c", p=P)).then_inc(q, 16)
                ld(vn[0:DS, s], t_out["fv"][new]).then_inc(q, 16)
                ld(ckTs[:, s, 0:PAST], t_in["past_ckvT"][b]).then_inc(q, 16)
                ld(krTs[64:96, s, 0:PAST], t_in["past_krT"][b]).then_inc(q, 16)
                ld(ckr[:, s], t_in["past_ckv"][b].rearrange("(j p) c -> p j c", p=P)).then_inc(q, 16)
                ld(ckn[0:DS, s], t_out["ckv"][new]).then_inc(q, 16)

            load_batch(0)
            load_batch(1)
            sp.wait_ge(pv_done, UNITS)
            ld(w_o[:], t_in["w_o"]).then_inc(wo_loaded, 16)
            for b in range(2, DB):
                load_batch(b)
            sp.wait_ge(up_done, 1)
            sp.wait_ge(o_copied, 8 + 2 * DB + 1)
            ld(x2[:], t_in["xr"].rearrange("(t p) c -> p t c", p=P)).then_inc(late_loaded, 16)
            ld(gffn[:], t_in["gffn"]).then_inc(late_loaded, 16)
            ld(gfin[:], t_in["gfin"]).then_inc(late_loaded, 16)
            ld(iota[:], t_in["iota"]).then_inc(late_loaded, 16)
            for h in range(PH):
                if h >= 2:
                    sp.wait_ge(pq_done, h - 1)
                ld(wpq[:, h % 2], t_in["wpq"][h]).then_inc(wpq_loaded[h % 2], 16)
                if h == 1:
                    sp.wait_ge(out_done, T)
                    ld(keysT[:], t_in["keysT"]).then_inc(late_loaded, 16)
            sp.sem_inc(stage_free, 2)
            with sp.Fori(0, CHUNKS) as c:
                sp.wait_ge(g_copied, (c + 1) * CHUNK // 4)
                ld(spill[bass.ds(c, 1)].rearrange("a p k t -> p (a k t)"),
                   stage[:, bass.ds(c % 2, 1)].rearrange("p a k t -> p (a k t)")).then_inc(g_stored, 16)
                sp.wait_ge(g_stored, 16 * c + 16)
                sp.sem_inc(stage_free, 1)
            sp.wait_ge(g_stored, 16 * CHUNKS)
            sp.wait_ge(sel_used, NTD + CHUNK)

            def load_u(block, slot):
                ld(ub[:, slot].rearrange("p k e -> p (k e)"),
                   t_in["peer_uT"][block].rearrange("a p k -> p (a k)")).then_inc(ub_loaded[slot], 16)

            load_u(slice(0, 1), 0)
            with sp.Fori(0, TG) as t:
                with sp.Fori(0, GI) as j:
                    i = t * GI + j
                    sp.wait_ge(g_used, i + 1)
                    for q in range(4):
                        cs = slice(q * CHUNKS // 4, (q + 1) * CHUNKS // 4)
                        ld(gbuf[:, bass.ds(i % 2, 1), cs].rearrange("p a c k t -> p (a c) (k t)"),
                           spill[cs, :, bass.ds(i * PER, PER), :].rearrange("c p k t -> p c (k t)")).then_inc(gb_loaded, 16)
                    for s in range(PER):
                        n = i * PER + s
                        sp.wait_ge(a_done, n + 1)
                        load_u(bass.ds((n + 1) % BLOCKS, 1), (s + 1) % PER)
                        sp.wait_ge(av_done, n + 1)
                        ld(vb[:, s], t_in["peer_v"][bass.ds(n * P, P), :]).then_inc(vb_loaded[s], 16)
            sp.wait_ge(ub_loaded[0], 16 * (BLOCKS // PER + 1))
            for t in range(T):
                sp.wait_ge(y_ready, t + 1)
                ld(t_out["y"][t * P:(t + 1) * P], yout[:, t]).then_inc(y_stored, 16)
            sp.wait_ge(y_stored, 16 * T)

        @block.gpsimd
        def _(pool):
            links = [0]

            def link(ins):
                links[0] += 1
                ins.then_inc(pool_chain, 1)
                pool.wait_ge(pool_chain, links[0])

            pool.wait_ge(tr_copied, 5)
            pool.wait_ge(proj_done, 23)
            for h in range(MH):
                nc.gpsimd.tensor_copy(kmT[64:96, h, :].rearrange("p (t k) -> p t k", t=TP),
                                      zT[64:96, 0:TP, 3, :]).then_inc(kr_copied, 1)
                pool.wait_ge(kr_copied, h + 1)
            link(nc.gpsimd.memset(qbd[:], 0.0))
            pool.wait_ge(proj_copied, 23)
            for c in range(4):
                for hh in range(2):
                    rows = slice(64 * hh, 64 * hh + 64)
                    nc.gpsimd.tensor_copy(qbd[rows, c, :, 2 * c + hh, :],
                                          fqT[rows, c, SEQ:NT].rearrange("p (b q) -> p b q", b=DB)).then_inc(qbd_ready, 1)
                    pool.wait_ge(qbd_ready, 2 * c + hh + 1)
            for b in range(DB):
                s = b % 2
                new = slice(b * DS, (b + 1) * DS)
                if b == 0:
                    pool.wait_ge(state_stored, 16 * 5)
                    pool.wait_ge(qs_ready, 3)
                    pool.wait_ge(mk_copied, 8)
                    pool.wait_ge(tr_copied, 10)
                if b >= 2:
                    pool.wait_ge(pv_done, UNITS + 2 * (b - 2) + 2)
                for i, (dst, src) in enumerate(((kTs[:, s, :, PAST:L], kT[:, :, SEQ + b * DS:SEQ + (b + 1) * DS]),
                                                (ckTs[:, s, PAST:L], zT[:, TP, 2, new]),
                                                (krTs[64:96, s, PAST:L], zT[64:96, TP, 3, new]))):
                    nc.gpsimd.tensor_copy(dst, src).then_inc(new_keys, 1)
                    pool.wait_ge(new_keys, 3 * b + i + 1)

            def gather(dst, table, slot, e, done):
                nc.gpsimd.indirect_dma_start(
                    out=dst[:, slot, e, :], out_offset=None, in_=t_in[table],
                    in_offset=bass.IndirectOffsetOnAxis(ix[:, slot, e:e + 1], 0),
                    bounds_check=NK * NK - 1, oob_is_err=True).then_inc(done[slot], 16)

            pool.wait_ge(topk_done, 1)
            pool.wait_ge(g_stored, 16 * CHUNKS)
            pool.wait_ge(sel_used, NTD + CHUNK)
            with pool.Fori(0, TG) as t:
                with pool.Fori(0, GI) as j:
                    i = t * GI + j
                    for s in range(PER):
                        n = i * PER + s
                        pool.wait_ge(acc_done, n + 1)
                        pool.sem_inc(wait_carrier, 1)
                        nc.gpsimd.tensor_copy(ix[:, s], eidx[:, bass.ds(n * GROUP, GROUP)]).then_inc(ix_ready, 1)
                        pool.wait_ge(ix_ready, n + 1)
                        pool.sem_inc(wait_carrier, 1)
                        for e in range(GROUP):
                            gather(ubuf, "peer_u", s, e, u_loaded)
                        for e in range(GROUP):
                            gather(vbuf, "peer_v", s, e, v_loaded)

        @block.scalar
        def _(act):
            links = [0]
            A = nc.scalar.activation

            def link(ins):
                links[0] += 1
                ins.then_inc(act_chain, 1)
                act.wait_ge(act_chain, links[0])

            act.wait_ge(x_loaded, 16)
            for k in range(KD):
                A(sq[:, k], hT[:, k], ACT.Square).then_inc(squares, 1)
            act.wait_ge(meansq, 1)
            act.wait_ge(dve_chain, 1)
            A(rmsb[:, 0:SEQ], ps[:, 0, :], ACT.Sqrt, scale=1.0 / D, bias=eps_col[:, 0:1]).then_inc(rms_ready, 1)
            A(rmsb[:, SEQ:NT], ps[:, 1, 0:P], ACT.Sqrt, scale=1.0 / D, bias=eps_col[:, 0:1]).then_inc(rms_ready, 1)

            def copy_projection(n):
                act.wait_ge(proj_done, n + 1)
                bank = ps[:, 2 + n % 4]
                if n < 5:
                    A(zr[:, n], bank[:, 0:RW], ACT.Copy).then_inc(proj_copied, 1)
                elif n < 10:
                    A(fk[:, n - 5], bank, ACT.Copy).then_inc(proj_copied, 1)
                elif n < 15:
                    A(fv[:, n - 10], bank, ACT.Copy).then_inc(proj_copied, 1)
                else:
                    c, part = divmod(n - 15, 2)
                    dst = fqT[:, c, SEQ:NT] if part else fqT[:, c, 0:SEQ]
                    A(dst, bank[:, 0:P] if part else bank, ACT.Copy, scale=FOX_SCALE).then_inc(proj_copied, 1)

            for n_ in range(10):
                copy_projection(n_)
            act.wait_ge(ss_ready, 1)
            A(small[:, 10:15], small[:, 0:5], ACT.Sqrt, scale=1.0 / QL, bias=eps_col[:, 0:1])
            A(small[:, 15:20], small[:, 5:10], ACT.Sqrt, scale=1.0 / KVL, bias=eps_col[:, 0:1]).then_inc(rt_ready, 1)
            act.wait_ge(ff_abs, 1)
            link(A(krl[:, :, 8:16], krl[:, :, 24:32], ACT.Exp))
            A(krl[:, :, 16:24], krl[:, :, 8:16], ACT.Ln, bias=1.0).then_inc(ff_log, 1)
            for n_ in range(10, 23):
                copy_projection(n_)
            for u in range(10):
                act.wait_ge(tr_done, u + 1)
                bank = ps[:, 6 + u % 2].rearrange("p (c k) -> p c k", c=4)
                if u < 5:
                    A(zT[:, u], bank, ACT.Copy).then_inc(tr_copied, 1)
                else:
                    A(kT[:, :, (u - 5) * P:(u - 4) * P], bank, ACT.Copy).then_inc(tr_copied, 1)
            for h in range(MH):
                b = 3 * (h % 2)
                act.wait_ge(mq_done, h + 1)
                A(qmT[0:NOPE, h, 0:SEQ], ps[0:NOPE, b], ACT.Copy, scale=MLA_SCALE)
                A(qmT[0:NOPE, h, SEQ:NT], ps[0:NOPE, b + 2, 0:P], ACT.Copy, scale=MLA_SCALE).then_inc(mq_nope, 1)
            for u in range(12):
                act.wait_ge(mk_done, u + 1)
                bank = ps[:, u % 4]
                if u < 8:
                    A(kmT[0:NOPE, u], bank[0:NOPE], ACT.Copy).then_inc(mk_copied, 1)
                else:
                    A(vm[:, u - 8], bank, ACT.Copy).then_inc(mk_copied, 1)
            for g in range(2):
                act.wait_ge(qp_done, g + 1)
                if g == 0:
                    act.wait_ge(rows_ready, 1)
                A(qps[:, :, 4 * g:4 * g + 4, :].rearrange("p b h q -> p h b q"),
                  ps[:, 4 + g].rearrange("p (h b q) -> p h b q", h=4, b=DB), ACT.Copy).then_inc(qs_ready, 1)
            act.wait_ge(mq_rope, MH)
            A(qrs[64:96].rearrange("p b h q -> p h b q"),
              qmT[64:96, :, SEQ:NT].rearrange("p h (b q) -> p h b q", b=DB), ACT.Copy).then_inc(qs_ready, 1)

            def exponentials(n):
                nk = keys_of(n)
                act.wait_ge(max_ready, n + 1)
                if n >= 4:
                    act.wait_ge(pt_done, n - 3)
                A(prob[:, n % 4, 0:nk], ps[:, n % 3, 0:nk], ACT.Exp, bias=small[:, 32 + n % 4:33 + n % 4],
                  accum_out=small[:, 36 + n % 4:37 + n % 4]).then_inc(exp_done, 1)

            def copy_transposed(n):
                act.wait_ge(pt_done, n + 1)
                if n >= 3:
                    act.wait_ge(pv_done, n - 2)
                bank = ps[:, 3 + n % 2]
                if n < UNITS:
                    nk = keys_of(n)
                    A(probT[:, n % 3, 0:nk], bank[:, 0:nk], ACT.Copy).then_inc(pt_copied, 1)
                else:
                    A(probT[:, n % 3, 0:PAST], bank[:, 0:PAST], ACT.Copy)
                    A(probT[0:DS, n % 3, PAST:PAST + P], bank[0:DS, PAST:PAST + P], ACT.Copy).then_inc(pt_copied, 1)

            for n_ in range(ALL + 2):
                if n_ < ALL:
                    exponentials(n_)
                if n_ >= 2:
                    copy_transposed(n_ - 2)
            for t in range(T):
                act.wait_ge(ss2_ready, t + 1)
                A(small[:, 45 + t:46 + t], small[:, 40 + t:41 + t], ACT.Sqrt, scale=1.0 / D,
                  bias=eps_col[:, 0:1]).then_inc(rt2_ready, 1)
                for g in range(2):
                    act.wait_ge(h2t_done, 2 * t + g + 1)
                    A(h2T[:, 4 * g:4 * g + 4, t * P:(t + 1) * P],
                      ps[:, 4 + g].rearrange("p (c k) -> p c k", c=4), ACT.Copy).then_inc(h2t_copied, 1)

            def copy_queries(h):
                act.wait_ge(pq_done, h + 1)
                if h >= 2:
                    act.wait_ge(sc_done, h - 1)
                s = h % 2
                A(pq[:, s, :, 0:SEQ], ps[:, 0:2, :], ACT.Copy)
                link(A(pq[:, s, :, SEQ:NT], ps[:, 2, 0:2 * P].rearrange("p (c k) -> p c k", c=2), ACT.Copy))
                A(pq2[:, s], pq[:, s], ACT.Square).then_inc(pq_copied, 1)

            def copy_scores(h):
                act.wait_ge(sc_done, h + 1)
                if h >= 2:
                    act.wait_ge(sc_read, h - 1)
                s = h % 2
                flat = scb[:, s].rearrange("p t c k -> p (t c k)")
                A(flat[:, 0:1024], ps[:, 3:5, :].rearrange("p a b -> p (a b)"), ACT.Copy)
                A(flat[:, 1024:1280], ps[:, 5, 0:256], ACT.Copy)
                A(rt[:, s, 0:T], ps[:, 6, 0:T], ACT.Sqrt, scale=1.0 / (2 * P), bias=eps_col[:, 0:1]).then_inc(sc_copied, 1)

            act.wait_ge(h2t_copied, 2 * T)
            A(hh[:], h2T[:, :, 0:NTD], ACT.Copy).then_inc(hh_ready, 1)
            copy_queries(0)
            for h in range(PH):
                if h + 1 < PH:
                    copy_queries(h + 1)
                copy_scores(h)
            act.wait_ge(gap_ready, 1)
            A(gap[:], gap[:], ACT.Exp).then_inc(gap_exp, 1)
            for u, dst in enumerate((i1T, i2T, gT)):
                act.wait_ge(selT_done, u + 1)
                A(dst[:], ps[:, u, 0:NTD], ACT.Copy).then_inc(selT_copied, 1)
            act.wait_ge(selT_copied, 3)
            act.sem_inc(bank_free, CHUNK // 4)
            with act.Fori(0, CHUNKS) as c:
                act.wait_ge(stage_free, c + 1)
                act.sem_inc(wait_carrier, 1)
                for g in range(CHUNK // 4):
                    act.wait_ge(sel_used, c * CHUNK + 4 * g + 4 + CHUNK)
                    act.sem_inc(wait_carrier, 1)
                    A(stage[:, bass.ds(c % 2, 1), :, 4 * g:4 * g + 4].rearrange("p a k t -> p (a t) k"),
                      ps[:, g].rearrange("p (t k) -> p t k", t=4), ACT.Copy).then_inc(g_copied, 1)
                    act.wait_ge(g_copied, c * (CHUNK // 4) + g + 1)
                    act.sem_inc(bank_free, 1)

            act.wait_ge(ub_loaded[0], 16)
            act.wait_ge(dense_open, 5)
            A(uh[:, 0], ub[:, 0], ACT.Copy).then_inc(uh_ready, 1)
            with act.Fori(0, TG) as t:
                with act.Fori(0, GI) as j:
                    i = t * GI + j
                    for s in range(PER):
                        n, nxt = i * PER + s, (s + 1) % PER
                        act.wait_ge(vb_loaded[s], 16 * i + 16)
                        act.wait_ge(av_done, n + 3)
                        A(vh[:, s % 2], vb[:, s], ACT.Copy).then_inc(vh_ready, 1)
                        act.wait_ge(ub_loaded[nxt], 16 * i + (32 if nxt == 0 else 16))
                        act.wait_ge(a_done, n + 3)
                        A(uh[:, nxt % 2], ub[:, nxt], ACT.Copy).then_inc(uh_ready, 1)
                        act.wait_ge(dots_done, n + 1)
                        A(gelu[:, s], dots[:, s], ACT.Gelu).then_inc(gelu_done, 1)
                        act.wait_ge(a_done, n + 4)
                        A(ga[:, s % 2], ps[:, 6 + s % 2, 0:NTD], ACT.Gelu).then_inc(ga_ready, 1)
                        act.wait_ge(act_ready, n + 1)
                        A(acth[:, s % 2], actv[:, s % 2], ACT.Copy).then_inc(acth_ready, 1)
            for t in range(T):
                act.wait_ge(ss3_ready, t + 1)
                A(small[:, 45 + t:46 + t], small[:, 40 + t:41 + t], ACT.Sqrt, scale=1.0 / D,
                  bias=eps_col[:, 0:1]).then_inc(rt4_ready, 1)

        @block.tensor
        def _(pe):
            mm, tr = nc.tensor.matmul, nc.tensor.transpose
            identb, fmask, mmask, nmask = cb[:, 0:P], cb[:, P:2 * P], cb[:, 2 * P:3 * P], cb[:, 3 * P:3 * P + DS]
            pe.wait_ge(c_loaded, 16 * 11)
            for k in range(KD):
                pe.wait_ge(squares, k + 1)
                mm(ps[:, 0, :], ones[:], sq[:, k, 0:SEQ], start=(k == 0), stop=(k == KD - 1))
                last = mm(ps[:, 1, 0:P], ones[:], sq[:, k, SEQ:NT], start=(k == 0), stop=(k == KD - 1))
            last.then_inc(meansq, 1)
            for n in range(23):
                if n >= 4:
                    pe.wait_ge(proj_copied, n - 3)
                bank = ps[:, 2 + n % 4]
                if n in (0, 5, 10, 15):
                    pe.wait_ge({0: wr_loaded, 5: wk_loaded, 10: wv_loaded, 15: wq_loaded}[n], 16)
                for k in range(KD):
                    if n == 0:
                        pe.wait_ge(h_ready, k + 1)
                    on = dict(start=(k == 0), stop=(k == KD - 1))
                    if n < 15:
                        t, w = n % 5, (wr, wk, wv)[n // 5]
                        last = mm(bank[:, 0:w.shape[2]], hT[:, k, t * P:(t + 1) * P], w[:, k, :], **on)
                    else:
                        c, part = divmod(n - 15, 2)
                        last = mm(bank[:, 0:P] if part else bank, wq[:, k, c * P:(c + 1) * P],
                                  hT[:, k, SEQ:NT] if part else hT[:, k, 0:SEQ], **on)
                last.then_inc(proj_done, 1)
            for u in range(10):
                if u == 0:
                    pe.wait_ge(rows_ready, 1)
                if u >= 2:
                    pe.wait_ge(tr_copied, u - 1)
                t = u % 5
                src = [cqn[:, t, 0:P], cqn[:, t, P:2 * P], ckvn[:, t], krl[:, t]] if u < 5 else \
                      [fk[:, t, c * P:(c + 1) * P] for c in range(4)]
                for c in range(4):
                    last = tr(ps[:, 6 + u % 2, c * P:(c + 1) * P], src[c], ident[:])
                last.then_inc(tr_done, 1)
            pe.wait_ge(wu_loaded, 16 * 4)
            pe.wait_ge(tr_copied, 5)
            pe.wait_ge(proj_copied, 23)
            for h in range(MH):
                b = 3 * (h % 2)
                if h >= 2:
                    pe.wait_ge(mq_nope, h - 1)
                    pe.wait_ge(mq_rope, h - 1)
                for k in range(2):
                    on = dict(start=(k == 0), stop=(k == 1))
                    mm(ps[0:96, b, :], w_uq[:, k, h, 0:96], zT[:, 0:TP, k, :], **on)
                    mm(ps[64:96, b + 1, :], w_uq[:, k, h, 96:P], zT[:, 0:TP, k, :], **on)
                for k in range(2):
                    mm(ps[0:96, b + 2, 0:P], w_uq[:, k, h, 0:96], zT[:, TP, k, :], start=(k == 0), stop=(k == 1))
                for k in range(2):
                    last = mm(ps[64:96, b + 2, P:2 * P], w_uq[:, k, h, 96:P], zT[:, TP, k, :],
                              start=(k == 0), stop=(k == 1))
                last.then_inc(mq_done, 1)
            pe.wait_ge(mq_nope, MH)
            pe.wait_ge(mq_rope, MH)
            for u in range(12):
                if u >= 4:
                    pe.wait_ge(mk_copied, u - 3)
                if u < 8:
                    mm(ps[0:NOPE, u % 4], w_uk[:, u], zT[:, 0:TP, 2, :], start=True, stop=True).then_inc(mk_done, 1)
                else:
                    mm(ps[:, u % 4], zT[:, u - 8, 2, :], w_uv[:], start=True, stop=True).then_inc(mk_done, 1)
            for h in range(MH):
                last = mm(ps[:, 4 + h // 4, (h % 4) * P:(h % 4 + 1) * P], w_ukT[0:NOPE, h], qmT[0:NOPE, h, SEQ:NT],
                          start=True, stop=True)
                if h % 4 == 3:
                    last.then_inc(qp_done, 1)

            def scores(n):
                bank = ps[:, n % 3]
                if n >= 3:
                    pe.wait_ge(exp_done, n - 2)
                if n == 0:
                    pe.wait_ge(mk_copied, 12)
                    pe.wait_ge(nc_ready, 1)
                if n == 32:
                    pe.wait_ge(kr_copied, MH)
                if n < UNITS:
                    kind, c, hh, i, nk = unit(n)
                    h = 2 * c + hh
                    diag = bank[:, i * P:(i + 1) * P]
                    if kind == 0:
                        rows = slice(64 * hh, 64 * hh + 64)
                        mm(bank[:, 0:nk], fqT[rows, c, i * P:(i + 1) * P], kT[rows, c, 0:nk], start=True, stop=False)
                        mm(bank[:, 0:nk], selh[0:FH, h], ncT[0:FH, 0:nk], start=False, stop=False)
                        mm(diag, identb, fmask, start=False, stop=True).then_inc(s_done, 1)
                    else:
                        mm(bank[:, 0:nk], qmT[0:96, h, i * P:(i + 1) * P], kmT[0:96, h, 0:nk], start=True, stop=False)
                        mm(diag, identb, mmask, start=False, stop=True).then_inc(s_done, 1)
                    return
                b, kind = divmod(n - UNITS, 2)
                s = b % 2
                if kind == 0:
                    pe.wait_ge(batch_loaded[s], 16 * 7 * (b // 2 + 1))
                    pe.wait_ge(new_keys, 3 * (b + 1))
                    if b == 0:
                        pe.wait_ge(qbd_ready, 8)
                        pe.wait_ge(ncs_ready, 1)
                        pe.wait_ge(qs_ready, 3)
                    for c in range(4):
                        mm(bank[:, 0:L], qbd[:, c, b].rearrange("p h q -> p (h q)"), kTs[:, s, c], start=(c == 0), stop=False)
                    mm(bank[:, 0:L], selb[0:64, b], ncS[0:64], start=False, stop=False)
                    mm(bank[:, PAST:L], identb, nmask, start=False, stop=True).then_inc(s_done, 1)
                else:
                    mm(bank[:, 0:L], qps[:, b].rearrange("p h q -> p (h q)"), ckTs[:, s], start=True, stop=False)
                    mm(bank[:, 0:L], qrs[64:96, b].rearrange("p h q -> p (h q)"), krTs[64:96, s],
                       start=False, stop=True).then_inc(s_done, 1)

            def transpose_probabilities(n):
                pe.wait_ge(p_ready, n + 1)
                if n >= 2:
                    pe.wait_ge(pt_copied, n - 1)
                nk = keys_of(n)
                for c in range((nk + P - 1) // P):
                    w = min(P, nk - c * P)
                    last = tr(ps[0:w, 3 + n % 2, c * P:(c + 1) * P], prob[:, n % 4, c * P:c * P + w], ident[:])
                last.then_inc(pt_done, 1)

            def values(n):
                pe.wait_ge(pt_copied, n + 1)
                pT = probT[:, n % 3]
                if n < UNITS:
                    kind, c, hh, i, nk = unit(n)
                    pair = n // 8
                    if n % 8 == 0 and pair >= 2:
                        pe.wait_ge(o_copied, pair - 1)
                    rows = slice(64 * hh, 64 * hh + 64)
                    for k in range(i + 1):
                        v = (fv, vm)[kind][:, k, (2 * c + hh) * 64:(2 * c + hh + 1) * 64]
                        last = mm(ps[rows, 5 + pair % 2, i * P:(i + 1) * P], v, pT[:, k * P:(k + 1) * P],
                                  start=(k == 0), stop=(k == i))
                    last.then_inc(pv_done, 1)
                    return
                m = n - UNITS
                b, kind = divmod(m, 2)
                s = b % 2
                pe.wait_ge(o_copied, 8 + m - 1)
                bank = ps[:, 5 + m % 2]
                for c in range(4 if kind == 0 else 1):
                    for k in range(3):
                        rows = slice(0, P if k < 2 else DS)
                        on = dict(start=(k == 0), stop=(k == 2))
                        if kind == 0:
                            v = vs[:, s, k, c * P:(c + 1) * P] if k < 2 else vn[0:DS, s, c * P:(c + 1) * P]
                            last = mm(bank[:, 32 * c:32 * c + 32], v, pT[rows, k * P + 32 * c:k * P + 32 * c + 32], **on)
                        else:
                            v = ckr[:, s, k] if k < 2 else ckn[0:DS, s]
                            last = mm(bank[:, 0:P], v, pT[rows, k * P:(k + 1) * P], **on)
                last.then_inc(pv_done, 1)

            for n in range(ALL + 3):
                if n >= UNITS + 3:
                    values(n - 3)
                if n < ALL:
                    scores(n)
                if 2 <= n < ALL + 2:
                    transpose_probabilities(n - 2)
                if 3 <= n < UNITS + 3:
                    values(n - 3)
            pe.wait_ge(o_copied, 8 + 2 * DB)
            for h in range(MH):
                last = mm(ps[64 * (h % 2):64 * (h % 2) + 64, 7, (h // 2) * P:(h // 2 + 1) * P],
                          w_uv[:, h * VD:(h + 1) * VD], latT[:, h], start=True, stop=True)
            last.then_inc(up_done, 1)

            def project_out(t):
                if t == 0:
                    pe.wait_ge(wo_loaded, 16)
                    pe.wait_ge(o_copied, 8 + 2 * DB + 1)
                if t >= 2:
                    pe.wait_ge(x2_ready, t - 1)
                for j in range(2):
                    for c in range(8):
                        last = mm(ps[:, 2 * (t % 2) + j], oT[:, c, t * P:(t + 1) * P], w_o[:, c, j * 512:(j + 1) * 512],
                                  start=(c == 0), stop=(c == 7))
                last.then_inc(out_done, 1)

            def transpose_h2(t):
                pe.wait_ge(h2_ready, t + 1)
                for g in range(2):
                    if t >= 1:
                        pe.wait_ge(h2t_copied, 2 * (t - 1) + g + 1)
                    for c in range(4):
                        k = 4 * g + c
                        last = tr(ps[:, 4 + g, c * P:(c + 1) * P], h2[:, t, k * P:(k + 1) * P], ident[:])
                    last.then_inc(h2t_done, 1)

            project_out(0)
            for t in range(T):
                if t + 1 < T:
                    project_out(t + 1)
                transpose_h2(t)

            def queries(h):
                pe.wait_ge(wpq_loaded[h % 2], 16 * (h // 2 + 1))
                if h == 0:
                    pe.wait_ge(h2t_copied, 2 * T)
                    pe.wait_ge(x2_ready, T)
                else:
                    pe.wait_ge(pq_copied, h)
                for k in range(KD):
                    for c in range(2):
                        mm(ps[:, c], wpq[:, h % 2, k, c * P:(c + 1) * P], h2T[:, k, 0:SEQ], start=(k == 0), stop=(k == KD - 1))
                for c in range(2):
                    for k in range(KD):
                        last = mm(ps[:, 2, c * P:(c + 1) * P], wpq[:, h % 2, k, c * P:(c + 1) * P], h2T[:, k, SEQ:NT],
                                  start=(k == 0), stop=(k == KD - 1))
                last.then_inc(pq_done, 1)

            def key_scores(h):
                pe.wait_ge(pq_copied, h + 1)
                if h == 0:
                    pe.wait_ge(late_loaded, 16 * 5)
                else:
                    pe.wait_ge(sc_copied, h)
                for t in range(T):
                    for c in range(2):
                        mm(ps[:, 3 + t // 2, 256 * (t % 2) + c * P:256 * (t % 2) + (c + 1) * P],
                           pq[:, h % 2, c, t * P:(t + 1) * P], keysT[:, 2 * h + c], start=True, stop=True)
                for t in range(T):
                    for c in range(2):
                        last = mm(ps[:, 6, t:t + 1], pq2[:, h % 2, c, t * P:(t + 1) * P], ones[:, 0:1],
                                  start=(c == 0), stop=(c == 1))
                last.then_inc(sc_done, 1)

            queries(0)
            for h in range(PH):
                if h + 1 < PH:
                    queries(h + 1)
                key_scores(h)
            pe.wait_ge(sc_copied, PH)
            pe.wait_ge(topk_done, 1)
            for u, src in enumerate((e1, e2, gate)):
                for t in range(TD):
                    last = tr(ps[:, u, t * P:(t + 1) * P], src[:, t], ident[:])
                last.then_inc(selT_done, 1)
            pe.wait_ge(selT_copied, 3)
            pe.sem_inc(sel_used, CHUNK)
            with pe.Fori(0, CHUNKS) as c:
                for q in range(2):
                    pe.wait_ge(sel_ready, 2 * c + q + 1)
                    for g in range(4):
                        pe.wait_ge(bank_free, c * (CHUNK // 4) + 4 * q + g + 1)
                        for k in range(4):
                            tok = 4 * g + k
                            last = mm(ps[:, 4 * q + g, k * P:(k + 1) * P], bsel[:, q, tok], asel[:, q, tok],
                                      start=True, stop=True)
                            last.then_inc(sel_used, 1)
            pe.wait_ge(g_copied, CHUNKS * CHUNK // 4)
            pe.wait_ge(dense_open, 5)
            pe.wait_ge(hl_ready, 1)
            for b in range(2 * TD):
                mm(ps[:, b], zero[:, 0:P], zero[:], start=True, stop=False, skip_group_check=True)

            def values_block(s):
                for d in range(TD):
                    for a, v in ((acth[:, s % 2], vh[:, s % 2]), (acth[:, s % 2], vl[:, s]), (actl[:, s % 2], vh[:, s % 2])):
                        for half in range(2):
                            last = mm(ps[:, 2 * d + half], a[:, d * P:(d + 1) * P], v[:, half * 512:(half + 1) * 512],
                                      start=False, stop=False, skip_group_check=True)
                last.then_inc(av_done, 1)

            pe.sem_inc(a_done, 3)
            pe.sem_inc(av_done, 3)
            with pe.Fori(0, TG) as t:
                with pe.Fori(0, GI) as j:
                    i = t * GI + j
                    for s in range(PER):
                        n, slot = i * PER + s, s % 2
                        pe.wait_ge(ul_ready, n + 1)
                        pe.wait_ge(ga_ready, n + 1)
                        for k in range(KD):
                            mm(ps[:, 6 + slot, 0:NTD], uh[:, slot, k], hh[:, k], start=(k == 0), stop=False)
                            mm(ps[:, 6 + slot, 0:NTD], uh[:, slot, k], hl[:, k], start=False, stop=False)
                            last = mm(ps[:, 6 + slot, 0:NTD], ul[:, s, k], hh[:, k], start=False, stop=(k == KD - 1))
                        last.then_inc(a_done, 1)
                        pe.wait_ge(actl_ready, n + 1)
                        pe.wait_ge(vl_ready, n + 1)
                        values_block((s - 1) % PER)
            pe.wait_ge(actl_ready, BLOCKS + 1)
            pe.wait_ge(vl_ready, BLOCKS + 1)
            values_block(PER - 1)
            for b in range(2 * TD):
                last = mm(ps[:, b], zero[:, 0:P], zero[:], start=False, stop=True, skip_group_check=True)
            last.then_inc(dense_done, 1)

        @block.vector
        def _(dve):
            V = nc.vector
            links = [0]

            def link(ins):
                links[0] += 1
                ins.then_inc(dve_chain, 1)
                dve.wait_ge(dve_chain, links[0])

            V.memset(krl[:], 0.0)
            link(V.memset(eps_col[:], EPS))
            dve.wait_ge(c_loaded, 16 * 11)
            dve.wait_ge(rms_ready, 2)
            link(V.reciprocal(rstdb[:], rmsb[:]))
            for k in range(KD):
                V.scalar_tensor_tensor(out=hT[:, k], in0=hT[:, k], scalar=gm[:, k:k + 1], in1=rstdb[:],
                                       op0=ALU.mult, op1=ALU.mult).then_inc(h_ready, 1)
            dve.wait_ge(proj_copied, 5)
            for t in range(T):
                for q, (off, width) in enumerate(((R_CQ, QL), (R_CKV, KVL))):
                    a = zr[:, t, off:off + width]
                    ins = V.tensor_tensor_reduce(out=(cqn, ckvn)[q][:, t], in0=a, in1=a, scale=1.0, scalar=0.0, op0=ALU.mult,
                                                 op1=ALU.add, accum_out=small[:, 5 * q + t:5 * q + t + 1])
            ins.then_inc(ss_ready, 1)
            x_ff = krl[:, :, 32:40]
            link(V.tensor_tensor(x_ff, zr[:, :, R_FF:R_FF + FH], bfb[:], ALU.add))
            V.scalar_tensor_tensor(out=krl[:, :, 24:32], in0=x_ff, scalar=-1.0, in1=x_ff, op0=ALU.mult,
                                   op1=ALU.min).then_inc(ff_abs, 1)
            cos, sin = c_rrow[:, 0], c_rrow[:, 1]
            k1_, k2_ = zr[:, :, R_KR:R_KR + 16], zr[:, :, R_KR + 16:RW]
            V.tensor_tensor(krl[:, :, 64:80], k1_, cos, ALU.mult)
            V.tensor_tensor(krl[:, :, 80:96], k1_, sin, ALU.mult)
            V.tensor_tensor(krl[:, :, 96:112], k2_, sin, ALU.mult)
            link(V.tensor_tensor(krl[:, :, 112:128], k2_, cos, ALU.mult))
            V.tensor_tensor(krl[:, :, 64:80], krl[:, :, 64:80], krl[:, :, 96:112], ALU.subtract)
            V.tensor_tensor(krl[:, :, 80:96], krl[:, :, 80:96], krl[:, :, 112:128], ALU.add)
            dve.wait_ge(rt_ready, 1)
            link(V.reciprocal(small[:, 20:30], small[:, 10:20]))
            for t in range(T):
                V.scalar_tensor_tensor(out=cqn[:, t], in0=zr[:, t, R_CQ:R_CKV], scalar=small[:, 20 + t:21 + t], in1=gq[:],
                                       op0=ALU.mult, op1=ALU.mult)
                V.scalar_tensor_tensor(out=ckvn[:, t], in0=zr[:, t, R_CKV:R_KR], scalar=small[:, 25 + t:26 + t], in1=gkv[:],
                                       op0=ALU.mult, op1=ALU.mult)
            dve.wait_ge(ff_log, 1)
            V.scalar_tensor_tensor(out=krl[:, :, 0:FH], in0=x_ff, scalar=0.0, in1=krl[:, :, 16:24],
                                   op0=ALU.min, op1=ALU.subtract).then_inc(rows_ready, 1)
            dve.wait_ge(tr_copied, 5)
            dve.wait_ge(proj_done, 23)
            lf = prob[0:FH, 0, :]
            link(V.tensor_scalar(lf.rearrange("p (t k) -> p t k", t=TP), zT[0:FH, 0:TP, 3, :], -1.0, None, ALU.mult))
            link(V.memset(prob[0:64, 1, :], 1.0))
            V.tensor_tensor_scan(ncT[0:FH], prob[0:FH, 1, :], lf, 0.0, ALU.mult, ALU.add).then_inc(nc_ready, 1)
            rr = slice(64, 96)
            for h in range(MH):
                b = 3 * (h % 2)
                dve.wait_ge(mq_done, h + 1)
                t1, t2 = prob[rr, 2], prob[rr, 3]
                V.tensor_tensor(t1, ps[rr, b], c_rope[rr, 0, 0:SEQ], ALU.mult)
                V.tensor_tensor(t2, ps[rr, b + 1], c_rope[rr, 1, 0:SEQ], ALU.mult)
                V.tensor_tensor(probT[rr, 0, 0:P], ps[rr, b + 2, 0:P], c_rope[rr, 0, SEQ:NT], ALU.mult)
                link(V.tensor_tensor(probT[rr, 1, 0:P], ps[rr, b + 2, P:2 * P], c_rope[rr, 1, SEQ:NT], ALU.mult))
                V.tensor_tensor(qmT[rr, h, 0:SEQ], t1, t2, ALU.add)
                V.tensor_tensor(qmT[rr, h, SEQ:NT], probT[rr, 0, 0:P], probT[rr, 1, 0:P], ALU.add).then_inc(mq_rope, 1)
                dve.wait_ge(mq_rope, h + 1)
            dve.wait_ge(lfs_loaded, 16 * (1 + DB))
            link(V.tensor_scalar(lfs[0:64], lfs[0:64], -1.0, None, ALU.mult))
            V.tensor_tensor_scan(ncS[0:64], prob[0:64, 1, 0:L], lfs[0:64], 0.0, ALU.mult, ALU.add).then_inc(ncs_ready, 1)
            dve.wait_ge(ncs_ready, 1)

            def row_max(n):
                dve.wait_ge(s_done, n + 1)
                V.tensor_reduce(small[:, 32 + n % 4:33 + n % 4], ps[:, n % 3, 0:keys_of(n)], AX.X, ALU.max,
                                negate=True).then_inc(max_ready, 1)

            def normalise(n):
                dve.wait_ge(exp_done, n + 1)
                q = small[:, 36 + n % 4:37 + n % 4]
                link(V.reciprocal(q, q))
                pr = prob[:, n % 4, 0:keys_of(n)]
                V.tensor_scalar(pr, pr, q, None, ALU.mult).then_inc(p_ready, 1)

            def copy_out(n):
                dve.wait_ge(pv_done, n + 1)
                if n < UNITS:
                    V.tensor_copy(oT[:, n // 8, 0:SEQ], ps[:, 5 + n // 8 % 2]).then_inc(o_copied, 1)
                    return
                m = n - UNITS
                b, kind = divmod(m, 2)
                bank = ps[:, 5 + m % 2, 0:P]
                new = slice(SEQ + b * DS, SEQ + (b + 1) * DS)
                if kind == 0:
                    for hh in range(2):
                        rows = slice(64 * hh, 64 * hh + 64)
                        ins = V.tensor_copy(oT[rows, 0:4, new],
                                            bank[rows].rearrange("p (c x) -> p c x", c=4)[:, :, DS * hh:DS * hh + DS])
                    ins.then_inc(o_copied, 1)
                else:
                    if b == 0:
                        dve.wait_ge(wo_loaded, 16)
                    V.tensor_copy(latT[:, :, b * DS:(b + 1) * DS], bank.rearrange("p (h q) -> p h q", h=MH)).then_inc(o_copied, 1)

            for n_ in range(ALL + 4):
                if n_ < ALL:
                    row_max(n_)
                if 1 <= n_ <= ALL:
                    normalise(n_ - 1)
                if n_ >= 4 and (n_ - 4 >= UNITS or (n_ - 4) % 8 == 7):
                    copy_out(n_ - 4)
            dve.wait_ge(up_done, 1)
            V.tensor_copy(oT[:, 4:8, SEQ:NT], ps[:, 7].rearrange("p (c k) -> p c k", c=4)).then_inc(o_copied, 1)
            dve.wait_ge(late_loaded, 64)
            for t in range(T):
                dve.wait_ge(out_done, t + 1)
                V.tensor_tensor(x2[:, t], x2[:, t], ps[:, 2 * (t % 2):2 * (t % 2) + 2].rearrange("p a b -> p (a b)"),
                                ALU.add).then_inc(x2_ready, 1)
                dve.wait_ge(x2_ready, t + 1)
                V.tensor_tensor_reduce(out=h2[:, t], in0=x2[:, t], in1=x2[:, t], scale=1.0, scalar=0.0, op0=ALU.mult,
                                       op1=ALU.add, accum_out=small[:, 40 + t:41 + t]).then_inc(ss2_ready, 1)
                dve.wait_ge(rt2_ready, t + 1)
                link(V.reciprocal(small[:, 45 + t:46 + t], small[:, 45 + t:46 + t]))
                V.scalar_tensor_tensor(out=h2[:, t], in0=x2[:, t], scalar=small[:, 45 + t:46 + t], in1=gffn[:],
                                       op0=ALU.mult, op1=ALU.mult).then_inc(h2_ready, 1)
            dve.wait_ge(hh_ready, 1)
            V.tensor_tensor(hl[:], h2T[:, :, 0:NTD], hh[:].bitcast(F32), ALU.subtract).then_inc(hl_ready, 1)
            dve.wait_ge(late_loaded, 16 * 5)
            LINKS = 14
            with dve.Fori(0, PH // 2) as pair:
                for s in range(2):
                    h = pair * 2 + s
                    q = [0]

                    def step(ins):
                        q[0] += 1
                        ins.then_inc(dve_loop, 1)
                        dve.wait_ge(dve_loop, h * LINKS + q[0])
                        dve.sem_inc(wait_carrier, 1)

                    def top16(src, rest, val, idx):
                        for a, v in zip(src, val):
                            ins = V.max(v[:, 0:8], a)
                        step(ins)
                        for a, r_, v, i_ in zip(src, rest, val, idx):
                            V.max_index(i_[:, 0:8], v[:, 0:8], a)
                            ins = V.match_replace(r_, v[:, 0:8], a, NEG)
                        step(ins)
                        for r_, v in zip(rest, val):
                            ins = V.max(v[:, 8:16], r_)
                        step(ins)
                        for r_, v, i_ in zip(rest, val, idx):
                            ins = V.max_index(i_[:, 8:16], v[:, 8:16], r_)
                        step(ins)

                    dve.wait_ge(sc_copied, h + 1)
                    dve.sem_inc(wait_carrier, 1)
                    both = [(t, c) for t in range(T) for c in range(2)]
                    V.reciprocal(rs[:, 0:T], rt[:, s, 0:T])
                    top16([scb[:, s, t, c] for t, c in both], [sr[:, t, c] for t, c in both],
                          [v16[:, t, c] for t, c in both], [i16[:, t, c] for t, c in both])
                    step(V.tensor_tensor(v16[:].rearrange("p t c k -> p t (c k)"), v16[:].rearrange("p t c k -> p t (c k)"),
                                         rs[:, 0:T].unsqueeze(2).broadcast_to([P, T, 2 * TK]), ALU.mult))
                    step(V.tensor_tensor(cand[:], v16[:, :, 0, :].unsqueeze(3).broadcast_to([P, T, TK, TK]),
                                         v16[:, :, 1, :].unsqueeze(2).broadcast_to([P, T, TK, TK]), ALU.add))
                    flat = lambda x, t: x[:, t].rearrange("p a b -> p (a b)")
                    top16([flat(cand, t) for t in range(T)], [flat(candr, t) for t in range(T)],
                          [cv[:, t] for t in range(T)], [ci[:, t] for t in range(T)])
                    heads = lambda x: x[:, :, bass.ds(h * TK, TK)]
                    V.tensor_scalar(hi[:], ci[:], 4, None, ALU.logical_shift_right)
                    V.tensor_scalar(lo[:], ci[:], TK - 1, None, ALU.bitwise_and)
                    step(V.tensor_tensor(heads(gap), cv[:], cv[:, :, 0:1].broadcast_to([P, T, TK]), ALU.subtract))
                    for pos, oh in ((hi, onehot), (lo, onehot2)):
                        ins = V.tensor_tensor(oh[:], pos[:].unsqueeze(3).broadcast_to([P, T, TK, TK]),
                                              iota[:, 0:TK].unsqueeze(1).unsqueeze(1).broadcast_to([P, T, TK, TK]), ALU.is_equal)
                    step(ins)
                    for c, oh in ((0, onehot), (1, onehot2)):
                        ins = V.tensor_tensor(oh[:], oh[:], i16[:, :, c, :].unsqueeze(2).broadcast_to([P, T, TK, TK]), ALU.mult)
                    step(ins)
                    V.tensor_reduce(heads(e1), onehot[:], AX.X, ALU.add)
                    ins = V.tensor_reduce(heads(e2), onehot2[:], AX.X, ALU.add)
                    step(ins)
                    assert q[0] == LINKS - 0, q[0]
                    ins = V.memset(rs[:, 6:8], 0.0)
                    ins.then_inc(sc_read, 1)
                    dve.wait_ge(sc_read, h + 1)
                    dve.sem_inc(wait_carrier, 1)
            V.memset(rs[:, 5:6], 0.0).then_inc(gap_ready, 1)
            V.scalar_tensor_tensor(out=eidx[:, 0:TG * SEL].rearrange("p (t k) -> p t k", t=TG), in0=e1[:, TD:T], scalar=float(NK),
                                   in1=e2[:, TD:T], op0=ALU.mult, op1=ALU.add)
            dve.wait_ge(gap_exp, 1)
            per_head = gap[:].rearrange("p t (h k) -> p (t h) k", h=PH)
            link(V.tensor_reduce(gsum[:, 0], per_head, AX.X, ALU.add))
            link(V.reciprocal(gsum[:, 1], gsum[:, 0]))
            V.tensor_tensor(gate[:].rearrange("p t (h k) -> p (t h) k", h=PH), per_head,
                            gsum[:, 1].unsqueeze(2).broadcast_to([P, T * PH, TK]), ALU.mult).then_inc(topk_done, 1)
            dve.wait_ge(selT_copied, 3)
            half_chunk = [P, CHUNK // 2, NK]
            keys = iota[:].unsqueeze(1).broadcast_to(half_chunk)
            with dve.Fori(0, CHUNKS) as c:
                for q in range(2):
                    cols = lambda x: x[:, bass.ds(c * CHUNK + q * (CHUNK // 2), CHUNK // 2)].unsqueeze(2).broadcast_to(half_chunk)
                    dve.wait_ge(sel_used, c * CHUNK + q * (CHUNK // 2) + CHUNK // 2)
                    V.tensor_tensor(asel[:, q], keys, cols(i1T), ALU.is_equal).then_inc(dve_loop2, 1)
                    V.tensor_tensor(bsel[:, q], keys, cols(i2T), ALU.is_equal)
                    dve.wait_ge(dve_loop2, 2 * c + q + 1)
                    V.tensor_tensor(asel[:, q], asel[:, q], cols(gT), ALU.mult).then_inc(sel_ready, 1)
            dve.wait_ge(sel_used, NTD + CHUNK)
            dve.wait_ge(g_stored, 16 * CHUNKS)
            for zeros in (zero[:], acth[:, 1], actl[:, 1], vh[:, 1], vl[:, PER - 1]):
                V.memset(zeros.bitcast(F32), 0.0).then_inc(dense_open, 1)
            dve.wait_ge(dense_open, 5)
            for first, count in ((actl_ready, 1), (vl_ready, 1), (g_used, 2), (ga_ready, 2), (acc_done, PER)):
                dve.sem_inc(first, count)

            def low_part(low, full, high, high_ready, count, done):
                dve.wait_ge(high_ready, count)
                V.tensor_tensor(low, full, high.bitcast(F32), ALU.subtract).then_inc(done, 1)

            low_part(ul[:, 0], ub[:, 0], uh[:, 0], uh_ready, 1, ul_ready)
            XL = PER * GROUP
            with dve.Fori(0, TG) as t:
                row = lambda x: x[:, bass.ds(t + TD, 1), :].rearrange("p a k -> p (a k)")
                with dve.Fori(0, GI) as j:
                    i = t * GI + j
                    q = [0]

                    def chained(ins):
                        q[0] += 1
                        ins.then_inc(y_link, 1)
                        dve.wait_ge(y_link, i * XL + q[0])

                    for s in range(PER):
                        n, slot, nxt = i * PER + s, s % 2, (s + 1) % PER
                        dve.wait_ge(u_loaded[s], 16 * GROUP * i + 16 * GROUP)
                        for e in range(GROUP):
                            ins = V.scalar_tensor_tensor(out=ubuf[:, s, e], in0=ubuf[:, s, e], scalar=1.0, in1=row(h2),
                                                         op0=ALU.mult, op1=ALU.mult, accum_out=dots[:, s, e:e + 1])
                        ins.then_inc(dots_done, 1)
                        low_part(vl[:, s], vb[:, s], vh[:, slot], vh_ready, n + 1, vl_ready)
                        low_part(ul[:, nxt], ub[:, nxt], uh[:, nxt % 2], uh_ready, n + 2, ul_ready)
                        if s == 0:
                            dve.wait_ge(gb_loaded, 64 * i + 64)
                        dve.wait_ge(ga_ready, n + 3)
                        V.tensor_tensor(actv[:, slot].rearrange("p (c t) -> p c t", c=CHUNKS),
                                        ga[:, slot].rearrange("p (c t) -> p c t", c=CHUNKS),
                                        gbuf[:, bass.ds(i % 2, 1), :, s, :].rearrange("p a c t -> p (a c) t"), ALU.mult).then_inc(act_ready, 1)
                        dve.wait_ge(gelu_done, n + 1)
                        chained(V.tensor_tensor(wts[:, s], gelu[:, s],
                                                gate[:].rearrange("p t k -> p (t k)")[:, bass.ds(TD * SEL + n * GROUP, GROUP)],
                                                ALU.mult))
                        low_part(actl[:, slot], actv[:, slot], acth[:, slot], acth_ready, n + 1, actl_ready)
                        if s == PER - 1:
                            dve.wait_ge(actl_ready, n + 2)
                            dve.sem_inc(g_used, 1)
                        dve.wait_ge(v_loaded[s], 16 * GROUP * i + 16 * GROUP)
                        for e in range(GROUP):
                            ins = V.scalar_tensor_tensor(out=row(x2), in0=vbuf[:, s, e], scalar=wts[:, s, e:e + 1],
                                                         in1=row(x2), op0=ALU.mult, op1=ALU.add)
                            if e < GROUP - 1:
                                chained(ins)
                        ins.then_inc(acc_done, 1)
                        dve.wait_ge(acc_done, n + 1 + PER)
                    assert q[0] == XL
            for t in range(T):
                if t == 0:
                    dve.wait_ge(dense_done, 1)
                if t < TD:
                    link(V.tensor_tensor(x2[:, t], x2[:, t], ps[:, 2 * t:2 * t + 2].rearrange("p a b -> p (a b)"), ALU.add))
                V.scalar_tensor_tensor(out=yout[:, t], in0=x2[:, t], scalar=1.0, in1=x2[:, t], op0=ALU.mult, op1=ALU.mult,
                                       accum_out=small[:, 40 + t:41 + t]).then_inc(ss3_ready, 1)
            for t in range(T):
                dve.wait_ge(rt4_ready, t + 1)
                link(V.reciprocal(small[:, 50 + t:51 + t], small[:, 45 + t:46 + t]))
                V.scalar_tensor_tensor(out=yout[:, t], in0=x2[:, t], scalar=small[:, 50 + t:51 + t], in1=gfin[:],
                                       op0=ALU.mult, op1=ALU.mult).then_inc(y_ready, 1)


def _rope_tables():
    half = ROPE // 2
    inv = (np.float32(10000.0) ** (-np.arange(half, dtype=np.float32) / np.float32(half))).astype(np.float32)
    pos = np.concatenate([np.arange(SEQ), np.tile(PAST + np.arange(DS), DB)]).astype(np.float32)
    ang = pos[:, None] * inv[None, :]
    return np.cos(ang).astype(np.float32), np.sin(ang).astype(np.float32)


def _constants():

    cos, sin = _rope_tables()
    j = np.arange(P) % 32
    sign = np.where(j < 16, -1.0, 1.0).astype(np.float32)[:, None]
    c_rope = np.stack([cos.T[j % 16], sin.T[j % 16] * sign], 1) * np.float32(MLA_SCALE)
    c_rrow = np.stack([cos, sin]).reshape(2, T, P, 16).transpose(2, 0, 1, 3)
    selh = np.zeros((FH, FH, P), np.float32)
    selh[np.arange(FH), np.arange(FH)] = 1
    selb = np.zeros((DB, FH, DB, FH, DS), np.float32)
    for b in range(DB):
        for h in range(FH):
            selb[b, h, b, h] = 1
    q, k = np.arange(P)[:, None], np.arange(P)[None]
    fmask = np.where(k <= q, 0, NEG)
    mmask = np.where(k // 64 <= q // 64, 0, NEG)
    nmask = np.where(np.arange(DS)[None] <= q % DS, 0, NEG)
    cb = np.concatenate([np.eye(P), fmask, mmask, nmask], 1).astype(mybir.dt.np(BF16))
    return {"ident": np.eye(P, dtype=np.float32), "ones": np.ones((P, P), np.float32), "c_rope": c_rope.astype(np.float32),
            "c_rrow": c_rrow, "iota": np.broadcast_to(np.arange(NK, dtype=np.float32), (P, NK)), "selh": selh, "selb": selb.reshape(DB * FH, DB, P), "cb": cb}


def _arrays(i):
    f = lambda x: np.asarray(x)
    fold = lambda w: w.reshape(KD, P, -1).transpose(1, 0, 2)
    x = np.concatenate([f(i["x_prompt"]).reshape(SEQ, D), f(i["x_sample"]).reshape(DB * DS, D)])
    w_in = f(i["w_in"])[0]
    fw = FH * HD
    w_ukv = f(i["w_ukv"])[0].reshape(KVL, MH, NOPE + VD)
    w_uq = f(i["w_uq"])[0].reshape(2, P, MH, NOPE + ROPE).transpose(1, 0, 2, 3)
    r1, r2 = w_uq[..., NOPE:NOPE + 16], w_uq[..., NOPE + 16:]
    ck = f(i["cache_fox_k"])[0].reshape(DB, PAST, 4, P)
    keys = f(i["peer_sub_keys"])[0]
    tile = lambda v: np.broadcast_to(v, (P,) + v.shape)
    return {
        **_constants(),
        "xT": fold(x.T), "xr": x,
        "gm": f(i["g_mix"])[0].reshape(KD, P).T,
        "wr": fold(w_in[:, 3 * fw:]), "wk": fold(w_in[:, fw:2 * fw]), "wv": fold(w_in[:, 2 * fw:3 * fw]), "wq": fold(w_in[:, :fw]),
        "bfb": tile(np.broadcast_to(f(i["b_f"])[0], (T, FH))),
        "gq": tile(f(i["g_q"])[0]), "gkv": tile(f(i["g_kv"])[0]),
        "w_uq": np.concatenate([w_uq, r2, r1], -1),
        "w_uk": w_ukv[..., :NOPE], "w_uv": w_ukv[..., NOPE:].reshape(KVL, MH * VD),
        "w_ukT": w_ukv[..., :NOPE].transpose(2, 1, 0),
        "past_k": ck.transpose(0, 3, 2, 1), "past_v": f(i["cache_fox_v"])[0].reshape(DB, PAST, fw),
        "past_logf": f(i["cache_fox_logf"])[0].transpose(0, 2, 1).reshape(DB * FH, PAST),
        "past_ckv": f(i["cache_mla_ckv"])[0], "past_ckvT": f(i["cache_mla_ckv"])[0].transpose(0, 2, 1),
        "past_krT": f(i["cache_mla_krope"])[0].transpose(0, 2, 1),
        "w_o": f(i["w_o"])[0].reshape(8, P, D).transpose(1, 0, 2),
        "gffn": tile(f(i["g_ffn"])[0]), "gfin": tile(f(i["g_final"])),
        "wpq": f(i["w_pq"])[0].reshape(KD, P, PH, 2 * P).transpose(2, 1, 0, 3),
        "keysT": keys.transpose(3, 1, 0, 2).reshape(P, 2 * PH, NK),
        "peer_uT": f(i["peer_u"])[0].reshape(BLOCKS, P, KD, P).transpose(0, 3, 2, 1).reshape(BLOCKS, P, D),
        "peer_u": f(i["peer_u"])[0], "peer_v": f(i["peer_v"])[0],
    }


_OUTS = {"y": (NT, D), "fk": (NT, FH * HD), "fv": (NT, FH * HD), "logf": (NT, FH), "ckv": (NT, KVL), "krope": (NT, ROPE)}


def kernel(**inputs):
    import concourse.bacc as _bacc
    from concourse.bass_utils import run_bass_kernel_spmd as _run

    nc = _bacc.Bacc("TRN2", target_bir_lowering=False, num_devices=1)
    arrays, t_in, t_out = {}, {}, {}
    for name, a in _arrays(inputs).items():
        a = np.ascontiguousarray(a)
        arrays[f"in_{name}"] = a
        t_in[name] = nc.dram_tensor(f"in_{name}", a.shape, mybir.dt.from_np(a.dtype), kind="ExternalInput").ap()
    for name, shape in _OUTS.items():
        t_out[name] = nc.dram_tensor(f"out_{name}", shape, F32, kind="ExternalOutput").ap()
    peer_step_kernel(nc, t_in, t_out)
    r = _run(nc, [arrays], core_ids=[0]).results[0]
    o = {name: r[f"out_{name}"] for name in _OUTS}
    p = lambda name, *s: o[name][:SEQ].reshape(1, 1, SEQ, *s)
    d = lambda name, *s: o[name][SEQ:].reshape(1, DB, DS, *s)
    return (o["y"][:SEQ].reshape(1, SEQ, D), o["y"][SEQ:].reshape(DB, DS, D),
            p("fk", FH, HD), p("fv", FH, HD), p("logf", FH), p("ckv", KVL), p("krope", ROPE),
            d("fk", FH, HD), d("fv", FH, HD), d("logf", FH), d("ckv", KVL), d("krope", ROPE))
```

```python
from contextlib import ExitStack

import numpy as np
import concourse.bass as bass
from concourse import mybir

F32 = mybir.dt.float32
F32R = mybir.dt.float32r
BF16 = mybir.dt.bfloat16
U32 = mybir.dt.uint32
ALU = mybir.AluOpType
ACT = mybir.ActivationFunctionType
AX = mybir.AxisListType

P = 128
D = 1024
KD = D // P
SEQ, DB, DS, PAST = 512, 8, 16, 256
TP = SEQ // P
T = TP + 1
NT = T * P
FH, HD = 8, 64
MH, NOPE, ROPE, VD = 8, 64, 32, 64
QL, KVL = 256, 128
L = PAST + DS
R_FF, R_CQ, R_CKV, R_KR = 0, FH, FH + QL, FH + QL + KVL
RW = R_KR + ROPE
FOX_SCALE = float(HD) ** -0.5
MLA_SCALE = float(NOPE + ROPE) ** -0.5
PH, NK, TK = 8, 128, 16
SEL = PH * TK
HALF = TK // 2
CAND = HALF * TK + HALF
EPS = 1e-6
NEG = -1e30
GROUP = 2
TD = 3
NTD = TD * P
TG = T - TD
BLOCKS = NK
PER = 4
GI = SEL // (PER * GROUP)
assert TG * GI * PER == BLOCKS
CHUNK = 32
CHUNKS = NTD // CHUNK
QUERY_ORDER = [("queries", 0), ("scores", 0), ("queries", 1), ("scores", 1)] + [
    (step, h + n) for h in range(2, PH, 2) for step in ("queries", "scores") for n in range(2)]
PARTS = 4
PART = CHUNK // PARTS
LAST_ORDER = [*range(TD, T), *range(TD)]


def peer_step_kernel(nc, t_in, t_out):
    base, end = 16512, 229344

    class Region:

        def __init__(self, at):
            self.at = at

        def __call__(self, name, shape, dtype=F32):
            size = int(np.prod(shape[1:])) * {F32: 4, F32R: 4, U32: 4, BF16: 2}[dtype]
            t = nc.alloc_sbuf_tensor_at(name, shape, dtype, offset=self.at)
            self.at += (size + 31) // 32 * 32
            assert self.at <= end, (name, self.at)
            return t

    with ExitStack() as ctx:
        def sem(name):
            return ctx.enter_context(nc.semaphore(name))

        r = Region(base)
        ident = r("ident", [P, P])
        ones = r("ones", [P, P])
        small = r("small", [P, 64])
        eps_col = r("eps_col", [P, 8])
        late_at = r.at
        c_rope = r("c_rope", [P, 2, NT])
        c_rrow = r("c_rrow", [P, 2, T, ROPE // 2])
        selh = r("selh", [P, FH, P], BF16)
        selb = r("selb", [P, DB, P])
        cb = r("cb", [P, 3 * P + DS], BF16)
        gm = r("gm", [P, KD])
        bfb = r("bfb", [P, T, FH])
        gq = r("gq", [P, QL])
        gkv = r("gkv", [P, KVL])
        fv = r("fv", [P, T, FH * HD])
        zt_at = r.at
        zT = r("zT", [P, T, 4, P])
        fqT = r("fqT", [P, 4, NT])
        kt_at = r.at
        kT = r("kT", [P, 4, NT])
        ncT = r("ncT", [P, SEQ])
        nc3 = r("nc3", [P, SEQ], BF16)
        nc_mid = r("nc_mid", [P, SEQ], BF16)
        w_uv = r("w_uv", [P, MH * VD])
        wu_at = r.at
        w_uq = r("w_uq", [P, 2, MH, P])
        w_uk = r("w_uk", [P, MH, NOPE])
        w_ukT = r("w_ukT", [P, MH, P])
        zr_at = r.at
        zr = r("zr", [P, T, RW])
        r2_at = r.at
        krl = r("krl", [P, T, P])
        cqn = r("cqn", [P, T, QL])
        ckvn = r("ckvn", [P, T, KVL])
        fk = r("fk", [P, T, FH * HD])
        a_at = r.at
        z = Region(zr_at)
        qps = z("qps", [P, DB, MH, DS])
        qrs = z("qrs", [P, DB, MH, DS])
        assert z.at <= r2_at
        a1 = Region(a_at)
        hT = a1("hT", [P, KD, NT])
        wv_at = a1.at
        rmsb = a1("rmsb", [P, NT])
        rstdb = a1("rstdb", [P, NT])
        wr_at = a1.at
        wr = a1("wr", [P, KD, RW])
        wk_at = a1.at
        wk = a1("wk", [P, KD, FH * HD])
        wv = Region(wv_at)("wv", [P, KD, FH * HD])
        assert wv_at + 4 * KD * FH * HD <= wk_at
        sq = Region(a1.at)("sq", [P, KD, NT])
        wk_hi = a1("wk_hi", [P, KD, FH * HD], F32R)
        wq_hi = Region(a1.at - 4 * KD * FH * HD)("wq_hi", [P, KD, FH * HD], F32R)
        wq_at = a1.at
        wq = a1("wq", [P, KD, FH * HD])
        wr_hi = Region(a1.at)("wr_hi", [P, KD, RW], F32R)
        wv_hi = a1("wv_hi", [P, KD, FH * HD], F32R)
        h_lo = Region(a_at)("h_lo", [P, KD, NT], F32R)
        wr_lo = Region(wr_at)("wr_lo", [P, KD, RW], F32R)
        wk_lo = Region(wk_at)("wk_lo", [P, KD, FH * HD], F32R)
        wv_lo = Region(wv_at)("wv_lo", [P, KD, FH * HD], F32R)
        wq_lo = Region(wq_at)("wq_lo", [P, KD, FH * HD], F32R)
        h_hi2 = [Region(at)(f"h_hi{n}", [P, KD // 2, NT], F32R) for n, at in enumerate((zt_at, kt_at))]

        def h_hi(k):
            return h_hi2[k // (KD // 2)][:, k % (KD // 2)]

        a2 = Region(a_at)
        qmT = a2("qmT", [P, MH, NT])
        kmT = a2("kmT", [P, MH, SEQ])
        vm = a2("vm", [P, TP, MH * VD])
        prob = a2("prob", [P, 4, SEQ])
        probT = a2("probT", [P, 3, SEQ])
        qbd = a2("qbd", [P, 4, DB, FH, DS])
        oT = a2("oT", [P, 8, NT])
        latT = a2("latT", [P, MH, P])
        s1 = Region(wu_at)
        vs = s1("vs", [P, 2, 2, FH * HD])
        ckTs = s1("ckTs", [P, 2, L])
        krTs = s1("krTs", [P, 2, L])
        assert s1.at <= zr_at
        s2 = Region(r2_at)
        kTs = s2("kTs", [P, 2, 4, L])
        vn = s2("vn", [P, 2, FH * HD])
        ckr = s2("ckr", [P, 2, 2, KVL])
        ckn = s2("ckn", [P, 2, KVL])
        lfs = s2("lfs", [P, L])
        ncS = s2("ncS", [P, L])
        assert s2.at <= a_at
        l1 = Region(late_at)
        x2 = l1("x2", [P, T, D])
        h2_at = l1.at
        h2 = l1("h2", [P, T, D])
        gfin = l1("gfin", [P, D])
        gate = l1("gate", [P, T, SEL])
        eidx = l1("eidx", [P, TG * SEL], U32)
        iota = l1("iota", [P, NK])
        gsum = l1("gsum", [P, 2, T * PH])
        ix = l1("ix", [P, PER, GROUP], U32)
        e_at = l1.at
        e1 = l1("e1", [P, T, SEL])
        e2 = l1("e2", [P, T, SEL])
        gap = l1("gap", [P, T, SEL])
        g_at = l1.at
        gffn = l1("gffn", [P, D])
        h2T = l1("h2T", [P, KD, NT])
        wpq = l1("wpq", [P, 2, KD, 2 * P])
        assert l1.at <= a_at
        l2 = Region(a_at)
        w_o = l2("w_o", [P, 8, D])
        assert l2.at <= a_at + 4 * MH * (NT + SEQ)
        top_at = end - 2 * 4 * KD * NTD
        hd = Region(top_at)
        hh = hd("hh", [P, KD, NTD], F32R)
        hl = hd("hl", [P, KD, NTD], F32R)
        l3 = Region(a_at)
        pq = l3("pq", [P, 2, 2, NT])
        pq2 = l3("pq2", [P, 2, 2, NT])
        keysT = l3("keysT", [P, 2 * PH, NK])
        scb = l3("scb", [P, 2, T, 2, NK])
        rt = l3("rt", [P, 2, 8])
        rs = l3("rs", [P, 2, 8])
        sr = l3("sr", [P, 2, T, 2, NK])
        cand_at = l3.at
        cand = l3("cand", [P, 2, T, CAND])
        candr = l3("candr", [P, 2, T, CAND])
        onehot = l3("onehot", [P, 2, T, TK, TK])
        onehot2 = Region(cand_at)("onehot2", [P, 2, T, TK, TK])
        assert TK * TK <= 2 * CAND
        v16 = l3("v16", [P, 2, T, 2, TK])
        i16 = l3("i16", [P, 2, T, 2, TK], U32)
        i16f = l3("i16f", [P, 2, T, 2, TK])
        cv = l3("cv", [P, 2, T, TK])
        ci = l3("ci", [P, 2, T, TK], U32)
        hi = l3("hi", [P, 2, T, TK], U32)
        lo = l3("lo", [P, 2, T, TK], U32)
        outer = l3("outer", [P, 2, T, TK], U32)
        assert l3.at <= top_at
        k9 = Region(g_at)
        i1T = k9("i1T", [P, NTD])
        i2T = k9("i2T", [P, NTD])
        gT = k9("gT", [P, NTD])
        bsel = k9("bsel", [P, PARTS, PART, NK])
        asel = k9("asel", [P, PARTS, PART, NK])
        stage = k9("stage", [P, 2, NK, CHUNK])
        assert k9.at <= top_at
        gbuf = Region(h2_at)("gbuf", [P, 2, CHUNKS, PER, CHUNK])
        assert TD * D >= 2 * PER * NTD
        z0 = Region(e_at)
        dots = z0("dots", [P, PER, GROUP])
        gelu = z0("gelu", [P, PER, GROUP])
        wts = z0("wts", [P, PER, GROUP])
        zero = z0("zero", [P, 512], F32R)
        actv = z0("actv", [P, 2, NTD])
        assert z0.at <= g_at
        k10 = Region(g_at)
        vbuf = k10("vbuf", [P, PER, GROUP, D])
        v_at = k10.at
        vb = k10("vb", [P, PER, D])
        vl = Region(v_at)("vl", [P, PER, D], F32R)
        vh = k10("vh", [P, 2, D], F32R)
        ga = k10("ga", [P, 2, NTD])
        acth = k10("acth", [P, 2, NTD], F32R)
        actl = k10("actl", [P, 2, NTD], F32R)
        k10 = Region(max(k9.at, k10.at))
        u_at = k10.at
        ub = k10("ub", [P, PER, KD, P])
        ul = Region(u_at)("ul", [P, PER, KD, P], F32R)
        uh = k10("uh", [P, 2, KD, P], F32R)
        ubuf = k10("ubuf", [P, PER, GROUP, D])
        assert k10.at <= top_at
        k11 = Region(g_at)
        yout = k11("yout", [P, T, D])

        spill = nc.dram_tensor("gate_matrix", [CHUNKS, P, NK, CHUNK], F32, kind="Internal").ap()
        ps = ctx.enter_context(nc.psum_tensor("ps", [P, 8, 512], F32))

        x_loaded, first_loaded = [sem("x_loaded0"), sem("x_loaded1")], sem("first_loaded")
        c_loaded, wr_loaded, wk_loaded, wv_loaded, wq_loaded, wu_loaded = (
            sem(n) for n in ("c_loaded", "wr_loaded", "wk_loaded", "wv_loaded", "wq_loaded", "wu_loaded"))
        squares, meansq, rms_ready, h_ready = (sem(n) for n in ("squares", "meansq", "rms_ready", "h_ready"))
        h_hi_ready, h_split, w_hi_ready, w_split = (
            sem(n) for n in ("h_hi_ready", "h_split", "w_hi_ready", "w_split"))
        proj_done, proj_copied = sem("proj_done"), sem("proj_copied")
        ss_ready, rt_ready, ff_abs, ff_log, rows_ready = (
            sem(n) for n in ("ss_ready", "rt_ready", "ff_abs", "ff_log", "rows_ready"))
        state_stored = sem("state_stored")
        tr_done, tr_copied = sem("tr_done"), sem("tr_copied")
        nc_ready, ncs_ready, lfs_loaded = sem("nc_ready"), sem("ncs_ready"), sem("lfs_loaded")
        mq_done, mq_nope, mq_rope = sem("mq_done"), sem("mq_nope"), sem("mq_rope")
        mk_done, mk_copied, kr_copied = sem("mk_done"), sem("mk_copied"), sem("kr_copied")
        qp_done, qs_ready, qbd_ready = sem("qp_done"), sem("qs_ready"), sem("qbd_ready")
        s_done, max_ready, exp_done, p_ready = sem("s_done"), sem("max_ready"), sem("exp_done"), sem("p_ready")
        pt_done, pt_copied, pv_done, o_copied = sem("pt_done"), sem("pt_copied"), sem("pv_done"), sem("o_copied")
        so_copied, lat_copied = sem("so_copied"), sem("lat_copied")
        batch_loaded = [sem("batch_loaded0"), sem("batch_loaded1")]
        new_keys = sem("new_keys")
        up_done = sem("up_done")
        wo_loaded, late_loaded, wpq_loaded = sem("wo_loaded"), sem("late_loaded"), [sem("wpq0"), sem("wpq1")]
        out_done, x2_ready, ss2_ready, rt2_ready, h2_ready = (
            sem(n) for n in ("out_done", "x2_ready", "ss2_ready", "rt2_ready", "h2_ready"))
        h2t_done, h2t_copied = sem("h2t_done"), sem("h2t_copied")
        pq_done, pq_copied, sc_done, sc_copied, sc_read = (
            sem(n) for n in ("pq_done", "pq_copied", "sc_done", "sc_copied", "sc_read"))
        hh_ready, hl_ready = sem("hh_ready"), sem("hl_ready")
        gap_ready, gap_exp, topk_done = sem("gap_ready"), sem("gap_exp"), sem("topk_done")
        selT_done, selT_copied = sem("selT_done"), sem("selT_copied")
        asel_ones, asel_ready, bsel_ready = sem("asel_ones"), sem("asel_ready"), sem("bsel_ready")
        sel_used, g_copied, g_stored = sem("sel_used"), sem("g_copied"), sem("g_stored")
        stage_free, bank_free, dense_open = sem("stage_free"), sem("bank_free"), sem("dense_open")
        ub_loaded = [sem(f"ub_loaded{k}") for k in range(PER)]
        vb_loaded = [sem(f"vb_loaded{k}") for k in range(PER)]
        gb_loaded = sem("gb_loaded")
        uh_ready, vh_ready, ul_ready, vl_ready = sem("uh_ready"), sem("vh_ready"), sem("ul_ready"), sem("vl_ready")
        a_done, ga_ready, act_ready, acth_ready, actl_ready, av_done = (
            sem(n) for n in ("a_done", "ga_ready", "act_ready", "acth_ready", "actl_ready", "av_done"))
        g_used, dense_done = sem("g_used"), sem("dense_done")
        ix_ready, eidx_ready = sem("ix_ready"), sem("eidx_ready")
        onehot_ready, decoded, decode_chain = sem("onehot_ready"), sem("decoded"), sem("decode_chain")
        u_loaded = [sem(f"u_loaded{k}") for k in range(PER)]
        v_loaded = [sem(f"v_loaded{k}") for k in range(PER)]
        dots_done, gelu_done, acc_done, y_link = sem("dots_done"), sem("gelu_done"), sem("acc_done"), sem("y_link")
        sum_ready = sem("sum_ready")
        ss3_ready, rt4_ready, y_ready, y_stored = (
            sem(n) for n in ("ss3_ready", "rt4_ready", "y_ready", "y_stored"))
        act_chain, dve_chain, dve_loop, pool_chain = (
            sem(n) for n in ("act_chain", "dve_chain", "dve_loop", "pool_chain"))
        wait_carrier = sem("wait_carrier")

        UNITS, SAMPLES = 64, 2 * DB
        plan = []
        for m in range(UNITS):
            plan.append(("prompt", m))
            plan += [("sample", k) for k in range(SAMPLES) if 8 + 7 * k // 2 == m + 1]
        ALL = len(plan)
        assert ALL == UNITS + SAMPLES
        place = {unit_: n for n, unit_ in enumerate(plan)}

        def is_prompt(n):
            return plan[n][0] == "prompt"

        def unit(n):
            m = plan[n][1]
            pair, hh, i = m // 8, m // 4 % 2, m % 4
            return 1 - pair // 4, pair % 4, hh, i, (i + 1) * P

        def keys_of(n):
            return unit(n)[4] if is_prompt(n) else L

        def batch_read(b):
            return place["sample", 2 * b + 1] + 1

        square = [P, 2 * T, TK, TK]

        def both(x):
            return x[:].rearrange("p s t k -> p (s t) k" if len(x.shape) == 4 else "p s t a b -> p (s t) a b")

        block = ctx.enter_context(nc.Block())

        @block.sync
        def _(sp):
            ld = sp.dma_start
            ld(ones[:], t_in["ones"]).then_inc(first_loaded, 16)
            ld(gm[:], t_in["gm"]).then_inc(first_loaded, 16)
            for n in range(2):
                k = slice(n * KD // 2, (n + 1) * KD // 2)
                ld(hT[:, k], t_in["xT"][:, k]).then_inc(x_loaded[n], 16)
            ld(wr[:], t_in["wr"]).then_inc(wr_loaded, 16)
            for dst, name in ((ident, "ident"), (c_rope, "c_rope"), (c_rrow, "c_rrow"),
                              (cb, "cb"), (bfb, "bfb"), (gq, "gq"), (gkv, "gkv")):
                ld(dst[:], t_in[name]).then_inc(c_loaded, 16)
            ld(selh[0:96], t_in["selh"]).then_inc(c_loaded, 16)
            ld(selb[0:DB * FH], t_in["selb"]).then_inc(c_loaded, 16)
            ld(wk[:], t_in["wk"]).then_inc(wk_loaded, 16)
            for dst, name in ((w_uq, "w_uq"), (w_uk, "w_uk"), (w_uv, "w_uv")):
                ld(dst[:], t_in[name]).then_inc(wu_loaded, 16)
            ld(w_ukT[0:NOPE], t_in["w_ukT"]).then_inc(wu_loaded, 16)
            sp.wait_ge(meansq, 1)
            ld(wq[:], t_in["wq"]).then_inc(wq_loaded, 16)
            sp.wait_ge(proj_done, 5)
            ld(wv[:], t_in["wv"]).then_inc(wv_loaded, 16)
            sp.wait_ge(proj_copied, 15)
            rows = lambda name: t_out[name].rearrange("(t p) c -> p t c", p=P)
            ld(rows("fk"), fk[:]).then_inc(state_stored, 16)
            ld(rows("fv"), fv[:]).then_inc(state_stored, 16)
            sp.wait_ge(rows_ready, 1)
            ld(rows("ckv"), ckvn[:]).then_inc(state_stored, 16)
            ld(rows("logf"), krl[:, :, 0:FH]).then_inc(state_stored, 16)
            ld(rows("krope"), krl[:, :, 64:64 + ROPE]).then_inc(state_stored, 16)
            sp.wait_ge(state_stored, 16 * 5)
            sp.wait_ge(tr_copied, 10)
            ld(lfs[0:64, 0:PAST], t_in["past_logf"]).then_inc(lfs_loaded, 16)
            new_logf = t_out["logf"][SEQ:NT].rearrange("(b q) h -> b h q", b=DB)
            for b in range(DB):
                ld(lfs[b * FH:(b + 1) * FH, PAST:L], new_logf[b], allow_slow_non_contiguous=True).then_inc(lfs_loaded, 16)

            def load_batch(b):
                s = b % 2
                if b == 0:
                    sp.wait_ge(qs_ready, 3)
                    sp.wait_ge(mk_copied, 8)
                if b >= 2:
                    sp.wait_ge(pv_done, batch_read(b - 2))
                q = batch_loaded[s]
                new = slice(SEQ + b * DS, SEQ + (b + 1) * DS)
                ld(kTs[:, s, :, 0:PAST], t_in["past_k"][b]).then_inc(q, 16)
                ld(vs[:, s], t_in["past_v"][b].rearrange("(j p) c -> p j c", p=P)).then_inc(q, 16)
                ld(vn[0:DS, s], t_out["fv"][new]).then_inc(q, 16)
                ld(ckTs[:, s, 0:PAST], t_in["past_ckvT"][b]).then_inc(q, 16)
                ld(krTs[64:96, s, 0:PAST], t_in["past_krT"][b]).then_inc(q, 16)
                ld(ckr[:, s], t_in["past_ckv"][b].rearrange("(j p) c -> p j c", p=P)).then_inc(q, 16)
                ld(ckn[0:DS, s], t_out["ckv"][new]).then_inc(q, 16)

            mla_read = place["prompt", UNITS // 2 - 1] + 1
            for b in range(DB):
                if b >= 2 and batch_read(b - 3 if b > 2 else 0) <= mla_read < batch_read(b - 2):
                    sp.wait_ge(pv_done, mla_read)
                    ld(w_o[:], t_in["w_o"]).then_inc(wo_loaded, 16)
                load_batch(b)
            sp.wait_ge(up_done, 1)
            sp.wait_ge(o_copied, 8)
            sp.wait_ge(lat_copied, 1)
            ld(x2[:], t_in["xr"].rearrange("(t p) c -> p t c", p=P)).then_inc(late_loaded, 16)
            ld(gffn[:], t_in["gffn"]).then_inc(late_loaded, 16)
            ld(gfin[:], t_in["gfin"]).then_inc(late_loaded, 16)
            ld(iota[:], t_in["iota"]).then_inc(late_loaded, 16)
            for h in range(PH):
                if h >= 2:
                    sp.wait_ge(pq_done, h - 1)
                ld(wpq[:, h % 2], t_in["wpq"][h]).then_inc(wpq_loaded[h % 2], 16)
                if h == 1:
                    sp.wait_ge(out_done, T)
                    ld(keysT[:], t_in["keysT"]).then_inc(late_loaded, 16)
            def load_u(block, slot):
                ld(ub[:, slot].rearrange("p k e -> p (k e)"),
                   t_in["peer_uT"][block].rearrange("a p k -> p (a k)")).then_inc(ub_loaded[slot], 16)

            sp.wait_ge(eidx_ready, 1)
            load_u(slice(0, 1), 0)
            sp.sem_inc(stage_free, 2)
            with sp.Fori(0, CHUNKS) as c:
                sp.wait_ge(g_copied, (c + 1) * CHUNK // 4)
                ld(spill[bass.ds(c, 1)].rearrange("a p k t -> p (a k t)"),
                   stage[:, bass.ds(c % 2, 1)].rearrange("p a k t -> p (a k t)")).then_inc(g_stored, 16)
                sp.wait_ge(g_stored, 16 * c + 16)
                sp.sem_inc(stage_free, 1)
            sp.wait_ge(g_stored, 16 * CHUNKS)
            sp.wait_ge(sel_used, NTD + CHUNK)

            with sp.Fori(0, TG) as t:
                with sp.Fori(0, GI) as j:
                    i = t * GI + j
                    sp.wait_ge(g_used, i + 1)
                    for q in range(4):
                        cs = slice(q * CHUNKS // 4, (q + 1) * CHUNKS // 4)
                        ld(gbuf[:, bass.ds(i % 2, 1), cs].rearrange("p a c k t -> p (a c) (k t)"),
                           spill[cs, :, bass.ds(i * PER, PER), :].rearrange("c p k t -> p c (k t)")).then_inc(gb_loaded, 16)
                    for s in range(PER):
                        n = i * PER + s
                        sp.wait_ge(a_done, n + 1)
                        load_u(bass.ds((n + 1) % BLOCKS, 1), (s + 1) % PER)
                        sp.wait_ge(av_done, n + 1)
                        ld(vb[:, s], t_in["peer_v"][bass.ds(n * P, P), :]).then_inc(vb_loaded[s], 16)
            sp.wait_ge(ub_loaded[0], 16 * (BLOCKS // PER + 1))
            for u, t in enumerate(LAST_ORDER):
                sp.wait_ge(y_ready, u + 1)
                ld(t_out["y"][t * P:(t + 1) * P], yout[:, t]).then_inc(y_stored, 16)
            sp.wait_ge(y_stored, 16 * T)

        @block.gpsimd
        def _(pool):
            links = [0]

            def link(ins):
                links[0] += 1
                ins.then_inc(pool_chain, 1)
                pool.wait_ge(pool_chain, links[0])

            pool.wait_ge(tr_copied, 5)
            pool.wait_ge(proj_done, 23)
            for h in range(MH):
                nc.gpsimd.tensor_copy(kmT[64:96, h, :].rearrange("p (t k) -> p t k", t=TP),
                                      zT[64:96, 0:TP, 3, :]).then_inc(kr_copied, 1)
                pool.wait_ge(kr_copied, h + 1)
            link(nc.gpsimd.memset(qbd[:], 0.0))
            pool.wait_ge(proj_copied, 23)
            for c in range(4):
                for hh in range(2):
                    rows = slice(64 * hh, 64 * hh + 64)
                    nc.gpsimd.tensor_copy(qbd[rows, c, :, 2 * c + hh, :],
                                          fqT[rows, c, SEQ:NT].rearrange("p (b q) -> p b q", b=DB)).then_inc(qbd_ready, 1)
                    pool.wait_ge(qbd_ready, 2 * c + hh + 1)
            for b in range(DB):
                s = b % 2
                new = slice(b * DS, (b + 1) * DS)
                if b == 0:
                    pool.wait_ge(state_stored, 16 * 5)
                    pool.wait_ge(qs_ready, 3)
                    pool.wait_ge(mk_copied, 8)
                    pool.wait_ge(tr_copied, 10)
                if b >= 2:
                    pool.wait_ge(pv_done, batch_read(b - 2))
                for i, (dst, src) in enumerate(((kTs[:, s, :, PAST:L], kT[:, :, SEQ + b * DS:SEQ + (b + 1) * DS]),
                                                (ckTs[:, s, PAST:L], zT[:, TP, 2, new]),
                                                (krTs[64:96, s, PAST:L], zT[64:96, TP, 3, new]))):
                    nc.gpsimd.tensor_copy(dst, src).then_inc(new_keys, 1)
                    pool.wait_ge(new_keys, 3 * b + i + 1)

            def gather(dst, table, slot, e, done):
                nc.gpsimd.indirect_dma_start(
                    out=dst[:, slot, e, :], out_offset=None, in_=t_in[table],
                    in_offset=bass.IndirectOffsetOnAxis(ix[:, slot, e:e + 1], 0),
                    bounds_check=NK * NK - 1, oob_is_err=True).then_inc(done[slot], 16)

            DECODE_LINKS = 8

            def decode(pair, parts):
                done = [0]

                def decode_step(ins):
                    done[0] += 1
                    ins.then_inc(decode_chain, 1)
                    pool.wait_ge(decode_chain, pair * DECODE_LINKS + done[0])
                    pool.sem_inc(wait_carrier, 1)

                for c, oh, dst in parts:
                    pool.wait_ge(onehot_ready, pair * 2 + (1 if c else 2))
                    pool.sem_inc(wait_carrier, 1)
                    x = both(oh)
                    index = i16f[:, :, :, c, :].rearrange("p s t k -> p (s t) k").unsqueeze(2).broadcast_to(square)
                    decode_step(nc.gpsimd.tensor_tensor(x, x, index, ALU.mult))
                    for w in (TK // 2, TK // 4, TK // 8):
                        decode_step(nc.gpsimd.tensor_tensor(x[:, :, :, 0:w], x[:, :, :, 0:w], x[:, :, :, w:2 * w], ALU.add))
                    for s in range(2):
                        ins = nc.gpsimd.tensor_tensor(dst[:, :, bass.ds((pair * 2 + s) * TK, TK)],
                                                      oh[:, s, :, :, 0], oh[:, s, :, :, 1], ALU.add)
                    ins.then_inc(decoded, 1)

            with pool.Fori(0, PH // 2 - 1) as pair:
                decode(pair, ((1, onehot2, e2), (0, onehot, e1)))
            decode(PH // 2 - 1, ((1, onehot2, e2),))

            pool.wait_ge(eidx_ready, 1)
            for s in range(PER):
                nc.gpsimd.tensor_copy(ix[:, s], eidx[:, s * GROUP:(s + 1) * GROUP]).then_inc(ix_ready, 1)
            pool.wait_ge(ix_ready, PER)
            for s in range(PER):
                for e in range(GROUP):
                    gather(ubuf, "peer_u", s, e, u_loaded)

            pool.wait_ge(selT_copied, 3)
            with pool.Fori(0, CHUNKS) as c:
                for q in range(PARTS):
                    pool.wait_ge(asel_ones, PARTS * c + q + 1)
                    pool.sem_inc(wait_carrier, 1)
                    nc.gpsimd.tensor_tensor(
                        asel[:, q], asel[:, q],
                        gT[:, bass.ds(c * CHUNK + q * PART, PART)].unsqueeze(2).broadcast_to([P, PART, NK]),
                        ALU.mult).then_inc(asel_ready, 1)

            pool.wait_ge(g_stored, 16 * CHUNKS)
            pool.wait_ge(sel_used, NTD + CHUNK)
            for s in range(PER):
                for e in range(GROUP):
                    gather(vbuf, "peer_v", s, e, v_loaded)
            with pool.Fori(1, TG * GI) as i:
                for s in range(PER):
                    n = i * PER + s
                    pool.wait_ge(acc_done, n + 1)
                    pool.sem_inc(wait_carrier, 1)
                    nc.gpsimd.tensor_copy(ix[:, s], eidx[:, bass.ds(n * GROUP, GROUP)]).then_inc(ix_ready, 1)
                    pool.wait_ge(ix_ready, n + 1)
                    pool.sem_inc(wait_carrier, 1)
                    for e in range(GROUP):
                        gather(ubuf, "peer_u", s, e, u_loaded)
                    for e in range(GROUP):
                        gather(vbuf, "peer_v", s, e, v_loaded)

        @block.scalar
        def _(act):
            links = [0]
            A = nc.scalar.activation

            def link(ins):
                links[0] += 1
                ins.then_inc(act_chain, 1)
                act.wait_ge(act_chain, links[0])

            for k in range(KD):
                if k % (KD // 2) == 0:
                    act.wait_ge(x_loaded[k // (KD // 2)], 16)
                A(sq[:, k], hT[:, k], ACT.Square).then_inc(squares, 1)
            act.wait_ge(wr_loaded, 16)
            A(wr_hi[:], wr[:], ACT.Copy).then_inc(w_hi_ready, 1)
            act.wait_ge(meansq, 1)
            act.wait_ge(dve_chain, 1)
            A(rmsb[:, 0:SEQ], ps[:, 0, :], ACT.Sqrt, scale=1.0 / D, bias=eps_col[:, 0:1]).then_inc(rms_ready, 1)
            A(rmsb[:, SEQ:NT], ps[:, 1, 0:P], ACT.Sqrt, scale=1.0 / D, bias=eps_col[:, 0:1]).then_inc(rms_ready, 1)

            for k in range(KD):
                act.wait_ge(h_ready, k + 1)
                A(h_hi(k), hT[:, k], ACT.Copy).then_inc(h_hi_ready, 1)
            act.wait_ge(wk_loaded, 16)
            A(wk_hi[:], wk[:], ACT.Copy).then_inc(w_hi_ready, 1)

            def copy_projection(n):
                act.wait_ge(proj_done, n + 1)
                bank = ps[:, 2 + n % 4]
                if n < 5:
                    A(zr[:, n], bank[:, 0:RW], ACT.Copy).then_inc(proj_copied, 1)
                elif n < 10:
                    A(fk[:, n - 5], bank, ACT.Copy).then_inc(proj_copied, 1)
                elif n < 15:
                    A(fv[:, n - 10], bank, ACT.Copy).then_inc(proj_copied, 1)
                else:
                    c, part = divmod(n - 15, 2)
                    A(fqT[:, c, part * NT // 2:(part + 1) * NT // 2], bank[:, 0:NT // 2], ACT.Copy,
                      scale=FOX_SCALE).then_inc(proj_copied, 1)

            for n_ in range(10):
                copy_projection(n_)
                if n_ == 6:
                    act.wait_ge(wv_loaded, 16)
                    A(wv_hi[:], wv[:], ACT.Copy).then_inc(w_hi_ready, 1)
            act.wait_ge(wq_loaded, 16)
            A(wq_hi[:], wq[:], ACT.Copy).then_inc(w_hi_ready, 1)
            act.wait_ge(ss_ready, 1)
            A(small[:, 10:15], small[:, 0:5], ACT.Sqrt, scale=1.0 / QL, bias=eps_col[:, 0:1])
            A(small[:, 15:20], small[:, 5:10], ACT.Sqrt, scale=1.0 / KVL, bias=eps_col[:, 0:1]).then_inc(rt_ready, 1)
            act.wait_ge(ff_abs, 1)
            link(A(krl[:, :, 8:16], krl[:, :, 24:32], ACT.Exp))
            A(krl[:, :, 16:24], krl[:, :, 8:16], ACT.Ln, bias=1.0).then_inc(ff_log, 1)
            for n_ in range(10, 23):
                copy_projection(n_)
            for u in range(10):
                act.wait_ge(tr_done, u + 1)
                bank = ps[:, 6 + u % 2].rearrange("p (c k) -> p c k", c=4)
                if u < 5:
                    A(zT[:, u], bank, ACT.Copy).then_inc(tr_copied, 1)
                else:
                    A(kT[:, :, (u - 5) * P:(u - 4) * P], bank, ACT.Copy).then_inc(tr_copied, 1)
            for h in range(MH):
                b = 3 * (h % 2)
                act.wait_ge(mq_done, h + 1)
                A(qmT[0:NOPE, h, 0:SEQ], ps[0:NOPE, b], ACT.Copy, scale=MLA_SCALE)
                A(qmT[0:NOPE, h, SEQ:NT], ps[0:NOPE, b + 2, 0:P], ACT.Copy, scale=MLA_SCALE).then_inc(mq_nope, 1)
            for u in range(12):
                act.wait_ge(mk_done, u + 1)
                bank = ps[:, u % 4]
                if u < 8:
                    A(kmT[0:NOPE, u], bank[0:NOPE], ACT.Copy).then_inc(mk_copied, 1)
                else:
                    A(vm[:, u - 8], bank, ACT.Copy).then_inc(mk_copied, 1)
            for g in range(2):
                act.wait_ge(qp_done, g + 1)
                if g == 0:
                    act.wait_ge(rows_ready, 1)
                A(qps[:, :, 4 * g:4 * g + 4, :].rearrange("p b h q -> p h b q"),
                  ps[:, 4 + g].rearrange("p (h b q) -> p h b q", h=4, b=DB), ACT.Copy).then_inc(qs_ready, 1)
            act.wait_ge(mq_rope, MH)
            A(qrs[64:96].rearrange("p b h q -> p h b q"),
              qmT[64:96, :, SEQ:NT].rearrange("p h (b q) -> p h b q", b=DB), ACT.Copy).then_inc(qs_ready, 1)

            def exponentials(n):
                nk = keys_of(n)
                act.wait_ge(max_ready, n + 1)
                if n >= 4:
                    act.wait_ge(pt_done, n - 3)
                A(prob[:, n % 4, 0:nk], ps[:, n % 3, 0:nk], ACT.Exp, bias=small[:, 32 + n % 4:33 + n % 4],
                  accum_out=small[:, 36 + n % 4:37 + n % 4]).then_inc(exp_done, 1)

            def copy_transposed(n):
                act.wait_ge(pt_done, n + 1)
                if n >= 3:
                    act.wait_ge(pv_done, n - 2)
                bank = ps[:, 3 + n % 2]
                if is_prompt(n):
                    nk = keys_of(n)
                    A(probT[:, n % 3, 0:nk], bank[:, 0:nk], ACT.Copy).then_inc(pt_copied, 1)
                else:
                    A(probT[:, n % 3, 0:PAST], bank[:, 0:PAST], ACT.Copy)
                    A(probT[0:DS, n % 3, PAST:PAST + P], bank[0:DS, PAST:PAST + P], ACT.Copy).then_inc(pt_copied, 1)

            for n_ in range(ALL + 2):
                if n_ < ALL:
                    exponentials(n_)
                if n_ >= 2:
                    copy_transposed(n_ - 2)
            for t in range(T):
                act.wait_ge(ss2_ready, t + 1)
                A(small[:, 45 + t:46 + t], small[:, 40 + t:41 + t], ACT.Sqrt, scale=1.0 / D,
                  bias=eps_col[:, 0:1]).then_inc(rt2_ready, 1)
                if t == T - 1:
                    act.wait_ge(h2t_copied, 2 * t)
                    A(hh[:], h2T[:, :, 0:NTD], ACT.Copy).then_inc(hh_ready, 1)
                for g in range(2):
                    act.wait_ge(h2t_done, 2 * t + g + 1)
                    A(h2T[:, 4 * g:4 * g + 4, t * P:(t + 1) * P],
                      ps[:, 4 + g].rearrange("p (c k) -> p c k", c=4), ACT.Copy).then_inc(h2t_copied, 1)

            def copy_queries(h):
                act.wait_ge(pq_done, h + 1)
                if h >= 2:
                    act.wait_ge(sc_done, h - 1)
                s = h % 2
                A(pq[:, s, :, 0:SEQ], ps[:, 0:2, :], ACT.Copy)
                link(A(pq[:, s, :, SEQ:NT], ps[:, 2, 0:2 * P].rearrange("p (c k) -> p c k", c=2), ACT.Copy))
                A(pq2[:, s], pq[:, s], ACT.Square).then_inc(pq_copied, 1)

            def copy_scores(h):
                act.wait_ge(sc_done, h + 1)
                if h >= 2:
                    act.wait_ge(sc_read, h - 1)
                s = h % 2
                flat = scb[:, s].rearrange("p t c k -> p (t c k)")
                A(flat[:, 0:1024], ps[:, 3:5, :].rearrange("p a b -> p (a b)"), ACT.Copy)
                A(flat[:, 1024:1280], ps[:, 5, 0:256], ACT.Copy)
                A(rt[:, s, 0:T], ps[:, 6, 0:T], ACT.Sqrt, scale=1.0 / (2 * P), bias=eps_col[:, 0:1]).then_inc(sc_copied, 1)

            for step, h in QUERY_ORDER:
                {"queries": copy_queries, "scores": copy_scores}[step](h)
            act.wait_ge(gap_ready, 1)
            A(gap[:], gap[:], ACT.Exp).then_inc(gap_exp, 1)
            for u, dst in enumerate((gT, i1T, i2T)):
                act.wait_ge(selT_done, u + 1)
                A(dst[:], ps[:, u, 0:NTD], ACT.Copy).then_inc(selT_copied, 1)
            act.wait_ge(selT_copied, 3)
            act.sem_inc(bank_free, CHUNK // 4)
            with act.Fori(0, CHUNKS) as c:
                act.wait_ge(stage_free, c + 1)
                act.sem_inc(wait_carrier, 1)
                for g in range(CHUNK // 4):
                    act.wait_ge(sel_used, c * CHUNK + 4 * g + 4 + CHUNK)
                    act.sem_inc(wait_carrier, 1)
                    A(stage[:, bass.ds(c % 2, 1), :, 4 * g:4 * g + 4].rearrange("p a k t -> p (a t) k"),
                      ps[:, g].rearrange("p (t k) -> p t k", t=4), ACT.Copy).then_inc(g_copied, 1)
                    act.wait_ge(g_copied, c * (CHUNK // 4) + g + 1)
                    act.sem_inc(bank_free, 1)

            act.wait_ge(ub_loaded[0], 16)
            A(uh[:, 0], ub[:, 0], ACT.Copy).then_inc(uh_ready, 1)
            with act.Fori(0, TG) as t:
                with act.Fori(0, GI) as j:
                    i = t * GI + j
                    for s in range(PER):
                        n, nxt = i * PER + s, (s + 1) % PER
                        act.wait_ge(vb_loaded[s], 16 * i + 16)
                        act.wait_ge(av_done, n + 3)
                        A(vh[:, s % 2], vb[:, s], ACT.Copy).then_inc(vh_ready, 1)
                        act.wait_ge(ub_loaded[nxt], 16 * i + (32 if nxt == 0 else 16))
                        act.wait_ge(a_done, n + 3)
                        A(uh[:, nxt % 2], ub[:, nxt], ACT.Copy).then_inc(uh_ready, 1)
                        act.wait_ge(dots_done, n + 1)
                        A(gelu[:, s], dots[:, s], ACT.Gelu).then_inc(gelu_done, 1)
                        act.wait_ge(a_done, n + 4)
                        A(ga[:, s % 2], ps[:, 6 + s % 2, 0:NTD], ACT.Gelu).then_inc(ga_ready, 1)
                        act.wait_ge(act_ready, n + 1)
                        A(acth[:, s % 2], actv[:, s % 2], ACT.Copy).then_inc(acth_ready, 1)
            for u, t in enumerate(LAST_ORDER[:TG]):
                act.wait_ge(ss3_ready, u + 1)
                A(small[:, 45 + t:46 + t], small[:, 40 + t:41 + t], ACT.Sqrt, scale=1.0 / D,
                  bias=eps_col[:, 0:1]).then_inc(rt4_ready, 1)
            for t in range(TD):
                act.wait_ge(sum_ready, t + 1)
                ins = A(yout[:, t], x2[:, t], ACT.Square, accum_out=small[:, 40 + t:41 + t])
            link(ins)
            A(small[:, 45:45 + TD], small[:, 40:40 + TD], ACT.Sqrt, scale=1.0 / D, bias=eps_col[:, 0:1]).then_inc(rt4_ready, 1)

        @block.tensor
        def _(pe):
            mm, tr = nc.tensor.matmul, nc.tensor.transpose
            identb, fmask, mmask, nmask = cb[:, 0:P], cb[:, P:2 * P], cb[:, 2 * P:3 * P], cb[:, 3 * P:3 * P + DS]
            pe.wait_ge(first_loaded, 32)
            for k in range(KD):
                pe.wait_ge(squares, k + 1)
                mm(ps[:, 0, :], ones[:], sq[:, k, 0:SEQ], start=(k == 0), stop=(k == KD - 1))
                last = mm(ps[:, 1, 0:P], ones[:], sq[:, k, SEQ:NT], start=(k == 0), stop=(k == KD - 1))
            last.then_inc(meansq, 1)
            for n in range(23):
                if n >= 4:
                    pe.wait_ge(proj_copied, n - 3)
                bank = ps[:, 2 + n % 4]
                if n in (0, 5, 10, 15):
                    pe.wait_ge(w_split, n // 5 + 1)
                for k in range(KD):
                    if n == 0:
                        pe.wait_ge(h_split, k + 1)
                    if n < 15:
                        rows = slice(n % 5 * P, (n % 5 + 1) * P)
                        w_hi, w_lo = ((wr_hi, wr_lo), (wk_hi, wk_lo), (wv_hi, wv_lo))[n // 5]
                        out = bank[:, 0:w_hi.shape[2]]
                        a_hi, a_lo, b_hi, b_lo = h_hi(k)[:, rows], h_lo[:, k, rows], w_hi[:, k, :], w_lo[:, k, :]
                    else:
                        c, part = divmod(n - 15, 2)
                        feats, cols = slice(c * P, (c + 1) * P), slice(part * NT // 2, (part + 1) * NT // 2)
                        out = bank[:, 0:NT // 2]
                        a_hi, a_lo, b_hi, b_lo = wq_hi[:, k, feats], wq_lo[:, k, feats], h_hi(k)[:, cols], h_lo[:, k, cols]
                    mm(out, a_hi, b_hi, start=(k == 0), stop=False)
                    mm(out, a_hi, b_lo, start=False, stop=False)
                    last = mm(out, a_lo, b_hi, start=False, stop=(k == KD - 1))
                last.then_inc(proj_done, 1)
            pe.wait_ge(c_loaded, 16 * 9)
            for u in range(10):
                if u == 0:
                    pe.wait_ge(rows_ready, 1)
                if u >= 2:
                    pe.wait_ge(tr_copied, u - 1)
                t = u % 5
                src = [cqn[:, t, 0:P], cqn[:, t, P:2 * P], ckvn[:, t], krl[:, t]] if u < 5 else \
                      [fk[:, t, c * P:(c + 1) * P] for c in range(4)]
                for c in range(4):
                    last = tr(ps[:, 6 + u % 2, c * P:(c + 1) * P], src[c], ident[:])
                last.then_inc(tr_done, 1)
            pe.wait_ge(wu_loaded, 16 * 4)
            pe.wait_ge(tr_copied, 5)
            pe.wait_ge(proj_copied, 23)
            for h in range(MH):
                b = 3 * (h % 2)
                if h >= 2:
                    pe.wait_ge(mq_nope, h - 1)
                    pe.wait_ge(mq_rope, h - 1)
                for k in range(2):
                    on = dict(start=(k == 0), stop=(k == 1))
                    mm(ps[0:96, b, :], w_uq[:, k, h, 0:96], zT[:, 0:TP, k, :], **on)
                    mm(ps[64:96, b + 1, :], w_uq[:, k, h, 96:P], zT[:, 0:TP, k, :], **on)
                for k in range(2):
                    mm(ps[0:96, b + 2, 0:P], w_uq[:, k, h, 0:96], zT[:, TP, k, :], start=(k == 0), stop=(k == 1))
                for k in range(2):
                    last = mm(ps[64:96, b + 2, P:2 * P], w_uq[:, k, h, 96:P], zT[:, TP, k, :],
                              start=(k == 0), stop=(k == 1))
                last.then_inc(mq_done, 1)
            pe.wait_ge(mq_nope, MH)
            pe.wait_ge(mq_rope, MH)
            for u in range(12):
                if u >= 4:
                    pe.wait_ge(mk_copied, u - 3)
                if u < 8:
                    mm(ps[0:NOPE, u % 4], w_uk[:, u], zT[:, 0:TP, 2, :], start=True, stop=True).then_inc(mk_done, 1)
                else:
                    mm(ps[:, u % 4], zT[:, u - 8, 2, :], w_uv[:], start=True, stop=True).then_inc(mk_done, 1)
            for h in range(MH):
                last = mm(ps[:, 4 + h // 4, (h % 4) * P:(h % 4 + 1) * P], w_ukT[0:NOPE, h], qmT[0:NOPE, h, SEQ:NT],
                          start=True, stop=True)
                if h % 4 == 3:
                    last.then_inc(qp_done, 1)

            def scores(n):
                bank = ps[:, n % 3]
                if n >= 3:
                    pe.wait_ge(exp_done, n - 2)
                if n == 0:
                    pe.wait_ge(mk_copied, 12)
                    pe.wait_ge(kr_copied, MH)
                if n == place["prompt", UNITS // 2]:
                    pe.wait_ge(nc_ready, 1)
                if is_prompt(n):
                    kind, c, hh, i, nk = unit(n)
                    h = 2 * c + hh
                    diag = bank[:, i * P:(i + 1) * P]
                    if kind == 0:
                        rows = slice(64 * hh, 64 * hh + 64)
                        mm(bank[:, 0:nk], fqT[rows, c, i * P:(i + 1) * P], kT[rows, c, 0:nk], start=True, stop=False)
                        mm(bank[:, 0:nk], selh[0:96, h], nc3[0:96, 0:nk], start=False, stop=False)
                        mm(diag, identb, fmask, start=False, stop=True).then_inc(s_done, 1)
                    else:
                        mm(bank[:, 0:nk], qmT[0:96, h, i * P:(i + 1) * P], kmT[0:96, h, 0:nk], start=True, stop=False)
                        mm(diag, identb, mmask, start=False, stop=True).then_inc(s_done, 1)
                    return
                b, kind = divmod(plan[n][1], 2)
                s = b % 2
                if kind == 0:
                    pe.wait_ge(batch_loaded[s], 16 * 7 * (b // 2 + 1))
                    pe.wait_ge(new_keys, 3 * (b + 1))
                    if b == 0:
                        pe.wait_ge(qbd_ready, 8)
                        pe.wait_ge(ncs_ready, 1)
                        pe.wait_ge(qs_ready, 3)
                    for c in range(4):
                        mm(bank[:, 0:L], qbd[:, c, b].rearrange("p h q -> p (h q)"), kTs[:, s, c], start=(c == 0), stop=False)
                    mm(bank[:, 0:L], selb[0:64, b], ncS[0:64], start=False, stop=False)
                    mm(bank[:, PAST:L], identb, nmask, start=False, stop=True).then_inc(s_done, 1)
                else:
                    mm(bank[:, 0:L], qps[:, b].rearrange("p h q -> p (h q)"), ckTs[:, s], start=True, stop=False)
                    mm(bank[:, 0:L], qrs[64:96, b].rearrange("p h q -> p (h q)"), krTs[64:96, s],
                       start=False, stop=True).then_inc(s_done, 1)

            def transpose_probabilities(n):
                pe.wait_ge(p_ready, n + 1)
                if n >= 2:
                    pe.wait_ge(pt_copied, n - 1)
                nk = keys_of(n)
                for c in range((nk + P - 1) // P):
                    w = min(P, nk - c * P)
                    last = tr(ps[0:w, 3 + n % 2, c * P:(c + 1) * P], prob[:, n % 4, c * P:c * P + w], ident[:])
                last.then_inc(pt_done, 1)

            def values(n):
                pe.wait_ge(pt_copied, n + 1)
                pT = probT[:, n % 3]
                if is_prompt(n):
                    kind, c, hh, i, nk = unit(n)
                    pair = plan[n][1] // 8
                    if plan[n][1] % 8 == 0 and pair >= 2:
                        pe.wait_ge(o_copied, pair - 1)
                    rows = slice(64 * hh, 64 * hh + 64)
                    for k in range(i + 1):
                        v = (fv, vm)[kind][:, k, (2 * c + hh) * 64:(2 * c + hh + 1) * 64]
                        last = mm(ps[rows, 5 + pair % 2, i * P:(i + 1) * P], v, pT[:, k * P:(k + 1) * P],
                                  start=(k == 0), stop=(k == i))
                    last.then_inc(pv_done, 1)
                    return
                m = plan[n][1]
                b, kind = divmod(m, 2)
                s = b % 2
                if m >= 1:
                    pe.wait_ge(so_copied, m)
                bank = ps[:, 7]
                for c in range(4 if kind == 0 else 1):
                    for k in range(3):
                        rows = slice(0, P if k < 2 else DS)
                        on = dict(start=(k == 0), stop=(k == 2))
                        if kind == 0:
                            v = vs[:, s, k, c * P:(c + 1) * P] if k < 2 else vn[0:DS, s, c * P:(c + 1) * P]
                            last = mm(bank[:, 32 * c:32 * c + 32], v, pT[rows, k * P + 32 * c:k * P + 32 * c + 32], **on)
                        else:
                            v = ckr[:, s, k] if k < 2 else ckn[0:DS, s]
                            last = mm(bank[:, 0:P], v, pT[rows, k * P:(k + 1) * P], **on)
                last.then_inc(pv_done, 1)

            for n in range(ALL + 3):
                if n < ALL:
                    scores(n)
                if 2 <= n < ALL + 2:
                    transpose_probabilities(n - 2)
                if n >= 3:
                    values(n - 3)
            pe.wait_ge(so_copied, SAMPLES)
            for h in range(MH):
                last = mm(ps[64 * (h % 2):64 * (h % 2) + 64, 7, (h // 2) * P:(h // 2 + 1) * P],
                          w_uv[:, h * VD:(h + 1) * VD], latT[:, h], start=True, stop=True)
            last.then_inc(up_done, 1)

            def project_out(t):
                if t == 0:
                    pe.wait_ge(wo_loaded, 16)
                    pe.wait_ge(o_copied, 8)
                    pe.wait_ge(lat_copied, 1)
                if t >= 2:
                    pe.wait_ge(x2_ready, t - 1)
                for j in range(2):
                    for c in range(8):
                        last = mm(ps[:, 2 * (t % 2) + j], oT[:, c, t * P:(t + 1) * P], w_o[:, c, j * 512:(j + 1) * 512],
                                  start=(c == 0), stop=(c == 7))
                last.then_inc(out_done, 1)

            def transpose_h2(t):
                pe.wait_ge(h2_ready, t + 1)
                for g in range(2):
                    if t >= 1:
                        pe.wait_ge(h2t_copied, 2 * (t - 1) + g + 1)
                    for c in range(4):
                        k = 4 * g + c
                        last = tr(ps[:, 4 + g, c * P:(c + 1) * P], h2[:, t, k * P:(k + 1) * P], ident[:])
                    last.then_inc(h2t_done, 1)

            def prompt_queries(h):
                pe.wait_ge(wpq_loaded[h % 2], 16 * (h // 2 + 1))
                if h == 0:
                    pe.wait_ge(h2t_copied, 2 * TP)
                    pe.wait_ge(x2_ready, T)
                else:
                    pe.wait_ge(pq_copied, h)
                for k in range(KD):
                    for c in range(2):
                        mm(ps[:, c], wpq[:, h % 2, k, c * P:(c + 1) * P], h2T[:, k, 0:SEQ], start=(k == 0), stop=(k == KD - 1))

            def sample_queries(h):
                if h == 0:
                    pe.wait_ge(h2t_copied, 2 * T)
                for c in range(2):
                    for k in range(KD):
                        last = mm(ps[:, 2, c * P:(c + 1) * P], wpq[:, h % 2, k, c * P:(c + 1) * P], h2T[:, k, SEQ:NT],
                                  start=(k == 0), stop=(k == KD - 1))
                last.then_inc(pq_done, 1)

            def queries(h):
                prompt_queries(h)
                sample_queries(h)

            project_out(0)
            for t in range(T):
                if t + 1 < T:
                    project_out(t + 1)
                else:
                    prompt_queries(0)
                transpose_h2(t)
            sample_queries(0)

            def key_scores(h):
                pe.wait_ge(pq_copied, h + 1)
                if h == 0:
                    pe.wait_ge(late_loaded, 16 * 5)
                else:
                    pe.wait_ge(sc_copied, h)
                for t in range(T):
                    for c in range(2):
                        mm(ps[:, 3 + t // 2, 256 * (t % 2) + c * P:256 * (t % 2) + (c + 1) * P],
                           pq[:, h % 2, c, t * P:(t + 1) * P], keysT[:, 2 * h + c], start=True, stop=True)
                for t in range(T):
                    for c in range(2):
                        last = mm(ps[:, 6, t:t + 1], pq2[:, h % 2, c, t * P:(t + 1) * P], ones[:, 0:1],
                                  start=(c == 0), stop=(c == 1))
                last.then_inc(sc_done, 1)

            for step, h in QUERY_ORDER:
                if (step, h) != ("queries", 0):
                    {"queries": queries, "scores": key_scores}[step](h)
            pe.wait_ge(sc_copied, PH)
            pe.wait_ge(topk_done, 1)
            for u, src in enumerate((gate, e1, e2)):
                if u == 1:
                    pe.wait_ge(eidx_ready, 1)
                for t in range(TD):
                    last = tr(ps[:, u, t * P:(t + 1) * P], src[:, t], ident[:])
                last.then_inc(selT_done, 1)
            pe.wait_ge(selT_copied, 3)
            pe.sem_inc(sel_used, CHUNK)
            with pe.Fori(0, CHUNKS) as c:
                for q in range(PARTS):
                    pe.wait_ge(asel_ready, PARTS * c + q + 1)
                    pe.wait_ge(bsel_ready, PARTS * c + q + 1)
                    for g in range(q * PART // 4, (q + 1) * PART // 4):
                        pe.wait_ge(bank_free, c * (CHUNK // 4) + g + 1)
                        for k in range(4):
                            tok = 4 * g + k - q * PART
                            last = mm(ps[:, g, k * P:(k + 1) * P], bsel[:, q, tok], asel[:, q, tok],
                                      start=True, stop=True)
                            last.then_inc(sel_used, 1)
            pe.wait_ge(g_copied, CHUNKS * CHUNK // 4)
            pe.wait_ge(dense_open, 5)
            pe.wait_ge(hl_ready, 1)
            for b in range(2 * TD):
                mm(ps[:, b], zero[:, 0:P], zero[:], start=True, stop=False, skip_group_check=True)

            def values_block(s, done, last_block=False):
                for d in range(TD):
                    for n, (a, v) in enumerate(((acth[:, s % 2], vh[:, s % 2]), (acth[:, s % 2], vl[:, s]),
                                                (actl[:, s % 2], vh[:, s % 2]))):
                        for half in range(2):
                            ins = mm(ps[:, 2 * d + half], a[:, d * P:(d + 1) * P], v[:, half * 512:(half + 1) * 512],
                                     start=False, stop=last_block and n == 2, skip_group_check=True)
                    if last_block or d == TD - 1:
                        ins.then_inc(done, 1)

            pe.sem_inc(a_done, 3)
            pe.sem_inc(av_done, 3)
            with pe.Fori(0, TG) as t:
                with pe.Fori(0, GI) as j:
                    i = t * GI + j
                    for s in range(PER):
                        n, slot = i * PER + s, s % 2
                        pe.wait_ge(ul_ready, n + 1)
                        pe.wait_ge(ga_ready, n + 1)
                        for k in range(KD):
                            mm(ps[:, 6 + slot, 0:NTD], uh[:, slot, k], hh[:, k], start=(k == 0), stop=False)
                            mm(ps[:, 6 + slot, 0:NTD], uh[:, slot, k], hl[:, k], start=False, stop=False)
                            last = mm(ps[:, 6 + slot, 0:NTD], ul[:, s, k], hh[:, k], start=False, stop=(k == KD - 1))
                        last.then_inc(a_done, 1)
                        pe.wait_ge(actl_ready, n + 1)
                        pe.wait_ge(vl_ready, n + 1)
                        values_block((s - 1) % PER, av_done)
            pe.wait_ge(actl_ready, BLOCKS + 1)
            pe.wait_ge(vl_ready, BLOCKS + 1)
            values_block(PER - 1, dense_done, last_block=True)

        @block.vector
        def _(dve):
            V = nc.vector
            links = [0]

            def link(ins):
                links[0] += 1
                ins.then_inc(dve_chain, 1)
                dve.wait_ge(dve_chain, links[0])

            def low_part(low, full, high, high_ready, count, done):
                dve.wait_ge(high_ready, count)
                V.tensor_tensor(low, full, high.bitcast(F32), ALU.subtract).then_inc(done, 1)

            V.memset(krl[:], 0.0)
            V.memset(nc3[:], 0.0)
            link(V.memset(eps_col[:], EPS))
            dve.wait_ge(first_loaded, 32)
            low_part(wr_lo[:], wr[:], wr_hi[:], w_hi_ready, 1, w_split)
            dve.wait_ge(rms_ready, 2)
            link(V.reciprocal(rstdb[:], rmsb[:]))
            for k in range(KD):
                V.scalar_tensor_tensor(out=hT[:, k], in0=hT[:, k], scalar=gm[:, k:k + 1], in1=rstdb[:],
                                       op0=ALU.mult, op1=ALU.mult).then_inc(h_ready, 1)
                if k >= 1:
                    low_part(h_lo[:, k - 1], hT[:, k - 1], h_hi(k - 1), h_hi_ready, k, h_split)
            low_part(h_lo[:, KD - 1], hT[:, KD - 1], h_hi(KD - 1), h_hi_ready, KD, h_split)
            low_part(wk_lo[:], wk[:], wk_hi[:], w_hi_ready, 2, w_split)
            dve.wait_ge(c_loaded, 16 * 9)
            dve.wait_ge(proj_copied, 5)
            for t in range(T):
                for q, (off, width) in enumerate(((R_CQ, QL), (R_CKV, KVL))):
                    a = zr[:, t, off:off + width]
                    ins = V.tensor_tensor_reduce(out=(cqn, ckvn)[q][:, t], in0=a, in1=a, scale=1.0, scalar=0.0, op0=ALU.mult,
                                                 op1=ALU.add, accum_out=small[:, 5 * q + t:5 * q + t + 1])
            ins.then_inc(ss_ready, 1)
            x_ff = krl[:, :, 32:40]
            link(V.tensor_tensor(x_ff, zr[:, :, R_FF:R_FF + FH], bfb[:], ALU.add))
            V.scalar_tensor_tensor(out=krl[:, :, 24:32], in0=x_ff, scalar=-1.0, in1=x_ff, op0=ALU.mult,
                                   op1=ALU.min).then_inc(ff_abs, 1)
            cos, sin = c_rrow[:, 0], c_rrow[:, 1]
            k1_, k2_ = zr[:, :, R_KR:R_KR + 16], zr[:, :, R_KR + 16:RW]
            V.tensor_tensor(krl[:, :, 64:80], k1_, cos, ALU.mult)
            V.tensor_tensor(krl[:, :, 80:96], k1_, sin, ALU.mult)
            V.tensor_tensor(krl[:, :, 96:112], k2_, sin, ALU.mult)
            link(V.tensor_tensor(krl[:, :, 112:128], k2_, cos, ALU.mult))
            V.tensor_tensor(krl[:, :, 64:80], krl[:, :, 64:80], krl[:, :, 96:112], ALU.subtract)
            V.tensor_tensor(krl[:, :, 80:96], krl[:, :, 80:96], krl[:, :, 112:128], ALU.add)
            low_part(wv_lo[:], wv[:], wv_hi[:], w_hi_ready, 3, w_split)
            dve.wait_ge(rt_ready, 1)
            link(V.reciprocal(small[:, 20:30], small[:, 10:20]))
            for t in range(T):
                V.scalar_tensor_tensor(out=cqn[:, t], in0=zr[:, t, R_CQ:R_CKV], scalar=small[:, 20 + t:21 + t], in1=gq[:],
                                       op0=ALU.mult, op1=ALU.mult)
                V.scalar_tensor_tensor(out=ckvn[:, t], in0=zr[:, t, R_CKV:R_KR], scalar=small[:, 25 + t:26 + t], in1=gkv[:],
                                       op0=ALU.mult, op1=ALU.mult)
            dve.wait_ge(ff_log, 1)
            V.scalar_tensor_tensor(out=krl[:, :, 0:FH], in0=x_ff, scalar=0.0, in1=krl[:, :, 16:24],
                                   op0=ALU.min, op1=ALU.subtract).then_inc(rows_ready, 1)
            low_part(wq_lo[:], wq[:], wq_hi[:], w_hi_ready, 4, w_split)
            dve.wait_ge(tr_copied, 5)
            dve.wait_ge(proj_done, 23)
            lf = prob[0:FH, 0, :]
            link(V.tensor_scalar(lf.rearrange("p (t k) -> p t k", t=TP), zT[0:FH, 0:TP, 3, :], -1.0, None, ALU.mult))
            link(V.memset(prob[0:64, 1, :], 1.0))
            link(V.tensor_tensor_scan(ncT[0:FH], prob[0:FH, 1, :], lf, 0.0, ALU.mult, ALU.add))
            rest = prob[0:FH, 0, :]
            link(V.tensor_copy(nc3[0:FH], ncT[0:FH]))
            link(V.tensor_tensor(rest, ncT[0:FH], nc3[0:FH], ALU.subtract))
            link(V.tensor_copy(nc_mid[0:FH], rest))
            V.tensor_copy(nc3[32:32 + FH], nc_mid[0:FH])
            link(V.tensor_tensor(rest, rest, nc_mid[0:FH], ALU.subtract))
            V.tensor_copy(nc3[64:64 + FH], rest).then_inc(nc_ready, 1)
            rr = slice(64, 96)
            for h in range(MH):
                b = 3 * (h % 2)
                dve.wait_ge(mq_done, h + 1)
                t1, t2 = prob[rr, 2], prob[rr, 3]
                V.tensor_tensor(t1, ps[rr, b], c_rope[rr, 0, 0:SEQ], ALU.mult)
                V.tensor_tensor(t2, ps[rr, b + 1], c_rope[rr, 1, 0:SEQ], ALU.mult)
                V.tensor_tensor(probT[rr, 0, 0:P], ps[rr, b + 2, 0:P], c_rope[rr, 0, SEQ:NT], ALU.mult)
                link(V.tensor_tensor(probT[rr, 1, 0:P], ps[rr, b + 2, P:2 * P], c_rope[rr, 1, SEQ:NT], ALU.mult))
                V.tensor_tensor(qmT[rr, h, 0:SEQ], t1, t2, ALU.add)
                V.tensor_tensor(qmT[rr, h, SEQ:NT], probT[rr, 0, 0:P], probT[rr, 1, 0:P], ALU.add).then_inc(mq_rope, 1)
                dve.wait_ge(mq_rope, h + 1)
            dve.wait_ge(lfs_loaded, 16 * (1 + DB))
            link(V.tensor_scalar(lfs[0:64], lfs[0:64], -1.0, None, ALU.mult))
            V.tensor_tensor_scan(ncS[0:64], prob[0:64, 1, 0:L], lfs[0:64], 0.0, ALU.mult, ALU.add).then_inc(ncs_ready, 1)
            dve.wait_ge(ncs_ready, 1)

            def row_max(n):
                dve.wait_ge(s_done, n + 1)
                V.tensor_reduce(small[:, 32 + n % 4:33 + n % 4], ps[:, n % 3, 0:keys_of(n)], AX.X, ALU.max,
                                negate=True).then_inc(max_ready, 1)

            def normalise(n):
                dve.wait_ge(exp_done, n + 1)
                q = small[:, 36 + n % 4:37 + n % 4]
                link(V.reciprocal(q, q))
                pr = prob[:, n % 4, 0:keys_of(n)]
                V.tensor_scalar(pr, pr, q, None, ALU.mult).then_inc(p_ready, 1)

            def copy_out(n):
                dve.wait_ge(pv_done, n + 1)
                if is_prompt(n):
                    if plan[n][1] % 8 == 7:
                        kind, c = unit(n)[:2]
                        V.tensor_copy(oT[:, 4 * kind + c, 0:SEQ], ps[:, 5 + plan[n][1] // 8 % 2]).then_inc(o_copied, 1)
                    return
                b, kind = divmod(plan[n][1], 2)
                bank = ps[:, 7, 0:P]
                new = slice(SEQ + b * DS, SEQ + (b + 1) * DS)
                if kind == 0:
                    for hh in range(2):
                        rows = slice(64 * hh, 64 * hh + 64)
                        ins = V.tensor_copy(oT[rows, 0:4, new],
                                            bank[rows].rearrange("p (c x) -> p c x", c=4)[:, :, DS * hh:DS * hh + DS])
                    ins.then_inc(so_copied, 1)
                else:
                    V.tensor_copy(latT[:, :, b * DS:(b + 1) * DS], bank.rearrange("p (h q) -> p h q", h=MH)).then_inc(so_copied, 1)

            for n_ in range(ALL + 4):
                if n_ < ALL:
                    row_max(n_)
                if 1 <= n_ <= ALL:
                    normalise(n_ - 1)
                if n_ >= 4:
                    copy_out(n_ - 4)
            dve.wait_ge(up_done, 1)
            V.tensor_copy(oT[:, 4:8, SEQ:NT], ps[:, 7].rearrange("p (c k) -> p c k", c=4)).then_inc(lat_copied, 1)
            dve.wait_ge(late_loaded, 64)
            for t in range(T):
                dve.wait_ge(out_done, t + 1)
                V.tensor_tensor(x2[:, t], x2[:, t], ps[:, 2 * (t % 2):2 * (t % 2) + 2].rearrange("p a b -> p (a b)"),
                                ALU.add).then_inc(x2_ready, 1)
                dve.wait_ge(x2_ready, t + 1)
                V.tensor_tensor_reduce(out=h2[:, t], in0=x2[:, t], in1=x2[:, t], scale=1.0, scalar=0.0, op0=ALU.mult,
                                       op1=ALU.add, accum_out=small[:, 40 + t:41 + t]).then_inc(ss2_ready, 1)
                dve.wait_ge(rt2_ready, t + 1)
                link(V.reciprocal(small[:, 45 + t:46 + t], small[:, 45 + t:46 + t]))
                V.scalar_tensor_tensor(out=h2[:, t], in0=x2[:, t], scalar=small[:, 45 + t:46 + t], in1=gffn[:],
                                       op0=ALU.mult, op1=ALU.mult).then_inc(h2_ready, 1)
            dve.wait_ge(hh_ready, 1)
            V.tensor_tensor(hl[:], h2T[:, :, 0:NTD], hh[:].bitcast(F32), ALU.subtract).then_inc(hl_ready, 1)
            dve.wait_ge(late_loaded, 16 * 5)
            LINKS = 18

            dve.sem_inc(decoded, 2)

            def head_pair(pair):
                q = [0]

                def step(ins):
                    q[0] += 1
                    ins.then_inc(dve_loop, 1)
                    dve.wait_ge(dve_loop, pair * LINKS + q[0])
                    dve.sem_inc(wait_carrier, 1)

                def top16(src, rest, val, idx, read=None):
                    for a, v in zip(src, val):
                        ins = V.max(v[:, 0:8], a)
                    step(ins)
                    for a, r_, v, i_ in zip(src, rest, val, idx):
                        V.max_index(i_[:, 0:8], v[:, 0:8], a)
                        ins = V.match_replace(r_, v[:, 0:8], a, NEG)
                    step(ins)
                    if read is not None:
                        dve.sem_inc(read, 1)
                    for r_, v in zip(rest, val):
                        ins = V.max(v[:, 8:16], r_)
                    step(ins)
                    for r_, v, i_ in zip(rest, val, idx):
                        ins = V.max_index(i_[:, 8:16], v[:, 8:16], r_)
                    step(ins)

                for s in range(2):
                    dve.wait_ge(sc_copied, pair * 2 + s + 1)
                    dve.sem_inc(wait_carrier, 1)
                    ins = V.reciprocal(rs[:, s, 0:T], rt[:, s, 0:T])
                    if s == 0:
                        step(ins)
                    rows = [(t, c) for t in range(T) for c in range(2)]
                    top16([scb[:, s, t, c] for t, c in rows], [sr[:, s, t, c] for t, c in rows],
                          [v16[:, s, t, c] for t, c in rows], [i16[:, s, t, c] for t, c in rows], read=sc_read)
                for s in range(2):
                    vs_ = v16[:, s].rearrange("p t c k -> p t (c k)")
                    ins = V.tensor_tensor(vs_, vs_, rs[:, s, 0:T].unsqueeze(2).broadcast_to([P, T, 2 * TK]), ALU.mult)
                step(ins)
                dve.wait_ge(decoded, pair * 2 + 1)
                dve.sem_inc(wait_carrier, 1)
                v_rows, v_cols = (v16[:, :, :, c, :].rearrange("p s t k -> p (s t) k") for c in range(2))
                V.tensor_tensor(both(cand)[:, :, 0:HALF * TK].rearrange("p n (a b) -> p n a b", a=HALF),
                                v_rows[:, :, 0:HALF].unsqueeze(3).broadcast_to([P, 2 * T, HALF, TK]),
                                v_cols.unsqueeze(2).broadcast_to([P, 2 * T, HALF, TK]), ALU.add)
                step(V.tensor_tensor(both(cand)[:, :, HALF * TK:], v_rows[:, :, HALF:],
                                     v_cols[:, :, 0:1].broadcast_to([P, 2 * T, HALF]), ALU.add))
                rows = [(s, t) for s in range(2) for t in range(T)]
                top16([cand[:, s, t] for s, t in rows], [candr[:, s, t] for s, t in rows],
                      [cv[:, s, t] for s, t in rows], [ci[:, s, t] for s, t in rows])
                heads = lambda x, s: x[:, :, bass.ds((pair * 2 + s) * TK, TK)]
                V.tensor_scalar(hi[:], ci[:], 4, None, ALU.logical_shift_right)
                step(V.tensor_scalar(lo[:], ci[:], TK - 1, None, ALU.bitwise_and))
                step(V.scalar_tensor_tensor(out=outer[:], in0=ci[:], scalar=float(HALF * TK), in1=lo[:],
                                            op0=ALU.is_ge, op1=ALU.mult))
                V.tensor_tensor(hi[:], hi[:], outer[:], ALU.add)
                V.tensor_tensor(lo[:], lo[:], outer[:], ALU.subtract)
                for s in range(2):
                    ins = V.tensor_tensor(heads(gap, s), cv[:, s], cv[:, s, :, 0:1].broadcast_to([P, T, TK]), ALU.subtract)
                step(ins)
                dve.wait_ge(decoded, pair * 2 + 2)
                dve.sem_inc(wait_carrier, 1)
                V.tensor_copy(i16f[:], i16[:])
                for pos, oh in ((lo, onehot2), (hi, onehot)):
                    V.tensor_tensor(both(oh), both(pos).unsqueeze(3).broadcast_to(square),
                                    iota[:, 0:TK].unsqueeze(1).unsqueeze(1).broadcast_to(square),
                                    ALU.is_equal).then_inc(onehot_ready, 1)
                dve.wait_ge(onehot_ready, pair * 2 + 2)
                dve.sem_inc(wait_carrier, 1)
                assert q[0] == LINKS, q[0]

            with dve.Fori(0, PH // 2 - 1) as pair:
                head_pair(pair)
            head_pair(PH // 2 - 1)
            link(V.tensor_tensor(both(onehot), both(onehot), i16f[:, :, :, 0, :].rearrange("p s t k -> p (s t) k").unsqueeze(2)
                                 .broadcast_to(square), ALU.mult))
            for s in range(2):
                ins = V.tensor_reduce(e1[:, :, (PH - 2 + s) * TK:(PH - 1 + s) * TK], onehot[:, s], AX.X, ALU.add)
            link(ins)
            V.memset(rs[:, 0, 5:6], 0.0).then_inc(gap_ready, 1)
            dve.wait_ge(gap_exp, 1)
            per_head = gap[:].rearrange("p t (h k) -> p (t h) k", h=PH)
            link(V.tensor_reduce(gsum[:, 0], per_head, AX.X, ALU.add))
            link(V.reciprocal(gsum[:, 1], gsum[:, 0]))
            V.tensor_tensor(gate[:].rearrange("p t (h k) -> p (t h) k", h=PH), per_head,
                            gsum[:, 1].unsqueeze(2).broadcast_to([P, T * PH, TK]), ALU.mult).then_inc(topk_done, 1)
            dve.wait_ge(decoded, 2 + PH - 1)
            V.scalar_tensor_tensor(out=eidx[:].rearrange("p (t k) -> p t k", t=TG), in0=e1[:, TD:T], scalar=float(NK),
                                   in1=e2[:, TD:T], op0=ALU.mult, op1=ALU.add).then_inc(eidx_ready, 1)
            dve.wait_ge(selT_copied, 3)
            part = [P, PART, NK]
            keys = iota[:].unsqueeze(1).broadcast_to(part)
            with dve.Fori(0, CHUNKS) as c:
                for q in range(PARTS):
                    cols = lambda x: x[:, bass.ds(c * CHUNK + q * PART, PART)].unsqueeze(2).broadcast_to(part)
                    dve.wait_ge(sel_used, c * CHUNK + q * PART + PART)
                    V.tensor_tensor(asel[:, q], keys, cols(i1T), ALU.is_equal).then_inc(asel_ones, 1)
                    V.tensor_tensor(bsel[:, q], keys, cols(i2T), ALU.is_equal).then_inc(bsel_ready, 1)
            low_part(ul[:, 0], ub[:, 0], uh[:, 0], uh_ready, 1, ul_ready)
            dve.wait_ge(sel_used, NTD + CHUNK)
            dve.wait_ge(g_stored, 16 * CHUNKS)
            for zeros in (zero[:], acth[:, 1], actl[:, 1], vh[:, 1], vl[:, PER - 1]):
                V.memset(zeros.bitcast(F32), 0.0).then_inc(dense_open, 1)
            dve.wait_ge(dense_open, 5)
            for first, count in ((actl_ready, 1), (vl_ready, 1), (g_used, 2), (ga_ready, 2), (acc_done, PER)):
                dve.sem_inc(first, count)

            XL = PER * GROUP
            with dve.Fori(0, TG) as t:
                row = lambda x: x[:, bass.ds(t + TD, 1), :].rearrange("p a k -> p (a k)")
                with dve.Fori(0, GI) as j:
                    i = t * GI + j
                    q = [0]

                    def chained(ins):
                        q[0] += 1
                        ins.then_inc(y_link, 1)
                        dve.wait_ge(y_link, i * XL + q[0])

                    for s in range(PER):
                        n, slot, nxt = i * PER + s, s % 2, (s + 1) % PER
                        dve.wait_ge(u_loaded[s], 16 * GROUP * i + 16 * GROUP)
                        for e in range(GROUP):
                            ins = V.scalar_tensor_tensor(out=ubuf[:, s, e], in0=ubuf[:, s, e], scalar=1.0, in1=row(h2),
                                                         op0=ALU.mult, op1=ALU.mult, accum_out=dots[:, s, e:e + 1])
                        ins.then_inc(dots_done, 1)
                        low_part(vl[:, s], vb[:, s], vh[:, slot], vh_ready, n + 1, vl_ready)
                        low_part(ul[:, nxt], ub[:, nxt], uh[:, nxt % 2], uh_ready, n + 2, ul_ready)
                        if s == 0:
                            dve.wait_ge(gb_loaded, 64 * i + 64)
                        dve.wait_ge(ga_ready, n + 3)
                        V.tensor_tensor(actv[:, slot].rearrange("p (c t) -> p c t", c=CHUNKS),
                                        ga[:, slot].rearrange("p (c t) -> p c t", c=CHUNKS),
                                        gbuf[:, bass.ds(i % 2, 1), :, s, :].rearrange("p a c t -> p (a c) t"), ALU.mult).then_inc(act_ready, 1)
                        dve.wait_ge(gelu_done, n + 1)
                        chained(V.tensor_tensor(wts[:, s], gelu[:, s],
                                                gate[:].rearrange("p t k -> p (t k)")[:, bass.ds(TD * SEL + n * GROUP, GROUP)],
                                                ALU.mult))
                        low_part(actl[:, slot], actv[:, slot], acth[:, slot], acth_ready, n + 1, actl_ready)
                        if s == PER - 1:
                            dve.wait_ge(actl_ready, n + 2)
                            dve.sem_inc(g_used, 1)
                        dve.wait_ge(v_loaded[s], 16 * GROUP * i + 16 * GROUP)
                        for e in range(GROUP):
                            ins = V.scalar_tensor_tensor(out=row(x2), in0=vbuf[:, s, e], scalar=wts[:, s, e:e + 1],
                                                         in1=row(x2), op0=ALU.mult, op1=ALU.add)
                            if e < GROUP - 1:
                                chained(ins)
                        ins.then_inc(acc_done, 1)
                        dve.wait_ge(acc_done, n + 1 + PER)
                    assert q[0] == XL
            def scale_rows(t):
                link(V.reciprocal(small[:, 50 + t:51 + t], small[:, 45 + t:46 + t]))
                V.scalar_tensor_tensor(out=yout[:, t], in0=x2[:, t], scalar=small[:, 50 + t:51 + t], in1=gfin[:],
                                       op0=ALU.mult, op1=ALU.mult).then_inc(y_ready, 1)

            for t in LAST_ORDER[:TG]:
                V.scalar_tensor_tensor(out=yout[:, t], in0=x2[:, t], scalar=1.0, in1=x2[:, t], op0=ALU.mult, op1=ALU.mult,
                                       accum_out=small[:, 40 + t:41 + t]).then_inc(ss3_ready, 1)
            for u, t in enumerate(LAST_ORDER[:TG]):
                dve.wait_ge(rt4_ready, u + 1)
                scale_rows(t)
            for t in range(TD):
                dve.wait_ge(dense_done, t + 1)
                V.tensor_tensor(x2[:, t], x2[:, t], ps[:, 2 * t:2 * t + 2].rearrange("p a b -> p (a b)"),
                                ALU.add).then_inc(sum_ready, 1)
            dve.wait_ge(sum_ready, TD)
            dve.wait_ge(rt4_ready, TG + 1)
            for t in range(TD):
                scale_rows(t)


def _rope_tables():
    half = ROPE // 2
    inv = (np.float32(10000.0) ** (-np.arange(half, dtype=np.float32) / np.float32(half))).astype(np.float32)
    pos = np.concatenate([np.arange(SEQ), np.tile(PAST + np.arange(DS), DB)]).astype(np.float32)
    ang = pos[:, None] * inv[None, :]
    return np.cos(ang).astype(np.float32), np.sin(ang).astype(np.float32)


def _constants():

    cos, sin = _rope_tables()
    j = np.arange(P) % 32
    sign = np.where(j < 16, -1.0, 1.0).astype(np.float32)[:, None]
    c_rope = np.stack([cos.T[j % 16], sin.T[j % 16] * sign], 1) * np.float32(MLA_SCALE)
    c_rrow = np.stack([cos, sin]).reshape(2, T, P, 16).transpose(2, 0, 1, 3)
    selh = np.zeros((3, 32, FH, P), mybir.dt.np(BF16))
    selh[:, np.arange(FH), np.arange(FH)] = 1
    selb = np.zeros((DB, FH, DB, FH, DS), np.float32)
    for b in range(DB):
        for h in range(FH):
            selb[b, h, b, h] = 1
    q, k = np.arange(P)[:, None], np.arange(P)[None]
    fmask = np.where(k <= q, 0, NEG)
    mmask = np.where(k // 64 <= q // 64, 0, NEG)
    nmask = np.where(np.arange(DS)[None] <= q % DS, 0, NEG)
    cb = np.concatenate([np.eye(P), fmask, mmask, nmask], 1).astype(mybir.dt.np(BF16))
    return {"ident": np.eye(P, dtype=np.float32), "ones": np.ones((P, P), np.float32), "c_rope": c_rope.astype(np.float32),
            "c_rrow": c_rrow, "iota": np.broadcast_to(np.arange(NK, dtype=np.float32), (P, NK)),
            "selh": selh.reshape(96, FH, P), "selb": selb.reshape(DB * FH, DB, P), "cb": cb}


def _arrays(i):
    f = lambda x: np.asarray(x)
    fold = lambda w: w.reshape(KD, P, -1).transpose(1, 0, 2)
    x = np.concatenate([f(i["x_prompt"]).reshape(SEQ, D), f(i["x_sample"]).reshape(DB * DS, D)])
    w_in = f(i["w_in"])[0]
    fw = FH * HD
    w_ukv = f(i["w_ukv"])[0].reshape(KVL, MH, NOPE + VD)
    w_uq = f(i["w_uq"])[0].reshape(2, P, MH, NOPE + ROPE).transpose(1, 0, 2, 3)
    r1, r2 = w_uq[..., NOPE:NOPE + 16], w_uq[..., NOPE + 16:]
    ck = f(i["cache_fox_k"])[0].reshape(DB, PAST, 4, P)
    keys = f(i["peer_sub_keys"])[0]
    tile = lambda v: np.broadcast_to(v, (P,) + v.shape)
    return {
        **_constants(),
        "xT": fold(x.T), "xr": x,
        "gm": f(i["g_mix"])[0].reshape(KD, P).T,
        "wr": fold(w_in[:, 3 * fw:]), "wk": fold(w_in[:, fw:2 * fw]), "wv": fold(w_in[:, 2 * fw:3 * fw]), "wq": fold(w_in[:, :fw]),
        "bfb": tile(np.broadcast_to(f(i["b_f"])[0], (T, FH))),
        "gq": tile(f(i["g_q"])[0]), "gkv": tile(f(i["g_kv"])[0]),
        "w_uq": np.concatenate([w_uq, r2, r1], -1),
        "w_uk": w_ukv[..., :NOPE], "w_uv": w_ukv[..., NOPE:].reshape(KVL, MH * VD),
        "w_ukT": w_ukv[..., :NOPE].transpose(2, 1, 0),
        "past_k": ck.transpose(0, 3, 2, 1), "past_v": f(i["cache_fox_v"])[0].reshape(DB, PAST, fw),
        "past_logf": f(i["cache_fox_logf"])[0].transpose(0, 2, 1).reshape(DB * FH, PAST),
        "past_ckv": f(i["cache_mla_ckv"])[0], "past_ckvT": f(i["cache_mla_ckv"])[0].transpose(0, 2, 1),
        "past_krT": f(i["cache_mla_krope"])[0].transpose(0, 2, 1),
        "w_o": f(i["w_o"])[0].reshape(8, P, D).transpose(1, 0, 2),
        "gffn": tile(f(i["g_ffn"])[0]), "gfin": tile(f(i["g_final"])),
        "wpq": f(i["w_pq"])[0].reshape(KD, P, PH, 2 * P).transpose(2, 1, 0, 3),
        "keysT": keys.transpose(3, 1, 0, 2).reshape(P, 2 * PH, NK),
        "peer_uT": f(i["peer_u"])[0].reshape(BLOCKS, P, KD, P).transpose(0, 3, 2, 1).reshape(BLOCKS, P, D),
        "peer_u": f(i["peer_u"])[0], "peer_v": f(i["peer_v"])[0],
    }


_OUTS = {"y": (NT, D), "fk": (NT, FH * HD), "fv": (NT, FH * HD), "logf": (NT, FH), "ckv": (NT, KVL), "krope": (NT, ROPE)}


def kernel(**inputs):
    import concourse.bacc as _bacc
    from concourse.bass_utils import run_bass_kernel_spmd as _run

    nc = _bacc.Bacc("TRN2", target_bir_lowering=False, num_devices=1)
    arrays, t_in, t_out = {}, {}, {}
    for name, a in _arrays(inputs).items():
        a = np.ascontiguousarray(a)
        arrays[f"in_{name}"] = a
        t_in[name] = nc.dram_tensor(f"in_{name}", a.shape, mybir.dt.from_np(a.dtype), kind="ExternalInput").ap()
    for name, shape in _OUTS.items():
        t_out[name] = nc.dram_tensor(f"out_{name}", shape, F32, kind="ExternalOutput").ap()
    peer_step_kernel(nc, t_in, t_out)
    r = _run(nc, [arrays], core_ids=[0]).results[0]
    o = {name: r[f"out_{name}"] for name in _OUTS}
    p = lambda name, *s: o[name][:SEQ].reshape(1, 1, SEQ, *s)
    d = lambda name, *s: o[name][SEQ:].reshape(1, DB, DS, *s)
    return (o["y"][:SEQ].reshape(1, SEQ, D), o["y"][SEQ:].reshape(DB, DS, D),
            p("fk", FH, HD), p("fv", FH, HD), p("logf", FH), p("ckv", KVL), p("krope", ROPE),
            d("fk", FH, HD), d("fv", FH, HD), d("logf", FH), d("ckv", KVL), d("krope", ROPE))
```
